# Optimizing a Trainium2 kernel written in Bass

```python
import jax, jax.numpy as jnp
from jax import lax
import numpy as np
import math

D_MODEL = 1024
BATCH = 1
SEQ = 256
DEPTH = 2

HEAD_DIM = 64
MEM_DIM = D_MODEL // 4
MEM_HEADS = MEM_DIM // HEAD_DIM
MEM_LEN = 256
FOX_DIM = D_MODEL - MEM_DIM
FOX_HEADS = FOX_DIM // HEAD_DIM
CONV_DIM = D_MODEL - MEM_DIM
CONV_WIDTH = 31
Q_BLOCK = 128
D_FF = ((8 * D_MODEL // 3 + 127) // 128) * 128
N_EXPERTS = 8
TOP_K = 2
EXPERT_FF = 7 * D_MODEL // 2
EXPERT_BLOCK = 128
N_FOX = (DEPTH + 1) // 2
N_CONV = DEPTH // 2
EPS = 1e-6
NEG_INF = -1e30


def rms_norm(x, g):
    xf = x.astype(jnp.float32)
    y = xf * lax.rsqrt(jnp.mean(xf * xf, axis=-1, keepdims=True) + EPS)
    return (y * g.astype(jnp.float32)).astype(x.dtype)

def layer_norm(x, g, b):
    xf = x.astype(jnp.float32)
    mu = jnp.mean(xf, axis=-1, keepdims=True)
    var = jnp.mean(jnp.square(xf - mu), axis=-1, keepdims=True)
    y = (xf - mu) * lax.rsqrt(var + EPS)
    return (y * g.astype(jnp.float32) + b.astype(jnp.float32)).astype(x.dtype)

def forget_attention(q, k, v, log_f):
    B, S, H, hd = q.shape
    nb = S // Q_BLOCK
    c = jnp.cumsum(log_f, axis=1).transpose(0, 2, 1)
    q_blocks = q.reshape(B, nb, Q_BLOCK, H, hd).transpose(1, 0, 2, 3, 4)
    c_blocks = c.reshape(B, H, nb, Q_BLOCK).transpose(2, 0, 1, 3)
    k_pos = jnp.arange(S)
    scale = hd ** -0.5

    def one_block(args):
        q_b, c_b, blk = args
        s = jnp.einsum('bqhd,bkhd->bhqk', q_b, k, preferred_element_type=jnp.float32) * scale
        s = s + (c_b[..., :, None] - c[:, :, None, :])
        q_pos = blk * Q_BLOCK + jnp.arange(Q_BLOCK)
        s = jnp.where(k_pos[None, :] <= q_pos[:, None], s, NEG_INF)
        p = jax.nn.softmax(s, axis=-1).astype(v.dtype)
        return jnp.einsum('bhqk,bkhd->bqhd', p, v)

    o = lax.map(one_block, (q_blocks, c_blocks, jnp.arange(nb)))
    return o.transpose(1, 0, 2, 3, 4).reshape(B, S, H * hd)

def memory_attention(xq, mk, mv, g_q, g_k):
    B, S, _ = xq.shape
    M = mk.shape[1]
    q = rms_norm(xq.reshape(B, S, MEM_HEADS, HEAD_DIM), g_q)
    k = rms_norm(mk.reshape(B, M, MEM_HEADS, HEAD_DIM), g_k)
    v = mv.reshape(B, M, MEM_HEADS, HEAD_DIM)
    s = jnp.einsum('bshd,bmhd->bhsm', q, k, preferred_element_type=jnp.float32) * (HEAD_DIM ** -0.5)
    p = jax.nn.softmax(s, axis=-1).astype(v.dtype)
    return jnp.einsum('bhsm,bmhd->bshd', p, v).reshape(B, S, MEM_DIM)

def conformer_conv(glu_in, dw, dw_b, ln_g, ln_b):
    a, gate = jnp.split(glu_in, 2, axis=-1)
    u = a * jax.nn.sigmoid(gate)
    u = lax.conv_general_dilated(
        u, dw[:, None, :].astype(u.dtype), window_strides=(1,),
        padding=[(CONV_WIDTH - 1, 0)], dimension_numbers=('NWC', 'WIO', 'NWC'),
        feature_group_count=CONV_DIM) + dw_b.astype(u.dtype)
    return jax.nn.silu(layer_norm(u, ln_g, ln_b))

def swiglu(h, w_gate, w_up, w_down):
    return (jax.nn.silu(h @ w_gate) * (h @ w_up)) @ w_down

def moe_swiglu(h, w_router, w_gate, w_up, w_down):
    B, S, D = h.shape
    xt = h.reshape(-1, D)
    T = xt.shape[0]
    A = T * TOP_K
    logits = (xt @ w_router).astype(jnp.float32)
    top_logit, top_idx = lax.top_k(logits, TOP_K)
    gates = jax.nn.softmax(top_logit, axis=-1)
    flat_e = top_idx.reshape(-1)
    order = jnp.argsort(flat_e)
    sorted_e = flat_e[order]
    sizes = jnp.bincount(flat_e, length=N_EXPERTS).astype(jnp.int32)
    padded = ((sizes + EXPERT_BLOCK - 1) // EXPERT_BLOCK) * EXPERT_BLOCK
    pad_end = jnp.cumsum(padded)
    pad_start = pad_end - padded
    start = jnp.cumsum(sizes) - sizes
    dest = pad_start[sorted_e] + (jnp.arange(A, dtype=jnp.int32) - start[sorted_e])
    n_blocks = -(-A // EXPERT_BLOCK) + N_EXPERTS
    rows = n_blocks * EXPERT_BLOCK
    tok_buf = jnp.full((rows,), T, jnp.int32).at[dest].set((order // TOP_K).astype(jnp.int32))
    gate_buf = jnp.zeros((rows,), jnp.float32).at[dest].set(gates.reshape(-1)[order])
    block_start = jnp.arange(n_blocks, dtype=jnp.int32) * EXPERT_BLOCK
    block_expert = jnp.minimum(jnp.searchsorted(pad_end, block_start, side='right'), N_EXPERTS - 1)
    xt_pad = jnp.concatenate([xt, jnp.zeros((1, D), xt.dtype)], axis=0)
    xs = xt_pad[tok_buf].reshape(n_blocks, EXPERT_BLOCK, D)

    def expert_block(args):
        xb, e = args
        return swiglu(xb, w_gate[e], w_up[e], w_down[e])

    ys = lax.map(expert_block, (xs, block_expert)).reshape(rows, D)
    ys = ys * gate_buf[:, None].astype(ys.dtype)
    out = jnp.zeros((T + 1, D), ys.dtype).at[tok_buf].add(ys)[:T]
    return out.reshape(B, S, D)

def first_inputs(seed: int = 0) -> dict:
    key = jax.random.key(seed)
    ks = iter(jax.random.split(key, 40))

    def nrm(shape, scale):
        return jax.random.normal(next(ks), shape, jnp.float32) * scale

    D = D_MODEL
    fox_in = 3 * FOX_DIM + FOX_HEADS + MEM_DIM
    conv_in = 2 * CONV_DIM + MEM_DIM
    return {
        "x": nrm((BATCH, SEQ, D), 1.0),
        "mem": nrm((BATCH, MEM_LEN, D), 1.0),
        "norm_mix": 1.0 + nrm((DEPTH, D), 0.02),
        "norm_mem": 1.0 + nrm((DEPTH, D), 0.02),
        "norm_ffn": 1.0 + nrm((DEPTH, D), 0.02),
        "w_mem_kv": nrm((DEPTH, D, 2 * MEM_DIM), D ** -0.5),
        "g_mq": 1.0 + nrm((DEPTH, HEAD_DIM), 0.02),
        "g_mk": 1.0 + nrm((DEPTH, HEAD_DIM), 0.02),
        "fox_w_in": nrm((N_FOX, D, fox_in), D ** -0.5),
        "fox_b_f": 3.0 + nrm((N_FOX, FOX_HEADS), 0.5),
        "fox_g_q": 1.0 + nrm((N_FOX, HEAD_DIM), 0.02),
        "fox_g_k": 1.0 + nrm((N_FOX, HEAD_DIM), 0.02),
        "fox_w_out": nrm((N_FOX, FOX_DIM + MEM_DIM, D), 0.5 * D ** -0.5),
        "conv_w_in": nrm((N_CONV, D, conv_in), D ** -0.5),
        "conv_b_in": nrm((N_CONV, 2 * CONV_DIM), 0.02),
        "conv_dw": nrm((N_CONV, CONV_WIDTH, CONV_DIM), CONV_WIDTH ** -0.5),
        "conv_dw_b": nrm((N_CONV, CONV_DIM), 0.02),
        "conv_ln_g": 1.0 + nrm((N_CONV, CONV_DIM), 0.02),
        "conv_ln_b": nrm((N_CONV, CONV_DIM), 0.02),
        "conv_w_out": nrm((N_CONV, CONV_DIM + MEM_DIM, D), 0.5 * D ** -0.5),
        "ffn_w_gate": nrm((N_FOX, D, D_FF), D ** -0.5),
        "ffn_w_up": nrm((N_FOX, D, D_FF), D ** -0.5),
        "ffn_w_down": nrm((N_FOX, D_FF, D), 0.5 * D_FF ** -0.5),
        "moe_router": nrm((N_CONV, D, N_EXPERTS), D ** -0.5),
        "moe_w_gate": nrm((N_CONV, N_EXPERTS, D, EXPERT_FF), D ** -0.5),
        "moe_w_up": nrm((N_CONV, N_EXPERTS, D, EXPERT_FF), D ** -0.5),
        "moe_w_down": nrm((N_CONV, N_EXPERTS, EXPERT_FF, D), 0.5 * EXPERT_FF ** -0.5),
    }

def first_block(x, mem, norm_mix, norm_mem, norm_ffn, w_mem_kv, g_mq, g_mk,
              fox_w_in, fox_b_f, fox_g_q, fox_g_k, fox_w_out,
              conv_w_in, conv_b_in, conv_dw, conv_dw_b, conv_ln_g, conv_ln_b, conv_w_out,
              ffn_w_gate, ffn_w_up, ffn_w_down,
              moe_router, moe_w_gate, moe_w_up, moe_w_down):
    B, S, D = x.shape
    h = x
    for i in range(DEPTH):
        j = i // 2
        u = rms_norm(h, norm_mix[i])
        m = rms_norm(mem, norm_mem[i])
        mk, mv = jnp.split(m @ w_mem_kv[i], 2, axis=-1)
        if i % 2 == 0:
            proj = u @ fox_w_in[j]
            q, k, v, f_logit, mq = jnp.split(
                proj, [FOX_DIM, 2 * FOX_DIM, 3 * FOX_DIM, 3 * FOX_DIM + FOX_HEADS], axis=-1)
            q = rms_norm(q.reshape(B, S, FOX_HEADS, HEAD_DIM), fox_g_q[j])
            k = rms_norm(k.reshape(B, S, FOX_HEADS, HEAD_DIM), fox_g_k[j])
            v = v.reshape(B, S, FOX_HEADS, HEAD_DIM)
            log_f = jax.nn.log_sigmoid((f_logit + fox_b_f[j]).astype(jnp.float32))
            mix = forget_attention(q, k, v, log_f)
            w_out = fox_w_out[j]
        else:
            proj = u @ conv_w_in[j]
            glu_in, mq = jnp.split(proj, [2 * CONV_DIM], axis=-1)
            mix = conformer_conv(glu_in + conv_b_in[j], conv_dw[j], conv_dw_b[j],
                                 conv_ln_g[j], conv_ln_b[j])
            w_out = conv_w_out[j]
        mem_out = memory_attention(mq, mk, mv, g_mq[i], g_mk[i])
        h = h + jnp.concatenate([mix, mem_out], axis=-1) @ w_out
        z = rms_norm(h, norm_ffn[i])
        if i % 2 == 0:
            h = h + swiglu(z, ffn_w_gate[j], ffn_w_up[j], ffn_w_down[j])
        else:
            h = h + moe_swiglu(z, moe_router[j], moe_w_gate[j], moe_w_up[j], moe_w_down[j])
    return h


DEPTH_2 = 1

CHUNK = 64
N_DIFF_HEADS = 4
N_SB_HEADS = 8
DIFF_WIDTH = N_DIFF_HEADS * 2 * HEAD_DIM
SB_WIDTH = N_SB_HEADS * HEAD_DIM
MIX_WIDTH = DIFF_WIDTH + SB_WIDTH
IN_WIDTH = 3 * MIX_WIDTH
D_FF_2 = 4 * D_MODEL
ROPE_THETA = 10000.0
NORM_EPS = 1e-6
N_MOD = 6


def rms_norm_2(x, g):
    xf = x.astype(jnp.float32)
    y = xf * lax.rsqrt(jnp.mean(xf * xf, axis=-1, keepdims=True) + NORM_EPS)
    return (y * g.astype(jnp.float32)).astype(x.dtype)

def rope_tables(seq_len, dim):
    inv = 1.0 / (ROPE_THETA ** (jnp.arange(0, dim, 2, dtype=jnp.float32) / dim))
    ang = jnp.arange(seq_len, dtype=jnp.float32)[:, None] * inv[None, :]
    ang = jnp.concatenate([ang, ang], axis=-1)
    return jnp.cos(ang), jnp.sin(ang)

def apply_rope(x, cos, sin):
    x1, x2 = jnp.split(x, 2, axis=-1)
    rot = jnp.concatenate([-x2, x1], axis=-1)
    return (x * cos + rot * sin).astype(x.dtype)

def diff_attention(q, k, v, lam, subln_g, lambda_init):
    seq_len = q.shape[3]
    scale = HEAD_DIM ** -0.5
    outs = []
    for blk in range(seq_len // Q_BLOCK):
        q0 = blk * Q_BLOCK
        kv_len = q0 + Q_BLOCK
        qb = q[:, :, :, q0:kv_len]
        kb = k[:, :, :, :kv_len]
        vb = v[:, :, :kv_len]
        s = jnp.einsum("bhmqd,bhmkd->bhmqk", qb, kb).astype(jnp.float32) * scale
        q_chunk = (q0 + jnp.arange(Q_BLOCK)) // CHUNK
        k_chunk = jnp.arange(kv_len) // CHUNK
        mask = k_chunk[None, :] <= q_chunk[:, None]
        p = jax.nn.softmax(jnp.where(mask, s, -jnp.inf), axis=-1)
        w = p[:, :, 0] - lam * p[:, :, 1]
        outs.append(jnp.einsum("bhqk,bhkd->bhqd", w.astype(vb.dtype), vb))
    o = jnp.concatenate(outs, axis=2)
    return rms_norm_2(o, subln_g) * (1.0 - lambda_init)

def stick_breaking_attention(q, k, v):
    seq_len = q.shape[2]
    scale = HEAD_DIM ** -0.5
    outs = []
    for blk in range(seq_len // Q_BLOCK):
        q0 = blk * Q_BLOCK
        kv_len = q0 + Q_BLOCK
        qb = q[:, :, q0:kv_len]
        kb = k[:, :, :kv_len]
        vb = v[:, :, :kv_len]
        z = jnp.einsum("bhqd,bhkd->bhqk", qb, kb).astype(jnp.float32) * scale
        t_idx = q0 + jnp.arange(Q_BLOCK)
        s_idx = jnp.arange(kv_len)
        causal = s_idx[None, :] < t_idx[:, None]
        log_beta = jax.nn.log_sigmoid(z)
        log_1m = jnp.where(causal, jax.nn.log_sigmoid(-z), 0.0)
        suffix = lax.cumsum(log_1m, axis=3, reverse=True) - log_1m
        a = jnp.where(causal, jnp.exp(log_beta + suffix), 0.0)
        outs.append(jnp.einsum("bhqk,bhkd->bhqd", a.astype(vb.dtype), vb))
    return jnp.concatenate(outs, axis=2)

def second_inputs(seed: int = 0) -> dict:
    key = jax.random.key(seed)
    ks = jax.random.split(key, 16)
    f32 = jnp.float32
    x = jax.random.normal(ks[0], (BATCH, SEQ, D_MODEL), f32)
    c = jax.random.normal(ks[1], (BATCH, D_MODEL), f32)
    ada_w = jax.random.normal(ks[2], (DEPTH_2, D_MODEL, N_MOD * D_MODEL), f32) * (0.5 * D_MODEL ** -0.5)
    ada_b = jax.random.normal(ks[3], (DEPTH_2, N_MOD * D_MODEL), f32) * 0.01
    mix_norm_g = 1.0 + 0.02 * jax.random.normal(ks[4], (DEPTH_2, D_MODEL), f32)
    w_in = jax.random.normal(ks[5], (DEPTH_2, D_MODEL, IN_WIDTH), f32) * D_MODEL ** -0.5
    lambda_q1 = 0.1 * jax.random.normal(ks[6], (DEPTH_2, HEAD_DIM), f32)
    lambda_k1 = 0.1 * jax.random.normal(ks[7], (DEPTH_2, HEAD_DIM), f32)
    lambda_q2 = 0.1 * jax.random.normal(ks[8], (DEPTH_2, HEAD_DIM), f32)
    lambda_k2 = 0.1 * jax.random.normal(ks[9], (DEPTH_2, HEAD_DIM), f32)
    diff_subln_g = 1.0 + 0.02 * jax.random.normal(ks[10], (DEPTH_2, 2 * HEAD_DIM), f32)
    w_out = jax.random.normal(ks[11], (DEPTH_2, MIX_WIDTH, D_MODEL), f32) * MIX_WIDTH ** -0.5
    ffn_norm_g = 1.0 + 0.02 * jax.random.normal(ks[12], (DEPTH_2, D_MODEL), f32)
    w_ff1 = jax.random.normal(ks[13], (DEPTH_2, D_MODEL, D_FF_2), f32) * D_MODEL ** -0.5
    w_ff2 = jax.random.normal(ks[14], (DEPTH_2, D_FF_2, D_MODEL), f32) * D_FF_2 ** -0.5
    final_norm_g = 1.0 + 0.02 * jax.random.normal(ks[15], (D_MODEL,), f32)
    return {"x": x, "c": c, "ada_w": ada_w, "ada_b": ada_b, "mix_norm_g": mix_norm_g,
            "w_in": w_in, "lambda_q1": lambda_q1, "lambda_k1": lambda_k1,
            "lambda_q2": lambda_q2, "lambda_k2": lambda_k2, "diff_subln_g": diff_subln_g,
            "w_out": w_out, "ffn_norm_g": ffn_norm_g, "w_ff1": w_ff1, "w_ff2": w_ff2,
            "final_norm_g": final_norm_g}

def second_block(x, c, ada_w, ada_b, mix_norm_g, w_in, lambda_q1, lambda_k1, lambda_q2,
              lambda_k2, diff_subln_g, w_out, ffn_norm_g, w_ff1, w_ff2, final_norm_g):
    bsz, seq_len, _ = x.shape
    cos, sin = rope_tables(seq_len, HEAD_DIM)
    cos = cos.astype(x.dtype)
    sin = sin.astype(x.dtype)
    c_act = jax.nn.silu(c)
    for layer in range(DEPTH_2):
        lambda_init = 0.8 - 0.6 * math.exp(-0.3 * layer)
        mod = c_act @ ada_w[layer] + ada_b[layer]
        sh_m, sc_m, g_m, sh_f, sc_f, g_f = [m[:, None, :] for m in jnp.split(mod, N_MOD, axis=-1)]

        h = rms_norm_2(x, mix_norm_g[layer]) * (1.0 + sc_m) + sh_m
        proj = h @ w_in[layer]
        dq, dk, dv, sq, sk, sv = jnp.split(proj, 6, axis=-1)
        dq = dq.reshape(bsz, seq_len, N_DIFF_HEADS, 2, HEAD_DIM).transpose(0, 2, 3, 1, 4)
        dk = dk.reshape(bsz, seq_len, N_DIFF_HEADS, 2, HEAD_DIM).transpose(0, 2, 3, 1, 4)
        dv = dv.reshape(bsz, seq_len, N_DIFF_HEADS, 2 * HEAD_DIM).transpose(0, 2, 1, 3)
        dq = apply_rope(dq, cos, sin)
        dk = apply_rope(dk, cos, sin)
        lam = (jnp.exp(jnp.sum(lambda_q1[layer].astype(jnp.float32) * lambda_k1[layer].astype(jnp.float32)))
               - jnp.exp(jnp.sum(lambda_q2[layer].astype(jnp.float32) * lambda_k2[layer].astype(jnp.float32)))
               + lambda_init)
        o_diff = diff_attention(dq, dk, dv, lam, diff_subln_g[layer], lambda_init)
        o_diff = o_diff.transpose(0, 2, 1, 3).reshape(bsz, seq_len, DIFF_WIDTH)

        sq = sq.reshape(bsz, seq_len, N_SB_HEADS, HEAD_DIM).transpose(0, 2, 1, 3)
        sk = sk.reshape(bsz, seq_len, N_SB_HEADS, HEAD_DIM).transpose(0, 2, 1, 3)
        sv = sv.reshape(bsz, seq_len, N_SB_HEADS, HEAD_DIM).transpose(0, 2, 1, 3)
        o_sb = stick_breaking_attention(sq, sk, sv)
        o_sb = o_sb.transpose(0, 2, 1, 3).reshape(bsz, seq_len, SB_WIDTH)

        mixed = jnp.concatenate([o_diff, o_sb], axis=-1) @ w_out[layer]
        x = x + g_m * mixed

        h = rms_norm_2(x, ffn_norm_g[layer]) * (1.0 + sc_f) + sh_f
        f = jnp.square(jax.nn.relu(h @ w_ff1[layer])) @ w_ff2[layer]
        x = x + g_f * f
    return rms_norm_2(x, final_norm_g)


def setup_inputs(seed=0):
    out = dict(first_inputs(seed))
    for name, value in second_inputs(seed + 1).items():
        if name != "x":
            out[name + "_2"] = value
    return out


def reference(
    x, mem, norm_mix, norm_mem, norm_ffn, w_mem_kv, g_mq, g_mk, fox_w_in, fox_b_f, fox_g_q,
    fox_g_k, fox_w_out, conv_w_in, conv_b_in, conv_dw, conv_dw_b, conv_ln_g, conv_ln_b,
    conv_w_out, ffn_w_gate, ffn_w_up, ffn_w_down, moe_router, moe_w_gate, moe_w_up, moe_w_down,
    c_2, ada_w_2, ada_b_2, mix_norm_g_2, w_in_2, lambda_q1_2, lambda_k1_2, lambda_q2_2,
    lambda_k2_2, diff_subln_g_2, w_out_2, ffn_norm_g_2, w_ff1_2, w_ff2_2, final_norm_g_2,
):
    x = first_block(
        x, mem, norm_mix, norm_mem, norm_ffn, w_mem_kv, g_mq, g_mk, fox_w_in, fox_b_f, fox_g_q,
        fox_g_k, fox_w_out, conv_w_in, conv_b_in, conv_dw, conv_dw_b, conv_ln_g, conv_ln_b,
        conv_w_out, ffn_w_gate, ffn_w_up, ffn_w_down, moe_router, moe_w_gate, moe_w_up,
        moe_w_down,
    )
    return second_block(
        x, c_2, ada_w_2, ada_b_2, mix_norm_g_2, w_in_2, lambda_q1_2, lambda_k1_2, lambda_q2_2,
        lambda_k2_2, diff_subln_g_2, w_out_2, ffn_norm_g_2, w_ff1_2, w_ff2_2, final_norm_g_2,
    )


_drawn_inputs = setup_inputs


def setup_inputs(seed=0):
    import zlib

    import numpy as np

    out = dict(_drawn_inputs(seed))
    spreads = {}
    factors = {'norm_mix': 3.631,
     'norm_mem': 8.0,
     'g_mq': 8.0,
     'g_mk': 8.0,
     'fox_g_q': 8.0,
     'fox_g_k': 7.895,
     'conv_b_in': 3.987,
     'conv_dw_b': 3.052,
     'conv_ln_g': 4.541,
     'conv_ln_b': 5.178,
     'ada_b_2': 3.416,
     'mix_norm_g_2': 8.0,
     'lambda_q1_2': 8.0,
     'lambda_k1_2': 8.0,
     'lambda_k2_2': 8.0,
     'diff_subln_g_2': 158.892,
     'ffn_norm_g_2': 18.603,
     'final_norm_g_2': 23.795}
    for name, (base, spread) in spreads.items():
        noise = np.random.default_rng([zlib.crc32(name.encode()), seed]).standard_normal(out[name].shape)
        drawn = base * np.exp(spread * noise) if base else spread * noise
        out[name] = __import__('jax').numpy.asarray(drawn.astype(out[name].dtype))
    for name, factor in factors.items():
        out[name] = (out[name] * factor).astype(out[name].dtype)
    return out
```

```python
from contextlib import ExitStack

import numpy as np

import concourse.bass as bass
from concourse import mybir

F32 = mybir.dt.float32
I32 = mybir.dt.int32
U32 = mybir.dt.uint32
ALU = mybir.AluOpType
ACT = mybir.ActivationFunctionType
AX_X = mybir.AxisListType.X

P = 128
D = 1024
KT = D // P
T = 256
TT = T // P
HD = 64
FOX_HEADS = 12
MEM_HEADS = 4
FOX = FOX_HEADS * HD
MEM = MEM_HEADS * HD
CONV = 768
CT = CONV // P
TAPS = 31
PAD = TAPS - 1
FF0 = 2816
E = 8
EFF = 3584
EFT = EFF // P
CAP = 96
EXTRA = 5
MAXBLK = E + EXTRA
FF2 = 4096
EPS = 1e-6
NEG = -1e30
SCALE = HD ** -0.5
LAMBDA_INIT = 0.2
SLOTS = 7
UW = 4096

C_ID, C_HEAD, C_ONES, C_ROT, C_SUF, C_TRI = (P * j for j in range(6))
C_COS = 6 * P
C_SIN = C_COS + T
C_FOXM = C_SIN + T
C_DIFM = C_FOXM + P
C_SBM = C_DIFM + P
C_IOTA = C_SBM + P
C_SID = C_IOTA + CAP
C_EI = C_SID + 1
C_LT = C_EI + E
C_XI = C_LT + E * E
C_END = C_XI + EXTRA * E


def constants():
    c = np.zeros((P, C_END), np.float32)
    r = np.arange(P)
    c[:, C_ID:C_ID + P] = np.eye(P)
    c[:, C_HEAD:C_HEAD + P] = r[:, None] // HD == r[None, :] // HD
    c[:, C_ONES:C_ONES + P] = 1.0
    for d in range(P):
        if d % HD < HD // 2:
            c[d + HD // 2, C_ROT + d] = -1.0
        else:
            c[d - HD // 2, C_ROT + d] = 1.0
    c[:, C_SUF:C_SUF + P] = r[:, None] > r[None, :]
    c[:, C_TRI:C_TRI + P] = r[:, None] <= r[None, :]
    inv = (np.float32(1.0) / (np.float32(10000.0) ** (np.arange(0, HD, 2, dtype=np.float32) / np.float32(HD))))
    ang = np.arange(T, dtype=np.float32)[:, None] * inv[None, :].astype(np.float32)
    ang = np.concatenate([ang, ang], -1).T
    c[:, C_COS:C_COS + T] = np.tile(np.cos(ang), (2, 1))
    c[:, C_SIN:C_SIN + T] = np.tile(np.sin(ang), (2, 1))
    c[:, C_FOXM:C_FOXM + P] = np.where(r[None, :] <= r[:, None], 0.0, NEG)
    c[:, C_DIFM:C_DIFM + P] = np.where(r[None, :] // 64 <= r[:, None] // 64, 0.0, NEG)
    c[:, C_SBM:C_SBM + P] = r[None, :] > r[:, None]
    c[:, C_IOTA:C_IOTA + CAP] = np.arange(CAP)[None, :]
    c[:, C_SID] = r
    c[:, C_EI:C_EI + E] = np.arange(E)[None, :]
    e = np.arange(E)
    c[:, C_LT:C_LT + E * E] = (e[None, :] < e[:, None]).reshape(1, -1)
    c[:, C_XI:C_XI + EXTRA * E] = np.repeat(np.arange(EXTRA), E)[None, :]
    return c


V_MIX, V_MEM, V_FFN = 0, 16, 32
V_CB, V_DWB, V_LNG, V_LNB = 48, 60, 66, 72
V_MIX2, V_FFN2, V_FIN2, V_C = 78, 86, 94, 102
V_SUB, V_FGQ, V_FGK, V_GMQ, V_GMK, V_LQ, V_LK = 110, 111, 112, 113, 115, 117, 118
V_ROWS = 119
V_ADA = V_ROWS
V_TAP = V_ADA + 48
V_END = V_TAP + TAPS * CT
TAPS_A = 16


class Sessions:

    def __init__(self):
        self.fills, self.drains, self.at = [0] * 8, [0] * 8, {}

    def add(self, name, bank, own_signal=False):
        assert name not in self.at, name
        self.at[name] = (bank, self.fills[bank] + 1, self.drains[bank])
        self.drains[bank] += 1
        if not own_signal:
            self.fills[bank] += 1


def build(nc, A, cst_dram, out):
    ctx = ExitStack()
    with ctx:
        def sb(name, shape, dt=F32):
            return ctx.enter_context(nc.sbuf_tensor(name, shape, dt))

        sems = {}

        def sem(name):
            if name not in sems:
                sems[name] = ctx.enter_context(nc.semaphore(name))
            return sems[name]

        ring = sb("ring", [P, SLOTS, UW])
        hT = sb("hT", [P, KT, T])
        actT = sb("actT", [P, KT, T])
        mixT = sb("mixT", [P, KT, T])
        big = sb("big", [P, 8192])
        sqz = sb("sqz", [P, 2048])
        cst = sb("cst", [P, C_END])
        cols = sb("cols", [P, V_END])
        mkz1 = sb("mkz1", [P, MEM_HEADS, T])
        mv1 = sb("mv1", [P, TT, MEM])
        att_p = sb("att_p", [P, 3, 512])
        att_pT = sb("att_pT", [P, 2, 512])
        rn = sb("rn", [P, T])
        negc = sb("negc", [P, T])
        bf_row = sb("bf_row", [P, FOX_HEADS])
        lsf = sb("lsf", [P, 2, TT, FOX_HEADS])
        ctok = sb("ctok", [P, TT, FOX_HEADS])
        nmx = sb("nmx", [P, 3, TT])
        ssum = sb("ssum", [P, 3, TT])
        rsum = sb("rsum", [P, 3, TT])
        gq8 = sb("gq8", [P, 3])
        ccol = sb("ccol", [P, KT])
        mod = sb("mod", [P, 48])
        gs = sb("gs", [P, 2, KT])
        lam = sb("lam", [P, 8])
        rt = sb("rt", [P, KT, E])
        mx8 = sb("mx8", [P, TT, 8])
        ix8 = sb("ix8", [P, TT, 8], U32)
        lg = sb("lg", [P, TT, E])
        ixf = sb("ixf", [P, TT, 2])
        oh = sb("oh", [P, 2, TT, E])
        plan_f = sb("plan_f", [P, 16, 16])
        lt8 = sb("lt8", [P, E, E])
        kcol = sb("kcol", [P, 2, TT])
        gcol = sb("gcol", [P, 2, TT])
        pexp = sb("pexp", [P, 32])
        etab = sb("etab", [1, 16], I32)
        nbt = sb("nbt", [1, 2], I32)

        def cc(at, n=P):
            return cst[:, at:at + n]

        ident, headones, ones, rot = cc(C_ID), cc(C_HEAD), cc(C_ONES), cc(C_ROT)
        sufx, tri = cc(C_SUF), cc(C_TRI)

        def flat(t):
            return t[:, :, :].rearrange("p a b -> p (a b)")

        def view(at, a, b, base=None):
            return (big if base is None else base)[:, at:at + a * b].rearrange("p (a b) -> p a b", a=a)

        qT = view(0, 8, T)
        kz = view(2048, 16, T)
        vv = view(6144, TT, 1024)
        x_tok = view(0, TT, D)
        mem_tok = view(2048, TT, D)
        mn1 = view(0, KT, T)
        aT = view(0, 32, T)
        upad = view(0, CT, PAD + T)
        cacc = view(1792, CT, T)
        abuf = view(3328, CT, T)
        q1 = view(4864, 2, T)
        maT = view(0, EFT, CAP)
        krow = view(4096, 4, T)
        sel = view(5120, TT, CAP)
        scat = big[:, 5376:5376 + T]
        scat_b = big[:, 5632:5632 + T]
        memT = mixT
        rows = flat(actT)[:, 0:512].rearrange("p (a b) -> p a b", a=4)
        selh = sqz[:, 0:FOX_HEADS * P].rearrange("p (h m) -> p h m", h=FOX_HEADS)
        z_tok = sqz[:, :].rearrange("p (a b) -> p a b", a=TT)
        out_tok = z_tok
        qk_sq = att_pT[:, 0, :]
        qk_r = att_pT[:, 1, :]
        xgT = flat(actT)[:, 0:KT * CAP].rearrange("p (a b) -> p a b", a=KT)
        yT = flat(mixT)[:, 0:KT * CAP].rearrange("p (a b) -> p a b", a=KT)
        y_tok = flat(mixT)[:, 1024:2048]
        sg = att_p
        sb_l = sqz[:, 0:768].rearrange("p (a b) -> p a b", a=2)
        sb_b = sqz[:, 768:1536].rearrange("p (a b) -> p a b", a=2)
        att_flat = flat(att_p)
        sb_m = att_flat[:, 0:768].rearrange("p (a b) -> p a b", a=2)
        sb_a = att_flat[:, 768:1536].rearrange("p (a b) -> p a b", a=2)

        ps = ctx.enter_context(nc.psum_tensor("ps", [P, 8, 512], F32))

        units = []

        def kview(w):
            return w.rearrange("(k p) n -> p k n", p=P)

        def add_cols(name, w, a, b):
            units.append((name, kview(w)[:, :, a:b], KT, b - a))

        def add_rows(name, w, n_tiles, per=4):
            for j in range(0, n_tiles, per):
                n = min(per, n_tiles - j)
                units.append((f"{name}{j // per}", kview(w)[:, j:j + n, :], n, D))

        for layer in range(2):
            add_cols(f"memkv{layer}", A["w_mem_kv"][layer], 0, 2 * MEM)
        fox_w = A["fox_w_in"][0]
        add_cols("foxf", fox_w, 3 * FOX, 3 * FOX + FOX_HEADS + MEM)
        for j in range(3):
            add_cols(f"foxqk{j}", fox_w, 512 * j, 512 * j + 512)
        add_cols("foxv0", fox_w, 2 * FOX, 2 * FOX + 512)
        add_cols("foxv1", fox_w, 2 * FOX + 512, 3 * FOX)
        for j in range(2):
            add_cols(f"foxout{j}", A["fox_w_out"][0], 512 * j, 512 * j + 512)
        FF0_CH = -(-FF0 // 512)
        for c in range(FF0_CH):
            add_cols(f"ffg{c}", A["ffn_w_gate"][0], 512 * c, min(FF0, 512 * c + 512))
            add_cols(f"ffu{c}", A["ffn_w_up"][0], 512 * c, min(FF0, 512 * c + 512))
        add_rows("ffd", A["ffn_w_down"][0], FF0 // P)
        for j in range(4):
            add_cols(f"convin{j}", A["conv_w_in"][0], 512 * j, min(2 * CONV + MEM, 512 * j + 512))
        for j in range(12):
            add_cols(f"ada{j}", A["ada_w_2"][0], 512 * j, 512 * j + 512)
        for j in range(2):
            add_cols(f"convout{j}", A["conv_w_out"][0], 512 * j, 512 * j + 512)
        U0 = len(units)
        MOE_CH = EFF // 512
        MOE_UNITS = 3 * MOE_CH
        assert MOE_UNITS % SLOTS == 0
        for j in range(6):
            add_cols(f"win{j}", A["w_in_2"][0], 512 * j, 512 * j + 512)
        for j in range(2):
            add_cols(f"wout{j}", A["w_out_2"][0], 512 * j, 512 * j + 512)
        for j in range(8):
            add_cols(f"ffa{j}", A["w_ff1_2"][0], 512 * j, 512 * j + 512)
        add_rows("ffb", A["w_ff2_2"][0], FF2 // P)
        number = {u[0]: n for n, u in enumerate(units)}
        gate_dram = A["moe_w_gate"][0].rearrange("e (k p) f -> e p k f", p=P)
        up_dram = A["moe_w_up"][0].rearrange("e (k p) f -> e p k f", p=P)
        down_dram = A["moe_w_down"][0].rearrange("e (k p) n -> e p k n", p=P)

        S = Sessions()
        for j in range(4):
            S.add(f"memT{j}", j)
        for j in range(4):
            S.add(f"xT{j}", 4 + j)
        S.add("colsT", 0)
        S.add("nsum0", 1)
        S.add("nsum1", 2)
        S.add("mk0", 3)
        S.add("mv0", 0)
        S.add("qsum0", 4)
        S.add("mk1", 1)
        S.add("mv1", 2)
        S.add("qsum1", 5)
        S.add("lam", 7)
        S.add("foxf", 3)
        S.add("mq0", 0)
        S.add("qsum2", 4)
        S.add("cum", 6)
        for j in range(6):
            S.add(f"foxqk{j}", (1 + j) % 4)
            S.add(f"qsum{3 + j}", (5, 4)[j % 2])
        S.add("foxv0", 3)
        S.add("foxv1", 0)
        S.add("foxv2", 1)

        maps = []

        def add_maps(stage, kinds):
            first = len(maps)
            for m in kinds:
                maps.append(dict(m, stage=stage))
            return range(first, len(maps))

        fox_maps = add_maps("fox", [
            dict(kind="fox" if h < FOX_HEADS else "mem", head=h, q=qT[:, h // 2, :], k=kz[:, h, :],
                 v=[vv[:, t, HD * h:HD * h + HD] for t in range(TT)], row=HD * (h % 2), m=HD, to=h // 2)
            for h in range(FOX_HEADS + MEM_HEADS)])
        mem_maps = add_maps("mem", [
            dict(kind="mem", head=h, q=q1[:, h // 2, :], k=mkz1[:, h, :],
                 v=[mv1[:, t, HD * h:HD * h + HD] for t in range(TT)], row=HD * (h % 2), m=HD, to=CT + h // 2)
            for h in range(MEM_HEADS)])
        diff_maps = add_maps("diff", [
            dict(kind="diff", head=m, q=qT[:, m // 2, :], k=kz[:, m, :],
                 v=[vv[:, t, P * (m // 2):P * (m // 2) + P] for t in range(TT)], row=0, m=P, to=m // 2)
            for m in range(8)])

        T_LAG, PV_LAG = 2, 3

        def add_attention(rng):
            n, a0 = len(rng), rng[0]
            for i in range(n + PV_LAG):
                if i < n:
                    S.add(f"sc{a0 + i}", (a0 + i) % 2)
                if 0 <= i - T_LAG < n:
                    S.add(f"pT{a0 + i - T_LAG}", 2 + (a0 + i) % 2)
                if 0 <= i - PV_LAG < n and (i - PV_LAG) % 2 == 0:
                    g = (a0 + i - PV_LAG) // 2
                    S.add(f"pv{g}", 4 + g % 2, own_signal=True)

        add_attention(fox_maps)
        for j in range(4):
            S.add(f"foxout{j}", j)
        S.add("nsum2", 6)
        FF0_PAIRS = FF0 // T
        for p in range(FF0_PAIRS):
            S.add(f"ffg{p}", 2 * (p % 2))
            S.add(f"ffu{p}", 2 * (p % 2) + 1)
        for j in range(4):
            S.add(f"ffd{j}", 4 + j)
        S.add("nsum3", 0)
        for j in range(7):
            S.add(f"convin{j}", (1 + j) % 4)
        S.add("qsum9", 4)
        add_attention(mem_maps)
        S.add("ada", 6)
        S.add("lnsum", 7)
        S.add("lnvar", 7)
        for j in range(4):
            S.add(f"convout{j}", j)
        S.add("nsum4", 4)
        S.add("router", 5)
        for j in range(4):
            S.add(f"ztok{j}", j)
        S.add("mcum", 5)
        S.add("krow", 6)
        S.add("grow", 7)
        for j in range(2):
            S.add(f"gather{j}", 4 + j)
        before_moe = list(S.drains)
        for j in range(2):
            S.add(f"ytok{j}", 6 + j)
        for j in range(4):
            S.add(f"scat{j}", 4 + j)
        S.add("nsum5", 0)
        for j, name in enumerate(["dq0", "dq1", "dk0", "dk1", "dv0", "dv1", "sq0", "sq1", "sk0", "sk1", "sv0", "sv1"]):
            S.add(name, (1 + j) % 4)
            if j < 4:
                S.add(f"rot{j}", 4 + j % 2)
        add_attention(diff_maps)
        SBH = 8
        for i in range(SBH + 2):
            if i < SBH:
                S.add(f"sbs{i}", i % 2)
            if 0 <= i - 1 < SBH:
                S.add(f"sbx{i - 1}", 2 + (i - 1) % 2)
            if 0 <= i - 2 < SBH and i % 2 == 0:
                S.add(f"sbo{(i - 2) // 2}", 4 + (i // 2) % 2, own_signal=True)
        S.add("sub0", 6)
        S.add("sub1", 7)
        for j in range(4):
            S.add(f"wout{j}", j)
        S.add("nsum6", 4)
        for p in range(16):
            S.add(f"ffa{p}", p % 4)
        for j in range(4):
            S.add(f"ffb{j}", 4 + j)
        S.add("nsum7", 0)
        for j in range(4):
            S.add(f"outT{j}", 1 + j)

        def bank(name):
            return ps[:, S.at[name][0], :]

        def claim(pe, name):
            b, _, k = S.at[name]
            if k:
                pe.wait_ge(sem(f"drained{b}"), k)

        def wait_filled(eng, name):
            b, k, _ = S.at[name]
            eng.wait_ge(sem(f"filled{b}"), k)

        def wait_drained(eng, name):
            b, _, k = S.at[name]
            eng.wait_ge(sem(f"drained{b}"), k + 1)

        def filled(name):
            return sem(f"filled{S.at[name][0]}")

        def drained(name):
            return sem(f"drained{S.at[name][0]}")

        last_use = {"memkv0": "mv0", "memkv1": "mv1", "foxf": "mq0", "foxqk0": "foxqk1", "foxqk1": "foxqk3",
                    "foxqk2": "foxqk5", "foxv0": "foxv1", "foxv1": "foxv2", "foxout0": "foxout1",
                    "foxout1": "foxout3", "convin0": "convin1", "convin1": "convin3", "convin2": "convin5",
                    "convin3": "convin6", "ada11": "ada", "convout0": "convout1", "convout1": "convout3",
                    "ffd5": "ffd3", "ffb7": "ffb3", "win0": "dq1", "win1": "dk1", "win2": "dv1", "win3": "sq1",
                    "win4": "sk1", "win5": "sv1", "wout0": "wout1", "wout1": "wout3"}
        for c in range(FF0_CH):
            last_use[f"ffg{c}"] = f"ffg{min(2 * c + 1, FF0_PAIRS - 1)}"
            last_use[f"ffu{c}"] = f"ffu{min(2 * c + 1, FF0_PAIRS - 1)}"
        for c in range(8):
            last_use[f"ffa{c}"] = f"ffa{2 * c + 1}"
        used_count = {}
        for name, *_ in units:
            if name not in last_use:
                used_count[name] = len(used_count) + 1

        def wait_unit_read(sp, n):
            name = units[n][0]
            if name in last_use:
                wait_filled(sp, last_use[name])
            else:
                sp.wait_ge(sem("ring_used"), used_count[name])

        def slot_of(n):
            return n % SLOTS

        def unit_ap(n):
            _, _, k, w = units[n]
            return ring[:, slot_of(n), 0:k * w].rearrange("p (k n) -> p k n", k=k)

        def wait_unit(pe, name, nb=None):
            n = number[name]
            turns = 16 * (n // SLOTS + 1)
            if n >= U0:
                turns = nb * (16 * MOE_UNITS // SLOTS) + turns
            pe.wait_ge(sem(f"ring_loaded{slot_of(n)}"), turns)
            return unit_ap(n)

        n_norm = 8
        NORM_GAIN = {1: V_MIX, 2: V_FFN, 3: V_MIX + 8, 4: V_FFN + 8}

        block = ctx.enter_context(nc.Block())

        @block.sync
        def _(sp):
            def load(n):
                _, src, k, w = units[n]
                sp.dma_start(unit_ap(n), src).then_inc(sem(f"ring_loaded{slot_of(n)}"), 16)

            for n in range(U0):
                if n >= SLOTS:
                    wait_unit_read(sp, n - SLOTS)
                load(n)

            def load_expert(j, e):
                s = (U0 + j) % SLOTS
                if j < 2 * MOE_CH:
                    w, c = (gate_dram, up_dram)[j % 2], j // 2
                    src = w[e, :, :, 512 * c:512 * c + 512]
                    dst = ring[:, s, :].rearrange("p (k n) -> p k n", k=KT)
                else:
                    c = j - 2 * MOE_CH
                    src = down_dram[e, :, 4 * c:4 * c + 4, :]
                    dst = ring[:, s, :].rearrange("p (k n) -> p k n", k=4)
                if len(src.shape) == 4:
                    src = src.rearrange("a p k n -> p (a k) n")
                sp.dma_start(dst, src).then_inc(sem(f"ring_loaded{s}"), 16)

            def wait_expert_read(j, i):
                if j < 2 * MOE_CH:
                    c, side = j // 2, j % 2
                    b = 2 * (c % 2) + side
                    sp.wait_ge(sem(f"moe_filled{b}"), i * (4 - c % 2) + c // 2 + 1)
                elif j < MOE_UNITS - 1:
                    sp.wait_ge(sem("moe_down_read"), i * (MOE_CH - 1) + (j - 2 * MOE_CH) + 1)
                else:
                    sp.wait_ge(sem("moe_filled5"), i * 2 + 2)

            for j in range(MOE_UNITS):
                if j < SLOTS:
                    wait_unit_read(sp, U0 + j - SLOTS)
                else:
                    wait_expert_read(j - SLOTS, 0)
                load_expert(j, slice(0, 1))
            sp.wait_ge(sem("moe_plan"), 2)
            last = sp.value_load(nbt[0:1, 1:2], min_val=E - 1, max_val=MAXBLK - 1)
            with sp.Fori(0, last) as i:
                e = sp.value_load(etab[0:1, bass.ds(i + 1, 1)], min_val=0, max_val=E - 1)
                for j in range(MOE_UNITS):
                    if j < SLOTS:
                        wait_expert_read(j + MOE_UNITS - SLOTS, i)
                    else:
                        wait_expert_read(j - SLOTS, i + 1)
                    load_expert(j, bass.ds(e, 1))
            for n in range(U0, len(units)):
                if n - U0 < SLOTS:
                    wait_expert_read(MOE_UNITS - SLOTS + n - U0, last)
                else:
                    wait_unit_read(sp, n - SLOTS)
                load(n)
            for t in range(TT):
                for half in range(2):
                    wait_drained(sp, f"outT{2 * t + half}")
                sp.dma_start(out[0, P * t:P * t + P, :], out_tok[:, t, :]).then_inc(sem("stored"), 16)
            sp.wait_ge(sem("stored"), 16 * TT)

        @block.gpsimd
        def _(pool):
            def row(lot, at, src, n):
                pool.dma_start(rows[at:at + n, lot, :], src).then_inc(sem("ld_rows"), 16)

            def vec(src):
                return src.rearrange("a (c p) -> (a c) p", p=P)

            row(0, V_MIX, vec(A["norm_mix"]), 16)
            row(0, V_MEM, vec(A["norm_mem"]), 16)
            row(0, V_FFN, vec(A["norm_ffn"]), 16)
            row(0, V_CB, vec(A["conv_b_in"]), 12)
            row(0, V_DWB, vec(A["conv_dw_b"]), 6)
            row(0, V_LNG, vec(A["conv_ln_g"]), 6)
            row(0, V_LNB, vec(A["conv_ln_b"]), 6)
            row(0, V_MIX2, vec(A["mix_norm_g_2"]), 8)
            row(0, V_FFN2, vec(A["ffn_norm_g_2"]), 8)
            row(0, V_FIN2, A["final_norm_g_2"].rearrange("(c p) -> c p", p=P), 8)
            row(0, V_C, vec(A["c_2"]), 8)
            row(0, V_SUB, A["diff_subln_g_2"], 1)

            def twin(at, first, second, n):
                pool.dma_start(rows[at:at + n, 0, 0:HD], first).then_inc(sem("ld_rows"), 16)
                pool.dma_start(rows[at:at + n, 0, HD:P], second).then_inc(sem("ld_rows"), 16)

            twin(V_FGQ, A["fox_g_q"], A["fox_g_q"], 1)
            twin(V_FGK, A["fox_g_k"], A["fox_g_k"], 1)
            twin(V_GMQ, A["g_mq"], A["g_mq"], 2)
            twin(V_GMK, A["g_mk"], A["g_mk"], 2)
            twin(V_LQ, A["lambda_q1_2"], A["lambda_q2_2"], 1)
            twin(V_LK, A["lambda_k1_2"], A["lambda_k2_2"], 1)
            row(1, 0, vec(A["ada_b_2"]), 48)
            taps = A["conv_dw"].rearrange("a t (c p) -> (a t c) p", p=P)
            row(2, 0, taps[0:TAPS_A * CT, :], TAPS_A * CT)
            row(3, 0, taps[TAPS_A * CT:TAPS * CT, :], (TAPS - TAPS_A) * CT)

            def zero_keys(keys, name):
                pool.memset(keys[:, :, :], 0.0).then_inc(sem(name), 1)

            zero_keys(mkz1, "keys_zeroed")
            pool.memset(negc[:, :], 0.0).then_inc(sem("negc_zeroed"), 1)
            for j in range(4):
                wait_filled(pool, f"memT{j}")
            zero_keys(kz, "keys_zeroed")

            def normalise(rng):
                for a in rng:
                    w0, w1 = (P, 3 * P) if maps[a]["kind"] != "mem" else (T, 2 * T)
                    pool.wait_ge(sem("att_rsum"), a + 1)
                    pool.tensor_scalar(att_p[:, a % 3, 0:w0], att_p[:, a % 3, 0:w0], rsum[:, a % 3, 0:1], None,
                                       ALU.mult).then_inc(sem("att_probs"), 1)
                    pool.tensor_scalar(att_p[:, a % 3, w0:w1], att_p[:, a % 3, w0:w1], rsum[:, a % 3, 1:2], None,
                                       ALU.mult).then_inc(sem("att_probs"), 1)

            normalise(fox_maps)
            pool.wait_ge(sem("norm_sq"), 4)
            pool.memset(upad[:, :, 0:PAD], 0.0).then_inc(sem("upad_zeroed"), 1)
            normalise(mem_maps)
            wait_filled(pool, "convout3")
            pool.memset(yT[:, :, :], 0.0).then_inc(sem("moe_zeroed"), 1)
            pool.memset(scat, 0.0).then_inc(sem("moe_zeroed"), 1)
            pool.wait_ge(sem("norm_sq"), 6)
            zero_keys(kz, "keys_zeroed")
            normalise(diff_maps)

            sbm = cc(C_SBM)
            for i in range(SBH + 1):
                if i < SBH:
                    b = i % 2
                    pool.wait_ge(sem("sb_m"), i + 1)
                    for at in (0, 2 * P):
                        pool.tensor_tensor(sb_m[:, b, at:at + P], sb_m[:, b, at:at + P], sbm,
                                           ALU.mult).then_inc(sem("sb_masked"), 1)
                if i >= 1:
                    b = (i - 1) % 2
                    pool.wait_ge(sem("sb_exp"), i)
                    for at in (0, 2 * P):
                        pool.tensor_tensor(sb_a[:, b, at:at + P], sb_a[:, b, at:at + P], sbm,
                                           ALU.mult).then_inc(sem("sb_probs"), 1)

        N_ROWS = 16 * (12 + 12 + 3)

        @block.scalar
        def _(act):
            act.dma_start(mem_tok, A["mem"][0].rearrange("(t p) d -> p t d", p=P)).then_inc(sem("ld_mem"), 16)
            act.dma_start(x_tok, A["x"][0].rearrange("(t p) d -> p t d", p=P)).then_inc(sem("ld_x"), 16)
            act.dma_start(cst[:, :], cst_dram).then_inc(sem("ld_cst"), 16)
            act.dma_start(bf_row[:, :], A["fox_b_f"].broadcast_to([P, FOX_HEADS])).then_inc(sem("ld_bf"), 16)
            act.dma_start(rt[:, :, :], A["moe_router"][0].rearrange("(k p) e -> p k e", p=P)).then_inc(sem("ld_rt"), 16)

            step = [0]

            def link(ins):
                step[0] += 1
                ins.then_inc(sem("act_step"), 1)
                act.wait_ge(sem("act_step"), step[0])

            for j in range(4):
                wait_filled(act, f"memT{j}")
                act.activation(memT[:, 2 * j:2 * j + 2, :].rearrange("p a b -> p (a b)"), bank(f"memT{j}"),
                               ACT.Copy).then_inc(drained(f"memT{j}"), 1)

            def norm_sq(k, src):
                if k:
                    wait_filled(act, f"nsum{k - 1}")
                act.activation(sqz[:, :], flat(src), ACT.Square).then_inc(sem("norm_sq"), 1)

            def norm_sd(k):
                wait_drained(act, f"nsum{k}")
                act.activation(rn[:, :], rn[:, :], ACT.Sqrt).then_inc(sem("norm_sd"), 1)

            def qk_square(k, name):
                wait_filled(act, name)
                if k:
                    wait_filled(act, f"qsum{k - 1}")
                act.activation(qk_sq, bank(name), ACT.Square).then_inc(sem("qk_sq"), 1)

            def qk_sd(k):
                wait_drained(act, f"qsum{k}")
                act.activation(qk_r, qk_r, ACT.Sqrt).then_inc(sem("qk_sd"), 1)

            def copy_out(name, dst, src=None):
                wait_filled(act, name)
                act.activation(dst, bank(name) if src is None else src, ACT.Copy).then_inc(drained(name), 1)

            for j in range(4):
                wait_drained(act, f"memT{j}")
            norm_sq(0, memT)
            norm_sd(0)
            for j in range(4):
                wait_drained(act, f"xT{j}")
            norm_sq(1, hT)
            qk_square(0, "mk0")
            wait_filled(act, "mv0")
            act.wait_ge(sem("keys_zeroed"), 2)
            for t in range(TT):
                ins = act.activation(vv[:, t, FOX:D], bank("mv0")[:, MEM * t:MEM * t + MEM], ACT.Copy)
            ins.then_inc(drained("mv0"), 1)
            qk_sd(0)
            norm_sd(1)
            qk_square(1, "mk1")
            copy_out("mv1", flat(mv1))
            qk_sd(1)
            act.wait_ge(sem("cols_ready"), 1)
            act.activation(ccol[:, :], cols[:, V_C:V_C + KT], ACT.Silu).then_inc(sem("ccol_ready"), 1)
            wait_filled(act, "lam")
            act.activation(lam[:, 2:4], bank("lam")[:, 0:2], ACT.Exp).then_inc(drained("lam"), 1)
            act.wait_ge(sem("fox_negabs"), 1)
            link(act.activation(lsf[:, 1, :, :], lsf[:, 1, :, :], ACT.Exp))
            act.activation(lsf[:, 1, :, :], lsf[:, 1, :, :], ACT.Ln, bias=1.0).then_inc(sem("fox_log1p"), 1)
            qk_square(2, "mq0")
            qk_sd(2)
            act.wait_ge(sem("negc_zeroed"), 1)
            wait_filled(act, "cum")
            act.activation(negc[0:FOX_HEADS, :], bank("cum")[0:FOX_HEADS, 0:T], ACT.Copy,
                           scale=-1.0).then_inc(sem("negc_ready"), 1)
            for j in range(6):
                qk_square(3 + j, f"foxqk{j}")
                qk_sd(3 + j)
            for t in range(TT):
                copy_out(f"foxv{t}", vv[:, t, 0:512])
            wait_filled(act, "foxv2")
            for t in range(TT):
                ins = act.activation(vv[:, t, 512:FOX], bank("foxv2")[:, T * t:T * t + T], ACT.Copy)
            ins.then_inc(drained("foxv2"), 1)

            def attention(rng):
                n, a0 = len(rng), rng[0]
                for i in range(n + T_LAG):
                    if i < n:
                        a = a0 + i
                        w0, w1 = (P, 3 * P) if maps[a]["kind"] != "mem" else (T, 2 * T)
                        act.wait_ge(sem("att_max"), 2 * (a + 1))
                        for t, (lo, hi) in enumerate(((0, w0), (w0, w1))):
                            act.activation(att_p[:, a % 3, lo:hi], att_p[:, a % 3, lo:hi], ACT.Exp,
                                           bias=nmx[:, a % 3, t:t + 1],
                                           accum_out=ssum[:, a % 3, t:t + 1]).then_inc(sem("att_exp"), 1)
                    if i >= T_LAG:
                        a = a0 + i - T_LAG
                        w = 3 * P if maps[a]["kind"] != "mem" else 4 * P
                        wait_filled(act, f"pT{a}")
                        if a >= 2:
                            act.wait_ge(sem("att_pv"), a - 1)
                        act.activation(att_pT[:, a % 2, 0:w], bank(f"pT{a}")[:, 0:w],
                                       ACT.Copy).then_inc(drained(f"pT{a}"), 1)

            attention(fox_maps)

            for j in range(4):
                wait_drained(act, f"foxout{j}")
            norm_sq(2, hT)
            norm_sd(2)
            for p in range(FF0_PAIRS):
                wait_filled(act, f"ffg{p}")
                if p >= 2:
                    wait_drained(act, f"ffu{p - 2}")
                act.activation(sg[:, p % 2, :], bank(f"ffg{p}"), ACT.Silu).then_inc(drained(f"ffg{p}"), 1)
            for j in range(4):
                wait_drained(act, f"ffd{j}")
            norm_sq(3, hT)
            norm_sd(3)

            for j in range(3):
                wait_filled(act, f"convin{j}")
                for t in range(2):
                    ins = act.activation(abuf[:, 2 * j + t, :], bank(f"convin{j}")[:, T * t:T * t + T], ACT.Identity,
                                         bias=cols[:, V_CB + 2 * j + t:V_CB + 2 * j + t + 1])
                ins.then_inc(drained(f"convin{j}"), 1)
            for j in range(3):
                wait_filled(act, f"convin{3 + j}")
                for t in range(2):
                    c = 2 * j + t
                    ins = act.activation(cacc[:, c, :], bank(f"convin{3 + j}")[:, T * t:T * t + T], ACT.Sigmoid,
                                         bias=cols[:, V_CB + CT + c:V_CB + CT + c + 1])
                ins.then_inc(drained(f"convin{3 + j}"), 1)
            qk_square(9, "convin6")
            qk_sd(9)
            attention(mem_maps)
            act.wait_ge(sem("ln_centred"), 1)
            act.activation(sqz[:, 0:CT * T], flat(cacc), ACT.Square).then_inc(sem("ln_sq"), 1)
            wait_drained(act, "lnvar")
            act.activation(rn[:, :], rn[:, :], ACT.Sqrt).then_inc(sem("ln_sd"), 1)
            act.wait_ge(sem("ln_scaled"), 1)
            for c in range(CT):
                act.activation(mixT[:, c, :], cacc[:, c, :], ACT.Silu, bias=cols[:, V_LNB + c:V_LNB + c + 1],
                               scale=cols[:, V_LNG + c:V_LNG + c + 1]).then_inc(sem("conv_mixed"), 1)
            for j in range(4):
                wait_drained(act, f"convout{j}")
            norm_sq(4, hT)
            norm_sd(4)
            for j in range(4):
                copy_out(f"ztok{j}", z_tok[:, j // 2, 512 * (j % 2):512 * (j % 2) + 512])
            act.wait_ge(sem("gate_diff"), 1)
            act.activation(pexp[:, 0:2], pexp[:, 0:2], ACT.Exp).then_inc(sem("gate_exp"), 1)
            wait_drained(act, "router")
            for j in range(2):
                copy_out(f"gather{j}", xgT[:, 4 * j:4 * j + 4, :].rearrange("p a b -> p (a b)"),
                         bank(f"gather{j}")[:, 0:4 * CAP])

            act.wait_ge(sem("moe_plan"), 2)
            nb = act.value_load(nbt[0:1, 0:1], min_val=E, max_val=MAXBLK)
            with act.Fori(0, nb) as i:
                def silu(c):
                    b = 2 * (c % 2)
                    act.wait_ge(sem(f"moe_filled{b}"), i * (4 - c % 2) + c // 2 + 1)
                    if c >= 2:
                        act.wait_ge(sem(f"moe_drained{b + 1}"), i * (4 - c % 2) + c // 2)
                    elif c == 1:
                        act.wait_ge(sem("moe_drained3"), i * 3)
                    else:
                        act.wait_ge(sem("moe_drained1"), i * 4)
                    act.activation(sg[:, c % 2, 0:4 * CAP], ps[:, b, 0:4 * CAP],
                                   ACT.Silu).then_inc(sem(f"moe_drained{b}"), 1)

                silu(0)
                for j in range(2):
                    act.wait_ge(sem(f"moe_filled{6 + j}"), i * 3 + 1)
                    act.activation(y_tok[0:CAP, 512 * j:512 * j + 512], ps[0:CAP, 6 + j, :],
                                   ACT.Copy).then_inc(sem(f"moe_drained{6 + j}"), 1)
                for c in range(1, MOE_CH):
                    silu(c)
                for j in range(2):
                    act.wait_ge(sem(f"moe_filled{6 + j}"), i * 3 + 3)
                    act.activation(xgT[:, 4 * j:4 * j + 4, :].rearrange("p a b -> p (a b)"), ps[:, 6 + j, 0:4 * CAP],
                                   ACT.Copy).then_inc(sem(f"moe_drained{6 + j}"), 1)
                for j in range(2):
                    act.wait_ge(sem(f"moe_filled{4 + j}"), i * 2 + 2)
                    act.activation(yT[:, 4 * j:4 * j + 4, :].rearrange("p a b -> p (a b)"), ps[:, 4 + j, 0:4 * CAP],
                                   ACT.Copy).then_inc(sem(f"moe_drained{4 + j}"), 1)
            for j in range(2):
                wait_filled(act, f"ytok{j}")
                act.activation(y_tok[0:CAP, 512 * j:512 * j + 512], bank(f"ytok{j}")[0:CAP, :],
                               ACT.Copy).then_inc(drained(f"ytok{j}"), 1)

            for j in range(4):
                wait_drained(act, f"scat{j}")
            norm_sq(5, hT)
            norm_sd(5)
            act.wait_ge(sem("norm_out"), NORM_OUT_5)
            for k in range(KT):
                act.activation(actT[:, k, :], actT[:, k, :], ACT.Identity,
                               bias=mod[:, k:k + 1]).then_inc(sem("shifted"), 1)
            for j in range(4):
                name = ("dq0", "dq1", "dk0", "dk1")[j]
                wait_filled(act, name)
                if j:
                    act.wait_ge(sem("rope_done"), rope_count(j))
                act.activation(qk_sq, bank(name), ACT.Copy).then_inc(drained(name), 1)
            act.wait_ge(sem("rope_done"), rope_count(4))
            for t in range(TT):
                copy_out(f"dv{t}", vv[:, t, 0:512])
            for j in range(2):
                wait_filled(act, f"sq{j}")
                act.activation(qT[:, 4 + 2 * j:6 + 2 * j, :].rearrange("p a b -> p (a b)"), bank(f"sq{j}"), ACT.Copy,
                               scale=SCALE).then_inc(drained(f"sq{j}"), 1)
            act.wait_ge(sem("keys_zeroed"), 3)
            for j in range(2):
                wait_filled(act, f"sk{j}")
                src = bank(f"sk{j}").rearrange("p (a b) -> p a b", a=2)
                act.activation(kz[0:HD, 8 + 4 * j:12 + 4 * j:2, :], src[0:HD, :, :], ACT.Copy)
                act.activation(kz[HD:P, 9 + 4 * j:12 + 4 * j:2, :], src[HD:P, :, :],
                               ACT.Copy).then_inc(drained(f"sk{j}"), 1)
            for t in range(TT):
                copy_out(f"sv{t}", vv[:, t, 512:1024])
            attention(diff_maps)

            for i in range(SBH + 1):
                if i < SBH:
                    b = i % 2
                    wait_filled(act, f"sbs{i}")
                    if i >= 2:
                        wait_drained(act, f"sbs{i - 2}")
                    link(act.activation(sb_l[:, b, :], bank(f"sbs{i}")[:, 0:384], ACT.Abs))
                    link(act.activation(sb_l[:, b, :], sb_l[:, b, :], ACT.Exp, scale=-1.0))
                    act.activation(sb_l[:, b, :], sb_l[:, b, :], ACT.Ln, bias=1.0).then_inc(sem("sb_log1p"), 1)
                if i >= 1:
                    j = i - 1
                    wait_drained(act, f"sbx{j}")
                    if j >= 2:
                        act.wait_ge(sem("sb_pv"), j - 1)
                    act.activation(sb_a[:, j % 2, :], sb_b[:, j % 2, :], ACT.Exp).then_inc(sem("sb_exp"), 1)

            act.wait_ge(sem("att_pv"), len(maps))
            for j in range(2):
                for g in range(2):
                    wait_drained(act, f"pv{diff_maps[0] // 2 + 2 * j + g}")
                if j:
                    wait_filled(act, "sub0")
                act.activation(qk_sq, mixT[:, 2 * j:2 * j + 2, :].rearrange("p a b -> p (a b)"),
                               ACT.Square).then_inc(sem("sub_sq"), 1)
                wait_drained(act, f"sub{j}")
                act.activation(qk_r, qk_r, ACT.Sqrt).then_inc(sem("sub_sd"), 1)

            for j in range(4):
                wait_drained(act, f"wout{j}")
            norm_sq(6, hT)
            norm_sd(6)
            act.wait_ge(sem("norm_out"), NORM_OUT_5 + KT)
            for k in range(KT):
                act.activation(actT[:, k, :], actT[:, k, :], ACT.Identity,
                               bias=mod[:, 24 + k:25 + k]).then_inc(sem("shifted"), 1)
            for j in range(4):
                wait_drained(act, f"ffb{j}")
            norm_sq(7, hT)
            norm_sd(7)
            for j in range(4):
                copy_out(f"outT{j}", out_tok[:, j // 2, 512 * (j % 2):512 * (j % 2) + 512])

        @block.tensor
        def _(pe):
            mm = nc.tensor.matmul
            pe.wait_ge(sem("ld_cst"), 16)

            def turn(name, pieces, src_wait=None):
                claim(pe, name)
                for at, src in pieces:
                    n = src.shape[0]
                    ins = pe.transpose(bank(name)[:, at:at + n], src, ident[0:n, 0:n])
                ins.then_inc(filled(name), 1)

            pe.wait_ge(sem("ld_mem"), 16)
            for j in range(4):
                turn(f"memT{j}", [(T * k + P * t, mem_tok[:, t, P * (2 * j + k):P * (2 * j + k) + P])
                                  for k in range(2) for t in range(TT)])
            pe.wait_ge(sem("ld_x"), 16)
            for j in range(4):
                turn(f"xT{j}", [(T * k + P * t, x_tok[:, t, P * (2 * j + k):P * (2 * j + k) + P])
                                for k in range(2) for t in range(TT)])
            pe.wait_ge(sem("ld_rows"), N_ROWS)
            turn("colsT", [(0, rows[0:V_ROWS, 0, :]), (V_ADA, rows[0:48, 1, :]),
                           (V_TAP, rows[0:TAPS_A * CT, 2, :]),
                           (V_TAP + TAPS_A * CT, rows[0:(TAPS - TAPS_A) * CT, 3, :])])

            def norm_sum(k):
                pe.wait_ge(sem("norm_sq"), k + 1)
                claim(pe, f"nsum{k}")
                for j in range(KT):
                    ins = mm(bank(f"nsum{k}")[:, 0:T], ones, sqz[:, T * j:T * j + T], start=(j == 0), stop=(j == KT - 1))
                ins.then_inc(filled(f"nsum{k}"), 1)

            def head_sum(k):
                pe.wait_ge(sem("qk_sq"), k + 1)
                claim(pe, f"qsum{k}")
                mm(bank(f"qsum{k}"), headones, qk_sq, start=True, stop=True).then_inc(filled(f"qsum{k}"), 1)

            def pair(name, w, at, src, ready=None):
                claim(pe, name)
                for t in range(2):
                    for k in range(KT):
                        if ready is not None:
                            ready(k)
                        ins = mm(bank(name)[:, T * t:T * t + T], w[:, k, at + P * t:at + P * t + P], src[:, k, :],
                                 start=(k == 0), stop=(k == KT - 1))
                    ready = None
                ins.then_inc(filled(name), 1)

            def by_tokens(name, w, at, n, src, tiles):
                claim(pe, name)
                for c, t in enumerate(tiles):
                    for k in range(KT):
                        ins = mm(bank(name)[:, n * c:n * c + n], src[:, k, P * t:P * t + P], w[:, k, at:at + n],
                                 start=(k == 0), stop=(k == KT - 1))
                ins.then_inc(filled(name), 1)

            def normed(base):
                return lambda k: pe.wait_ge(sem("norm_out"), base + k + 1)

            norm_sum(0)
            norm_sum(1)
            w = wait_unit(pe, "memkv0")
            pair("mk0", w, 0, actT, normed(0))
            by_tokens("mv0", w, MEM, MEM, actT, (0, 1))
            head_sum(0)
            w = wait_unit(pe, "memkv1")
            pair("mk1", w, 0, mn1, normed(KT))
            by_tokens("mv1", w, MEM, MEM, mn1, (0, 1))
            head_sum(1)
            pe.wait_ge(sem("lam_prod"), 2)
            claim(pe, "lam")
            mm(bank("lam")[:, 0:2], ones, lam[:, 0:2], start=True, stop=True).then_inc(filled("lam"), 1)

            w = wait_unit(pe, "foxf")
            normed(2 * KT)(KT - 1)
            by_tokens("foxf", w, 0, FOX_HEADS, actT, (0, 1))
            pair("mq0", w, FOX_HEADS, actT)
            head_sum(2)
            pe.wait_ge(sem("fox_logf"), 1)
            claim(pe, "cum")
            lf = lsf[:, 0, :, :]
            cum = bank("cum")
            mm(cum[0:FOX_HEADS, 0:P], lf[:, 0, :], tri, start=True, stop=True)
            mm(cum[0:FOX_HEADS, P:T], lf[:, 0, :], ones, start=True, stop=False)
            mm(cum[0:FOX_HEADS, P:T], lf[:, 1, :], tri, start=False, stop=True)
            mm(cum[:, T:T + FOX_HEADS], tri, lf[:, 0, :], start=True, stop=True)
            mm(cum[:, T + FOX_HEADS:T + 2 * FOX_HEADS], ones, lf[:, 0, :], start=True, stop=False)
            mm(cum[:, T + FOX_HEADS:T + 2 * FOX_HEADS], tri, lf[:, 1, :], start=False,
               stop=True).then_inc(filled("cum"), 1)
            for j in range(6):
                if j % 2 == 0:
                    w = wait_unit(pe, f"foxqk{j // 2}")
                pair(f"foxqk{j}", w, 2 * P * (j % 2), actT)
                head_sum(3 + j)
            w = wait_unit(pe, "foxv0")
            for t in range(TT):
                by_tokens(f"foxv{t}", w, 0, 512, actT, (t,))
            w = wait_unit(pe, "foxv1")
            by_tokens("foxv2", w, 0, T, actT, (0, 1))

            def attention(rng):
                n, a0 = len(rng), rng[0]
                for i in range(n + PV_LAG):
                    if i < n:
                        a = a0 + i
                        m, s = maps[a], bank(f"sc{a}")
                        full = m["kind"] == "mem"
                        claim(pe, f"sc{a}")
                        for t, (at, nk) in enumerate(((0, T), (T, T)) if full else ((0, P), (P, T))):
                            fox = m["kind"] == "fox"
                            ins = mm(s[:, at:at + nk], m["q"][:, P * t:P * t + P], m["k"][:, 0:nk],
                                     start=True, stop=not fox)
                            if fox:
                                ins = mm(s[:, at:at + nk], selh[:, m["head"], :], negc[:, 0:nk],
                                         start=False, stop=True)
                        ins.then_inc(filled(f"sc{a}"), 1)
                    if 0 <= i - T_LAG < n:
                        a = a0 + i - T_LAG
                        pe.wait_ge(sem("att_probs"), 2 * (a + 1))
                        order = (0, 2, 1, 3) if maps[a]["kind"] == "mem" else (0, 1, 2)
                        turn(f"pT{a}", [(P * c, att_p[:, a % 3, P * o:P * o + P]) for c, o in enumerate(order)])
                    if 0 <= i - PV_LAG < n:
                        a = a0 + i - PV_LAG
                        m, g = maps[a], a // 2
                        if a % 2 == 0:
                            claim(pe, f"pv{g}")
                        o = bank(f"pv{g}")[m["row"]:m["row"] + m["m"], :]
                        wait_drained(pe, f"pT{a}")
                        pT = att_pT[:, a % 2, :]
                        second = m["kind"] == "diff" and a % 2 == 1
                        last = m["kind"] != "diff" or a % 2 == 1
                        mm(o[:, 0:T], m["v"][0], pT[:, 0:T], start=not second, stop=False, skip_group_check=True)
                        if m["kind"] == "mem":
                            ins = mm(o[:, 0:T], m["v"][1], pT[:, T:2 * T], start=False, stop=last,
                                     skip_group_check=True)
                        else:
                            ins = mm(o[:, P:T], m["v"][1], pT[:, T:T + P], start=False, stop=last,
                                     skip_group_check=True)
                        ins.then_inc(sem("att_pv"), 1)

            pe.wait_ge(sem("keys_zeroed"), 2)
            for name in ["mk0", "mq0"] + [f"foxqk{j}" for j in range(6)]:
                wait_drained(pe, name)
            pe.wait_ge(sem("negc_ready"), 1)
            pe.wait_ge(sem("selh_ready"), 1)
            for t in range(3):
                wait_drained(pe, f"foxv{t}")
            wait_drained(pe, "mv0")
            attention(fox_maps)

            def mixer_out(names, units_, nb=None):
                for j in range(4):
                    if j % 2 == 0:
                        w = wait_unit(pe, units_[j // 2], nb)
                    pair(names[j], w, 2 * P * (j % 2), mixT)

            for g in range(8):
                wait_drained(pe, f"pv{g}")
            mixer_out([f"foxout{j}" for j in range(4)], ["foxout0", "foxout1"])
            norm_sum(2)

            def down(prefix, unit, n_tiles, src, ready, nb=None):
                for j in range(4):
                    claim(pe, f"{prefix}{j}")
                n_units = -(-n_tiles // 4)
                for u in range(n_units):
                    w = wait_unit(pe, f"{unit}{u}", nb)
                    ks = range(4 * u, min(n_tiles, 4 * u + 4))
                    ready(ks[-1])
                    for o in range(KT):
                        for k in ks:
                            ins = mm(bank(f"{prefix}{o // 2}")[:, T * (o % 2):T * (o % 2) + T],
                                     w[:, k - 4 * u, P * o:P * o + P], src[:, k, :],
                                     start=(k == 0 and o % 2 == 0), stop=(k == n_tiles - 1), skip_group_check=True)
                        if u == n_units - 1 and o % 2 == 1:
                            ins.then_inc(filled(f"{prefix}{o // 2}"), 1)
                    if u < n_units - 1:
                        ins.then_inc(sem("ring_used"), 1)

            normed(3 * KT)(KT - 1)
            for p in range(FF0_PAIRS):
                if p % 2 == 0:
                    wg = wait_unit(pe, f"ffg{p // 2}")
                    wu = wait_unit(pe, f"ffu{p // 2}")
                pair(f"ffg{p}", wg, 2 * P * (p % 2), actT)
                pair(f"ffu{p}", wu, 2 * P * (p % 2), actT)
            down("ffd", "ffd", FF0 // P, aT, lambda k: wait_drained(pe, f"ffu{k // 2}"))

            norm_sum(3)
            w = wait_unit(pe, "convin0")
            normed(4 * KT)(KT - 1)
            for j in range(7):
                if j and j % 2 == 0:
                    w = wait_unit(pe, f"convin{j // 2}")
                pair(f"convin{j}", w, 2 * P * (j % 2), actT)
            head_sum(9)
            for name in ("mk1", "mv1", "convin6"):
                wait_drained(pe, name)
            attention(mem_maps)
            pe.wait_ge(sem("ccol_ready"), 1)
            claim(pe, "ada")
            for j in range(12):
                w = wait_unit(pe, f"ada{j}")
                for c in range(4):
                    for k in range(KT):
                        ins = mm(bank("ada")[:, 4 * j + c:4 * j + c + 1], w[:, k, P * c:P * c + P], ccol[:, k:k + 1],
                                 start=(k == 0), stop=(k == KT - 1))
                ins.then_inc(filled("ada") if j == 11 else sem("ring_used"), 1)

            def channel_sum(name, src):
                claim(pe, name)
                for c in range(CT):
                    ins = mm(bank(name)[:, 0:T], ones, src(c), start=(c == 0), stop=(c == CT - 1))
                ins.then_inc(filled(name), 1)

            pe.wait_ge(sem("conv_done"), CT)
            channel_sum("lnsum", lambda c: cacc[:, c, :])
            pe.wait_ge(sem("ln_sq"), 1)
            channel_sum("lnvar", lambda c: sqz[:, T * c:T * c + T])
            pe.wait_ge(sem("conv_mixed"), CT)
            for g in range(mem_maps[0] // 2, mem_maps[0] // 2 + 2):
                wait_drained(pe, f"pv{g}")
            mixer_out([f"convout{j}" for j in range(4)], ["convout0", "convout1"])
            norm_sum(4)

            normed(5 * KT)(KT - 1)
            pe.wait_ge(sem("ld_rt"), 16)
            by_tokens("router", rt, 0, E, actT, (0, 1))
            for j in range(4):
                t = j // 2
                turn(f"ztok{j}", [(P * c, actT[:, 4 * (j % 2) + c, P * t:P * t + P]) for c in range(4)])
            pe.wait_ge(sem("moe_marks"), 1)
            claim(pe, "mcum")
            b = bank("mcum")
            M = [plan_f[:, 0, E * t:E * t + E] for t in range(TT)]
            mm(b[:, 0:E], tri, M[0], start=True, stop=True)
            mm(b[:, E:2 * E], ones, M[0], start=True, stop=False)
            mm(b[:, E:2 * E], tri, M[1], start=False, stop=True)
            mm(b[:, 2 * E:3 * E], ones, M[0], start=True, stop=False)
            mm(b[:, 2 * E:3 * E], ones, M[1], start=False, stop=True).then_inc(filled("mcum"), 1)

            def as_rows(name, src):
                claim(pe, name)
                for a in range(2):
                    for t in range(TT):
                        ins = mm(bank(name)[:, T * a + P * t:T * a + P * t + P],
                                 src[:, a, t:t + 1].broadcast_to([P, P]), ident, start=True, stop=True)
                ins.then_inc(filled(name), 1)

            pe.wait_ge(sem("moe_keys"), 1)
            as_rows("krow", kcol)
            pe.wait_ge(sem("moe_gates"), 2)
            as_rows("grow", gcol)

            def gather(psum, j):
                for c in range(4):
                    for t in range(TT):
                        ins = mm(psum[:, CAP * c:CAP * c + CAP], z_tok[:, t, P * (4 * j + c):P * (4 * j + c) + P],
                                 sel[:, t, :], start=(t == 0), stop=(t == TT - 1))
                return ins

            for j in range(4):
                wait_drained(pe, f"ztok{j}")
            pe.wait_ge(sem("moe_sel"), TT)
            for j in range(2):
                claim(pe, f"gather{j}")
                gather(bank(f"gather{j}"), j).then_inc(filled(f"gather{j}"), 1)

            def slots_to_rows(psum, j):
                for c in range(4):
                    ins = pe.transpose(psum[0:CAP, P * c:P * c + P], yT[:, 4 * j + c, :], ident)
                return ins

            def scatter(psum, j):
                for c in range(2):
                    o = 2 * j + c
                    ins = mm(psum[:, T * c:T * c + T], y_tok[0:CAP, P * o:P * o + P], scat[0:CAP, :],
                             start=True, stop=True)
                return ins

            pe.wait_ge(sem("moe_plan"), 2)
            nb = pe.value_load(nbt[0:1, 0:1], min_val=E, max_val=MAXBLK)
            for b in range(8):
                pe.wait_ge(sem(f"drained{b}"), before_moe[b])
            pe.wait_ge(sem("moe_zeroed"), 2)
            with pe.Fori(0, nb) as i:
                def loaded(j):
                    n = U0 + j
                    pe.wait_ge(sem(f"ring_loaded{n % SLOTS}"), i * (16 * MOE_UNITS // SLOTS) + 16 * (n // SLOTS + 1))
                    return ring[:, n % SLOTS, :]

                def chunk(c):
                    for side in range(2):
                        b = 2 * (c % 2) + side
                        w = loaded(2 * c + side).rearrange("p (k n) -> p k n", k=KT)
                        pe.wait_ge(sem(f"moe_drained{b}"), i * (4 - c % 2) + c // 2)
                        for f in range(4):
                            for k in range(KT):
                                ins = mm(ps[:, b, CAP * f:CAP * f + CAP], w[:, k, P * f:P * f + P], xgT[:, k, :],
                                         start=(k == 0), stop=(k == KT - 1))
                        ins.then_inc(sem(f"moe_filled{b}"), 1)

                for j in range(2):
                    pe.wait_ge(sem(f"moe_drained{6 + j}"), i * 3)
                chunk(0)
                for j in range(2):
                    pe.wait_ge(sem(f"moe_drained{4 + j}"), i * 2)
                for j in range(2):
                    slots_to_rows(ps[:, 6 + j, :], j).then_inc(sem(f"moe_filled{6 + j}"), 1)
                chunk(1)
                for j in range(2):
                    pe.wait_ge(sem(f"moe_drained{6 + j}"), i * 3 + 1)
                pe.wait_ge(sem("moe_scat"), i)
                for j in range(4):
                    scatter(ps[:, 4 + j, :], j).then_inc(sem(f"moe_filled{4 + j}"), 1)
                for c in range(2, MOE_CH):
                    chunk(c)
                pe.wait_ge(sem("moe_sel"), i * TT + 2 * TT)
                for j in range(2):
                    pe.wait_ge(sem(f"moe_drained{6 + j}"), i * 3 + 2)
                    gather(ps[:, 6 + j, :], j).then_inc(sem(f"moe_filled{6 + j}"), 1)
                for j in range(2):
                    pe.wait_ge(sem(f"moe_drained{4 + j}"), i * 2 + 1)
                for u in range(MOE_CH):
                    w = loaded(2 * MOE_CH + u).rearrange("p (k n) -> p k n", k=4)
                    pe.wait_ge(sem(f"moe_drained{2 * (u % 2) + 1}"), i * (4 - u % 2) + u // 2 + 1)
                    for o in range(KT):
                        for k in range(4):
                            ins = mm(ps[:, 4 + o // 4, CAP * (o % 4):CAP * (o % 4) + CAP], w[:, k, P * o:P * o + P],
                                     maT[:, 4 * u + k, :], start=(u == 0 and k == 0 and o % 4 == 0),
                                     stop=(u == MOE_CH - 1 and k == 3), skip_group_check=True)
                        if u == MOE_CH - 1 and o % 4 == 3:
                            ins.then_inc(sem(f"moe_filled{4 + o // 4}"), 1)
                    if u < MOE_CH - 1:
                        ins.then_inc(sem("moe_down_read"), 1)
            for j in range(2):
                pe.wait_ge(sem(f"moe_drained{4 + j}"), nb * 2)
                pe.wait_ge(sem(f"moe_drained{6 + j}"), nb * 3)
            for j in range(2):
                slots_to_rows(bank(f"ytok{j}"), j).then_inc(filled(f"ytok{j}"), 1)
            pe.wait_ge(sem("moe_scat"), nb)
            for j in range(2):
                wait_drained(pe, f"ytok{j}")
            for j in range(4):
                scatter(bank(f"scat{j}"), j).then_inc(filled(f"scat{j}"), 1)

            for b in range(4):
                pe.wait_ge(sem(f"moe_drained{b}"), nb * (4 - b // 2))
            norm_sum(5)
            pe.wait_ge(sem("shifted"), KT)
            w = wait_unit(pe, "win0", nb)
            for j, name in enumerate(("dq0", "dq1", "dk0", "dk1")):
                if j == 2:
                    w = wait_unit(pe, "win1", nb)
                pair(name, w, 2 * P * (j % 2), actT)
                wait_drained(pe, name)
                claim(pe, f"rot{j}")
                mm(bank(f"rot{j}"), rot, qk_sq, start=True, stop=True).then_inc(filled(f"rot{j}"), 1)
            w = wait_unit(pe, "win2", nb)
            for t in range(TT):
                by_tokens(f"dv{t}", w, 0, 512, actT, (t,))
            for j, name in enumerate(("sq0", "sq1", "sk0", "sk1")):
                if j % 2 == 0:
                    w = wait_unit(pe, f"win{3 + j // 2}", nb)
                pair(name, w, 2 * P * (j % 2), actT)
            w = wait_unit(pe, "win5", nb)
            for t in range(TT):
                by_tokens(f"sv{t}", w, 0, 512, actT, (t,))
            pe.wait_ge(sem("rope_done"), rope_count(4))
            for name in ("dv0", "dv1", "sq0", "sq1", "sk0", "sk1", "sv0", "sv1"):
                wait_drained(pe, name)
            attention(diff_maps)

            for i in range(SBH + 2):
                if i < SBH:
                    s, k, q = bank(f"sbs{i}"), kz[:, 8 + i, :], qT[:, 4 + i // 2, :]
                    claim(pe, f"sbs{i}")
                    mm(s[:, 0:T], k[:, 0:P], q, start=True, stop=True)
                    mm(s[:, T:T + P], k[:, P:T], q[:, P:T], start=True, stop=True).then_inc(filled(f"sbs{i}"), 1)
                if 0 <= i - 1 < SBH:
                    j = i - 1
                    x, m = bank(f"sbx{j}"), sb_m[:, j % 2, :]
                    pe.wait_ge(sem("sb_masked"), 2 * (j + 1))
                    claim(pe, f"sbx{j}")
                    mm(x[:, 0:T], sufx, m[:, 0:T], start=True, stop=False, skip_group_check=True)
                    mm(x[:, P:T], ones, m[:, T:T + P], start=False, stop=True, skip_group_check=True)
                    mm(x[:, T:T + P], sufx, m[:, T:T + P], start=True, stop=True,
                       skip_group_check=True).then_inc(filled(f"sbx{j}"), 1)
                if 0 <= i - 2 < SBH:
                    j = i - 2
                    if j % 2 == 0:
                        claim(pe, f"sbo{j // 2}")
                    o = bank(f"sbo{j // 2}")[HD * (j % 2):HD * (j % 2) + HD, :]
                    pe.wait_ge(sem("sb_probs"), 2 * (j + 1))
                    v = [vv[:, t, 512 + HD * j:512 + HD * j + HD] for t in range(TT)]
                    mm(o[:, 0:T], v[0], sb_a[:, j % 2, 0:T], start=True, stop=False, skip_group_check=True)
                    mm(o[:, P:T], v[1], sb_a[:, j % 2, T:T + P], start=False, stop=True,
                       skip_group_check=True).then_inc(sem("sb_pv"), 1)
            for j in range(2):
                pe.wait_ge(sem("sub_sq"), j + 1)
                claim(pe, f"sub{j}")
                mm(bank(f"sub{j}"), ones, qk_sq, start=True, stop=True).then_inc(filled(f"sub{j}"), 1)
            pe.wait_ge(sem("sub_out"), 2)
            for j in range(SBH // 2):
                wait_drained(pe, f"sbo{j}")
            mixer_out([f"wout{j}" for j in range(4)], ["wout0", "wout1"], nb)
            norm_sum(6)
            pe.wait_ge(sem("shifted"), 2 * KT)
            for p in range(16):
                if p % 2 == 0:
                    w = wait_unit(pe, f"ffa{p // 2}", nb)
                pair(f"ffa{p}", w, 2 * P * (p % 2), actT)
            down("ffb", "ffb", FF2 // P, aT, lambda k: wait_drained(pe, f"ffa{k // 2}"), nb)
            norm_sum(7)
            normed(NORM_OUT_5 + KT)(KT - 1)
            for j in range(4):
                t = j // 2
                turn(f"outT{j}", [(P * c, actT[:, 4 * (j % 2) + c, P * t:P * t + P]) for c in range(4)])

        @block.vector
        def _(dve):
            V = nc.vector
            step = [0]

            def link(ins):
                step[0] += 1
                ins.then_inc(sem("dve_step"), 1)
                dve.wait_ge(sem("dve_step"), step[0])

            def stt(out_, in0, scalar, in1, op0, op1):
                return V.scalar_tensor_tensor(out=out_, in0=in0, scalar=scalar, in1=in1, op0=op0, op1=op1)

            def col(at):
                return cols[:, at:at + 1]

            for j in range(4):
                wait_filled(dve, f"xT{j}")
                V.tensor_copy(hT[:, 2 * j:2 * j + 2, :].rearrange("p a b -> p (a b)"),
                              bank(f"xT{j}")).then_inc(drained(f"xT{j}"), 1)
            wait_filled(dve, "colsT")
            V.tensor_copy(cols[:, :], bank("colsT")[:, 0:V_END]).then_inc(drained("colsT"), 1)
            wait_drained(dve, "colsT")
            V.tensor_scalar(gq8[:, 0:1], col(V_FGQ), SCALE, None, ALU.mult).then_inc(sem("cols_ready"), 1)
            link(V.tensor_scalar(gq8[:, 1:3], cols[:, V_GMQ:V_GMQ + 2], SCALE, None, ALU.mult))
            link(V.tensor_tensor(lam[:, 4:5], col(V_LQ), col(V_LK), ALU.mult))
            V.tensor_tensor(lam[:, 0:1], lam[:, 4:5], headones[:, 0:1], ALU.mult).then_inc(sem("lam_prod"), 1)
            V.tensor_tensor(lam[:, 1:2], lam[:, 4:5], headones[:, HD:HD + 1], ALU.mult).then_inc(sem("lam_prod"), 1)

            def norm_scale(k, outs):
                wait_filled(dve, f"nsum{k}")
                if k:
                    dve.wait_ge(sem("norm_out"), KT * (k + 1))
                V.tensor_scalar(rn[:, :], bank(f"nsum{k}")[:, 0:T], 1.0 / D, EPS, ALU.mult,
                                ALU.add).then_inc(drained(f"nsum{k}"), 1)
                dve.wait_ge(sem("norm_sd"), k + 1)
                link(V.reciprocal(rn[:, :], rn[:, :]))
                for src, gain, dst in outs:
                    for j in range(KT):
                        stt(dst[:, j, :], src[:, j, :], gain[:, j:j + 1], rn[:, :], ALU.mult,
                            ALU.mult).then_inc(sem("norm_out"), 1)

            def gains(at):
                return cols[:, at:at + KT]

            scaled_pairs = []

            def qk_scale(k, name, outs):
                wait_filled(dve, f"qsum{k}")
                if scaled_pairs:
                    wait_drained(dve, scaled_pairs[-1])
                scaled_pairs.append(name)
                V.tensor_scalar(qk_r, bank(f"qsum{k}"), 1.0 / HD, EPS, ALU.mult, ALU.add).then_inc(drained(f"qsum{k}"), 1)
                dve.wait_ge(sem("qk_sd"), k + 1)
                link(V.reciprocal(qk_r, qk_r))
                raw = bank(name).rearrange("p (a b) -> p a b", a=2)
                r = qk_r.rearrange("p (a b) -> p a b", a=2)
                for dst, lo, hi, gain in outs:
                    ins = stt(dst, raw[lo:hi, :, :], gain[lo:hi, :], r[lo:hi, :, :], ALU.mult, ALU.mult)
                ins.then_inc(drained(name), 1)

            def keys(k, name, keys_, at, gain):
                qk_scale(k, name, [(keys_[0:HD, at:at + 4:2, :], 0, HD, gain),
                                   (keys_[HD:P, at + 1:at + 4:2, :], HD, P, gain)])

            norm_scale(0, [(memT, gains(V_MEM), actT)])
            for j in range(KT):
                stt(mn1[:, j, :], memT[:, j, :], col(V_MEM + 8 + j), rn[:, :], ALU.mult,
                    ALU.mult).then_inc(sem("norm_out"), 1)
            dve.wait_ge(sem("keys_zeroed"), 2)
            keys(0, "mk0", kz, FOX_HEADS, col(V_GMK))
            wait_filled(dve, "mv0")
            norm_scale(1, [(hT, gains(V_MIX), actT)])
            keys(1, "mk1", mkz1, 0, col(V_GMK + 1))
            dve.wait_ge(sem("ld_bf"), 16)
            wait_filled(dve, "foxf")
            V.tensor_tensor(lsf[:, 0, :, :], bank("foxf")[:, 0:2 * FOX_HEADS].rearrange("p (a b) -> p a b", a=2),
                            bf_row[:, :].unsqueeze(1).broadcast_to([P, TT, FOX_HEADS]),
                            ALU.add).then_inc(drained("foxf"), 1)
            wait_drained(dve, "foxf")
            stt(lsf[:, 1, :, :], lsf[:, 0, :, :], -1.0, lsf[:, 0, :, :], ALU.mult,
                ALU.min).then_inc(sem("fox_negabs"), 1)
            dve.wait_ge(sem("fox_log1p"), 1)
            stt(lsf[:, 0, :, :], lsf[:, 0, :, :], 0.0, lsf[:, 1, :, :], ALU.min,
                ALU.subtract).then_inc(sem("fox_logf"), 1)
            wait_filled(dve, "mv1")
            qk_scale(2, "mq0", [(qT[:, 6:8, :], 0, P, gq8[:, 1:2])])
            wait_filled(dve, "nsum1")
            V.tensor_copy(selh, ident[:, 0:FOX_HEADS].unsqueeze(2).broadcast_to([P, FOX_HEADS, P])).then_inc(
                sem("selh_ready"), 1)
            wait_filled(dve, "cum")
            dve.wait_ge(sem("negc_ready"), 1)
            V.tensor_copy(flat(ctok), bank("cum")[:, T:T + 2 * FOX_HEADS]).then_inc(drained("cum"), 1)
            wait_drained(dve, "cum")
            for j in range(3):
                qk_scale(3 + j, f"foxqk{j}", [(qT[:, 2 * j:2 * j + 2, :], 0, P, gq8[:, 0:1])])
            for j in range(3):
                keys(6 + j, f"foxqk{3 + j}", kz, 4 * j, col(V_FGK))

            def attention(rng):
                n, a0 = len(rng), rng[0]
                for i in range(n + PV_LAG + 1):
                    if i < n:
                        a = a0 + i
                        m, s, p = maps[a], bank(f"sc{a}"), att_p[:, a % 3, :]
                        wait_filled(dve, f"sc{a}")
                        if a >= 3:
                            wait_filled(dve, f"pT{a - 3}")
                        if m["kind"] == "fox":
                            h = m["head"]
                            c0, c1 = ctok[:, 0, h:h + 1], ctok[:, 1, h:h + 1]
                            stt(p[:, 0:P], s[:, 0:P], c0, cc(C_FOXM), ALU.add, ALU.add)
                            V.tensor_scalar(p[:, P:2 * P], s[:, P:2 * P], c1, None, ALU.add)
                            stt(p[:, 2 * P:3 * P], s[:, 2 * P:3 * P], c1, cc(C_FOXM), ALU.add,
                                ALU.add).then_inc(drained(f"sc{a}"), 1)
                            w0, w1 = P, 3 * P
                        elif m["kind"] == "diff":
                            V.tensor_tensor(p[:, 0:P], s[:, 0:P], cc(C_DIFM), ALU.add)
                            V.tensor_copy(p[:, P:2 * P], s[:, P:2 * P])
                            V.tensor_tensor(p[:, 2 * P:3 * P], s[:, 2 * P:3 * P], cc(C_DIFM),
                                            ALU.add).then_inc(drained(f"sc{a}"), 1)
                            w0, w1 = P, 3 * P
                        else:
                            V.tensor_copy(p, s).then_inc(drained(f"sc{a}"), 1)
                            w0, w1 = T, 2 * T
                        wait_drained(dve, f"sc{a}")
                        for t, (lo, hi) in enumerate(((0, w0), (w0, w1))):
                            V.tensor_reduce(nmx[:, a % 3, t:t + 1], p[:, lo:hi], AX_X, ALU.max,
                                            negate=True).then_inc(sem("att_max"), 1)
                    if 0 <= i - 1 < n:
                        a = a0 + i - 1
                        dve.wait_ge(sem("att_exp"), 2 * (a + 1))
                        ins = V.reciprocal(rsum[:, a % 3, :], ssum[:, a % 3, :])
                        if maps[a]["kind"] == "diff" and a % 2 == 1:
                            link(ins)
                            ins = V.tensor_scalar(rsum[:, a % 3, :], rsum[:, a % 3, :], lam[:, 6:7], None, ALU.mult)
                        ins.then_inc(sem("att_rsum"), 1)
                    if 0 <= i - PV_LAG - 1 < n and (i - PV_LAG - 1) % 2 == 1:
                        g = (a0 + i - PV_LAG - 1) // 2
                        dve.wait_ge(sem("att_pv"), 2 * (g + 1))
                        V.tensor_copy(mixT[:, maps[2 * g]["to"], :], bank(f"pv{g}")[:, 0:T]).then_inc(drained(f"pv{g}"), 1)

            attention(fox_maps)

            def residual(name, j):
                wait_filled(dve, name)
                h2 = hT[:, 2 * j:2 * j + 2, :].rearrange("p a b -> p (a b)")
                V.tensor_tensor(h2, h2, bank(name), ALU.add).then_inc(drained(name), 1)

            for j in range(4):
                residual(f"foxout{j}", j)
            norm_scale(2, [(hT, gains(V_FFN), actT)])
            for p in range(FF0_PAIRS):
                wait_filled(dve, f"ffu{p}")
                wait_drained(dve, f"ffg{p}")
                V.tensor_tensor(aT[:, 2 * p:2 * p + 2, :].rearrange("p a b -> p (a b)"), sg[:, p % 2, :],
                                bank(f"ffu{p}"), ALU.mult).then_inc(drained(f"ffu{p}"), 1)
            for j in range(4):
                residual(f"ffd{j}", j)
            norm_scale(3, [(hT, gains(V_MIX + 8), actT)])

            dve.wait_ge(sem("upad_zeroed"), 1)
            for j in range(3):
                wait_drained(dve, f"convin{3 + j}")
                V.tensor_tensor(upad[:, 2 * j:2 * j + 2, PAD:PAD + T], abuf[:, 2 * j:2 * j + 2, :],
                                cacc[:, 2 * j:2 * j + 2, :], ALU.mult).then_inc(sem("glu"), 1)
            qk_scale(9, "convin6", [(q1[:, :, :], 0, P, gq8[:, 2:3])])
            attention(mem_maps)
            dve.wait_ge(sem("glu"), 3)
            for tap in range(TAPS):
                for c in range(CT):
                    if tap:
                        dve.wait_ge(sem("conv_tap"), CT * (tap - 1) + c + 1)
                    w = col(V_TAP + CT * tap + c)
                    u = upad[:, c, tap:tap + T]
                    if tap == 0:
                        ins = V.tensor_scalar(cacc[:, c, :], u, w, col(V_DWB + c), ALU.mult, ALU.add)
                    else:
                        ins = stt(cacc[:, c, :], u, w, cacc[:, c, :], ALU.mult, ALU.add)
                    ins.then_inc(sem("conv_tap") if tap < TAPS - 1 else sem("conv_done"), 1)
            wait_filled(dve, "ada")
            V.tensor_tensor(mod[:, :], bank("ada")[:, 0:48], cols[:, V_ADA:V_ADA + 48], ALU.add).then_inc(drained("ada"), 1)
            wait_drained(dve, "ada")
            stt(gs[:, 0, :], mod[:, 8:16], 1.0, gains(V_MIX2), ALU.add, ALU.mult)
            stt(gs[:, 1, :], mod[:, 32:40], 1.0, gains(V_FFN2), ALU.add, ALU.mult).then_inc(sem("gs_ready"), 1)
            wait_drained(dve, "lam")
            link(V.tensor_tensor(lam[:, 5:6], lam[:, 3:4], lam[:, 2:3], ALU.subtract))
            link(V.tensor_scalar(lam[:, 6:7], lam[:, 5:6], LAMBDA_INIT, None, ALU.subtract))
            link(V.tensor_scalar(lam[:, 7:8], col(V_SUB), 1.0 - LAMBDA_INIT, None, ALU.mult))
            wait_filled(dve, "lnsum")
            dve.wait_ge(sem("norm_out"), 5 * KT)
            V.tensor_scalar(rn[:, :], bank("lnsum")[:, 0:T], 1.0 / CONV, None, ALU.mult).then_inc(drained("lnsum"), 1)
            wait_drained(dve, "lnsum")
            rn_all = rn[:, :].unsqueeze(1).broadcast_to([P, CT, T])
            V.tensor_tensor(cacc, cacc, rn_all, ALU.subtract).then_inc(sem("ln_centred"), 1)
            wait_filled(dve, "lnvar")
            dve.wait_ge(sem("ln_centred"), 1)
            V.tensor_scalar(rn[:, :], bank("lnvar")[:, 0:T], 1.0 / CONV, EPS, ALU.mult, ALU.add).then_inc(drained("lnvar"), 1)
            dve.wait_ge(sem("ln_sd"), 1)
            link(V.reciprocal(rn[:, :], rn[:, :]))
            V.tensor_tensor(cacc, cacc, rn_all, ALU.mult).then_inc(sem("ln_scaled"), 1)
            for j in range(4):
                residual(f"convout{j}", j)
            norm_scale(4, [(hT, gains(V_FFN + 8), actT)])

            ei = cc(C_EI, E)
            wait_filled(dve, "router")
            V.tensor_copy(flat(lg), bank("router")[:, 0:TT * E]).then_inc(drained("router"), 1)
            wait_drained(dve, "router")
            for t in range(TT):
                link(V.max(mx8[:, t, :], lg[:, t, :]))
                link(V.max_index(ix8[:, t, :], mx8[:, t, :], lg[:, t, :]))
            link(V.tensor_copy(ixf[:, :, :], ix8[:, :, 0:2]))
            for a in range(2):
                for t in range(TT):
                    link(V.tensor_scalar(oh[:, a, t, :], ei, ixf[:, t, a:a + 1], None, ALU.is_equal))
            marks = plan_f[:, 0, :]
            V.tensor_tensor(marks, oh[:, 0, :, :].rearrange("p a b -> p (a b)"),
                            oh[:, 1, :, :].rearrange("p a b -> p (a b)"), ALU.add).then_inc(sem("moe_marks"), 1)
            V.tensor_tensor(pexp[:, 0:2].unsqueeze(2), mx8[:, :, 1:2], mx8[:, :, 0:1],
                            ALU.subtract).then_inc(sem("gate_diff"), 1)
            wait_filled(dve, "mcum")
            dve.wait_ge(sem("moe_marks"), 1)
            link(V.tensor_tensor(plan_f[:, 1, :], bank("mcum")[:, 0:2 * E], marks, ALU.subtract))
            pos = plan_f[:, 1, :]
            V.tensor_copy(plan_f[:, 2, 0:E], bank("mcum")[:, 2 * E:3 * E]).then_inc(drained("mcum"), 1)
            wait_drained(dve, "mcum")
            cnt = plan_f[:, 2, 0:E]
            link(V.tensor_scalar(plan_f[:, 3, 0:E], cnt, float(CAP), None, ALU.is_gt))
            link(stt(plan_f[:, 4, 0:E], cnt, float(2 * CAP), plan_f[:, 3, 0:E], ALU.is_gt, ALU.add))
            extra = plan_f[:, 4, 0:E]
            link(V.tensor_tensor(lt8[:, :, :], cc(C_LT, E * E).rearrange("p (a b) -> p a b", a=E),
                                 extra.unsqueeze(1).broadcast_to([P, E, E]), ALU.mult))
            link(V.tensor_reduce(plan_f[:, 5, 0:E], lt8[:, :, :], AX_X, ALU.add))
            before = plan_f[:, 5, 0:E]
            link(stt(plan_f[:, 6, 0:E], before, float(E - 1), ei, ALU.add, ALU.subtract))
            link(V.tensor_scalar(plan_f[:, 7, 0:E], plan_f[:, 6, 0:E], float(CAP), None, ALU.mult))
            link(V.tensor_scalar(plan_f[:, 8, :], pos, float(CAP), None, ALU.is_ge))
            two = lambda r: plan_f[:, r, :].rearrange("p (a b) -> p a b", a=TT)
            link(V.tensor_tensor(two(9), two(8), plan_f[:, 7, 0:E].unsqueeze(1).broadcast_to([P, TT, E]), ALU.mult))
            link(V.tensor_tensor(plan_f[:, 10, :], plan_f[:, 9, :], pos, ALU.add))
            link(V.tensor_scalar(plan_f[:, 11, 0:E], ei, float(CAP), None, ALU.mult))
            link(V.tensor_tensor(two(12), two(10), plan_f[:, 11, 0:E].unsqueeze(1).broadcast_to([P, TT, E]), ALU.add))
            for a in range(2):
                r = plan_f[:, 13 + a, :].rearrange("p (a b) -> p a b", a=TT)
                link(V.tensor_tensor(r, oh[:, a, :, :], two(12), ALU.mult))
                ins = V.tensor_reduce(kcol[:, a, :], r, AX_X, ALU.add)
                if a == 0:
                    link(ins)
            ins.then_inc(sem("moe_keys"), 1)
            link(V.tensor_tensor(plan_f[0:1, 15, 0:E], plan_f[0:1, 5, 0:E], plan_f[0:1, 4, 0:E], ALU.add))
            link(V.tensor_scalar(pexp[0:1, 8:9], plan_f[0:1, 15, E - 1:E], float(E), None, ALU.add))
            link(V.tensor_tensor(lt8[0:1, 0:EXTRA, :], plan_f[0:1, 15, 0:E].unsqueeze(1).broadcast_to([1, EXTRA, E]),
                                 cst[0:1, C_XI:C_XI + EXTRA * E].rearrange("p (a b) -> p a b", a=EXTRA), ALU.is_le))
            link(V.tensor_reduce(pexp[0:1, 16:16 + EXTRA], lt8[0:1, 0:EXTRA, :], AX_X, ALU.add))
            link(V.tensor_scalar(pexp[0:1, 16:16 + EXTRA], pexp[0:1, 16:16 + EXTRA], float(E - 1), None, ALU.min))
            V.tensor_copy(etab[0:1, 0:E], cst[0:1, C_EI:C_EI + E])
            V.tensor_copy(etab[0:1, E:E + EXTRA], pexp[0:1, 16:16 + EXTRA]).then_inc(sem("moe_plan"), 1)
            V.tensor_copy(nbt[0:1, 0:1], pexp[0:1, 8:9])
            V.tensor_scalar(nbt[0:1, 1:2], pexp[0:1, 8:9], -1.0, None, ALU.add).then_inc(sem("moe_plan"), 1)
            dve.wait_ge(sem("gate_exp"), 1)
            link(V.tensor_scalar(pexp[:, 2:4], pexp[:, 0:2], 1.0, None, ALU.add))
            V.reciprocal(gcol[:, 0, :], pexp[:, 2:4]).then_inc(sem("moe_gates"), 1)
            dve.wait_ge(sem("moe_gates"), 1)
            V.tensor_tensor(gcol[:, 1, :], gcol[:, 0, :], pexp[:, 0:2], ALU.mult).then_inc(sem("moe_gates"), 1)
            wait_filled(dve, "krow")
            V.tensor_copy(krow[:, 0:2, :].rearrange("p a b -> p (a b)"), bank("krow")).then_inc(drained("krow"), 1)
            wait_filled(dve, "grow")
            V.tensor_copy(krow[:, 2:4, :].rearrange("p a b -> p (a b)"), bank("grow")).then_inc(drained("grow"), 1)
            wait_drained(dve, "krow")
            wait_drained(dve, "grow")

            iota = cc(C_IOTA, CAP)

            def select(count, first=False):
                if not first:
                    dve.wait_ge(sem("keys_moved"), count)
                for t in range(TT):
                    V.tensor_scalar(sel[:, t, :], iota, kcol[:, 0, t:t + 1], None,
                                    ALU.is_equal).then_inc(sem("sel_half"), 1)
                dve.wait_ge(sem("sel_half"), count * TT + TT)
                for t in range(TT):
                    stt(sel[:, t, :], iota, kcol[:, 1, t:t + 1], sel[:, t, :], ALU.is_equal,
                        ALU.add).then_inc(sem("moe_sel"), 1)
                dve.wait_ge(sem("moe_sel"), count * TT + TT)
                V.tensor_scalar(kcol[:, :, :], kcol[:, :, :], -float(CAP), None, ALU.add).then_inc(sem("keys_moved"), 1)

            wait_filled(dve, "krow")
            select(0, first=True)
            sid = cst[:, C_SID:C_SID + 1]
            dve.wait_ge(sem("moe_zeroed"), 2)
            dve.wait_ge(sem("moe_plan"), 2)
            nb = dve.value_load(nbt[0:1, 0:1], min_val=E, max_val=MAXBLK)
            with dve.Fori(0, nb) as i:
                def product(c):
                    b = 2 * (c % 2)
                    n = i * (4 - c % 2) + c // 2 + 1
                    dve.wait_ge(sem(f"moe_filled{b + 1}"), n)
                    dve.wait_ge(sem(f"moe_drained{b}"), n)
                    V.tensor_tensor(maT[:, 4 * c:4 * c + 4, :].rearrange("p a b -> p (a b)"), sg[:, c % 2, 0:4 * CAP],
                                    ps[:, b + 1, 0:4 * CAP], ALU.mult).then_inc(sem(f"moe_drained{b + 1}"), 1)

                product(0)
                product(1)
                for j in range(4):
                    b = 4 + j
                    dve.wait_ge(sem(f"moe_filled{b}"), i * (2 if b < 6 else 3) + (1 if b < 6 else 2))
                    h2 = hT[:, 2 * j:2 * j + 2, :].rearrange("p a b -> p (a b)")
                    V.tensor_tensor(h2, h2, ps[:, b, :], ALU.add).then_inc(sem(f"moe_drained{b}"), 1)
                select(i + 1)
                stt(scat, krow[:, 0, :], sid, krow[:, 2, :], ALU.is_equal, ALU.mult).then_inc(sem("scat_half"), 1)
                stt(scat_b, krow[:, 1, :], sid, krow[:, 3, :], ALU.is_equal, ALU.mult).then_inc(sem("scat_half"), 1)
                dve.wait_ge(sem("scat_half"), i * 3 + 2)
                V.tensor_scalar(krow[:, 0:2, :], krow[:, 0:2, :], -float(CAP), None,
                                ALU.add).then_inc(sem("scat_half"), 1)
                dve.wait_ge(sem("scat_half"), i * 3 + 3)
                V.tensor_tensor(scat, scat, scat_b, ALU.add).then_inc(sem("moe_scat"), 1)
                for c in range(2, MOE_CH):
                    product(c)
            for j in range(4):
                residual(f"scat{j}", j)

            norm_scale(5, [(hT, gs[:, 0, :], actT)])
            cos2 = cc(C_COS, T).unsqueeze(1).broadcast_to([P, 2, T])
            sin2 = cc(C_SIN, T).unsqueeze(1).broadcast_to([P, 2, T])
            raw2 = qk_sq.rearrange("p (a b) -> p a b", a=2)
            t1 = qk_r.rearrange("p (a b) -> p a b", a=2)
            t2 = sqz[:, 0:512].rearrange("p (a b) -> p a b", a=2)
            dve.wait_ge(sem("keys_zeroed"), 3)
            for j, name in enumerate(("dq0", "dq1", "dk0", "dk1")):
                scale = SCALE if j < 2 else 1.0
                wait_drained(dve, name)
                link(stt(t1, raw2, scale, cos2, ALU.mult, ALU.mult))
                wait_filled(dve, f"rot{j}")
                stt(t2, bank(f"rot{j}").rearrange("p (a b) -> p a b", a=2), scale, sin2, ALU.mult,
                    ALU.mult).then_inc(drained(f"rot{j}"), 1)
                wait_drained(dve, f"rot{j}")
                if j < 2:
                    V.tensor_tensor(qT[:, 2 * j:2 * j + 2, :], t1, t2, ALU.add).then_inc(sem("rope_done"), 1)
                else:
                    at = 4 * (j - 2)
                    V.tensor_tensor(kz[0:HD, at:at + 4:2, :], t1[0:HD, :, :], t2[0:HD, :, :],
                                    ALU.add).then_inc(sem("rope_done"), 1)
                    V.tensor_tensor(kz[HD:P, at + 1:at + 4:2, :], t1[HD:P, :, :], t2[HD:P, :, :],
                                    ALU.add).then_inc(sem("rope_done"), 1)
            attention(diff_maps)

            wait_filled(dve, f"pT{len(maps) - 1}")
            for i in range(SBH + 2):
                if i < SBH:
                    b, s = i % 2, bank(f"sbs{i}")[:, 0:384]
                    dve.wait_ge(sem("sb_log1p"), i + 1)
                    if i >= 2:
                        wait_filled(dve, f"sbx{i - 2}")
                    stt(sb_m[:, b, :], s, 0.0, sb_l[:, b, :], ALU.max, ALU.add).then_inc(sem("sb_m"), 1)
                    if i >= 2:
                        dve.wait_ge(sem("sb_exp"), i - 1)
                    stt(sb_b[:, b, :], s, 0.0, sb_l[:, b, :], ALU.min, ALU.subtract).then_inc(drained(f"sbs{i}"), 1)
                if 0 <= i - 1 < SBH:
                    j = i - 1
                    wait_filled(dve, f"sbx{j}")
                    wait_drained(dve, f"sbs{j}")
                    V.tensor_tensor(sb_b[:, j % 2, :], sb_b[:, j % 2, :], bank(f"sbx{j}")[:, 0:384],
                                    ALU.subtract).then_inc(drained(f"sbx{j}"), 1)
                if 0 <= i - 2 < SBH and i % 2 == 1:
                    g = (i - 2) // 2
                    dve.wait_ge(sem("sb_pv"), 2 * (g + 1))
                    V.tensor_copy(mixT[:, 4 + g, :], bank(f"sbo{g}")[:, 0:T]).then_inc(drained(f"sbo{g}"), 1)
            for j in range(2):
                wait_filled(dve, f"sub{j}")
                if j:
                    dve.wait_ge(sem("sub_out"), j)
                V.tensor_scalar(qk_r, bank(f"sub{j}"), 1.0 / P, EPS, ALU.mult, ALU.add).then_inc(drained(f"sub{j}"), 1)
                dve.wait_ge(sem("sub_sd"), j + 1)
                link(V.reciprocal(qk_r, qk_r))
                m2 = mixT[:, 2 * j:2 * j + 2, :].rearrange("p a b -> p (a b)")
                stt(m2, m2, lam[:, 7:8], qk_r, ALU.mult, ALU.mult).then_inc(sem("sub_out"), 1)

            def gated_residual(name, j, at):
                wait_filled(dve, name)
                for t in range(2):
                    o = 2 * j + t
                    ins = stt(hT[:, o, :], bank(name)[:, T * t:T * t + T], mod[:, at + o:at + o + 1], hT[:, o, :],
                              ALU.mult, ALU.add)
                ins.then_inc(drained(name), 1)

            for j in range(4):
                gated_residual(f"wout{j}", j, 16)
            norm_scale(6, [(hT, gs[:, 1, :], actT)])
            for p in range(16):
                wait_filled(dve, f"ffa{p}")
                a = att_p[:, p % 2, :]
                if p >= 2:
                    wait_drained(dve, f"ffa{p - 2}")
                link(V.tensor_scalar(a, bank(f"ffa{p}"), 0.0, None, ALU.max))
                V.tensor_tensor(aT[:, 2 * p:2 * p + 2, :].rearrange("p a b -> p (a b)"), a, bank(f"ffa{p}"),
                                ALU.mult).then_inc(drained(f"ffa{p}"), 1)
            for j in range(4):
                gated_residual(f"ffb{j}", j, 40)
            norm_scale(7, [(hT, gains(V_FIN2), actT)])


NORM_OUT_5 = 7 * KT


def rope_count(j):
    return min(j, 2) + 2 * max(0, j - 2)


_INS = ["x", "mem", "norm_mix", "norm_mem", "norm_ffn", "w_mem_kv", "g_mq", "g_mk", "fox_w_in", "fox_b_f", "fox_g_q",
        "fox_g_k", "fox_w_out", "conv_w_in", "conv_b_in", "conv_dw", "conv_dw_b", "conv_ln_g", "conv_ln_b",
        "conv_w_out", "ffn_w_gate", "ffn_w_up", "ffn_w_down", "moe_router", "moe_w_gate", "moe_w_up", "moe_w_down",
        "c_2", "ada_w_2", "ada_b_2", "mix_norm_g_2", "w_in_2", "lambda_q1_2", "lambda_k1_2", "lambda_q2_2",
        "lambda_k2_2", "diff_subln_g_2", "w_out_2", "ffn_norm_g_2", "w_ff1_2", "w_ff2_2", "final_norm_g_2"]


def kernel(**inputs):
    import concourse.bacc as bacc
    from concourse.bass_utils import run_bass_kernel_spmd

    nc = bacc.Bacc("TRN2", target_bir_lowering=False, num_devices=1)
    arrays, aps = {}, {}
    for name in _INS:
        a = np.ascontiguousarray(inputs[name])
        arrays[f"in_{name}"] = a
        aps[name] = nc.dram_tensor(f"in_{name}", a.shape, mybir.dt.from_np(a.dtype), kind="ExternalInput").ap()
    arrays["in_constants"] = constants()
    cst = nc.dram_tensor("in_constants", (P, C_END), F32, kind="ExternalInput").ap()
    out = nc.dram_tensor("out_0", (1, T, D), F32, kind="ExternalOutput").ap()
    build(nc, aps, cst, out)
    r = run_bass_kernel_spmd(nc, [arrays], core_ids=[0])
    return r.results[0]["out_0"]
```

```python
from contextlib import ExitStack

import numpy as np

import concourse.bass as bass
from concourse import mybir

F32 = mybir.dt.float32
F32R = mybir.dt.float32r
I32 = mybir.dt.int32
U32 = mybir.dt.uint32
ALU = mybir.AluOpType
ACT = mybir.ActivationFunctionType
AX_X = mybir.AxisListType.X

P = 128
D = 1024
KT = D // P
T = 256
TT = T // P
HD = 64
FOX_HEADS = 12
MEM_HEADS = 4
FOX = FOX_HEADS * HD
MEM = MEM_HEADS * HD
CONV = 768
CT = CONV // P
TAPS = 31
PAD = TAPS - 1
FF0 = 2816
E = 8
EFF = 3584
EFT = EFF // P
CAP = 128
EXTRA = 3
MAXBLK = E + EXTRA
FF2 = 4096
EPS = 1e-6
NEG = -1e30
SCALE = HD ** -0.5
LAMBDA_INIT = 0.2
UW = 2048
RAW = 6
SPL = 3

C_ID, C_HEAD, C_ONES, C_ROT, C_SUF, C_TRI = (P * j for j in range(6))
C_COS = 6 * P
C_SIN = C_COS + T
C_FOXM = C_SIN + T
C_DIFM = C_FOXM + P
C_SBM = C_DIFM + P
C_IOTA = C_SBM + P
C_SID = C_IOTA + CAP
C_EI = C_SID + 1
C_LT = C_EI + E
C_XI = C_LT + E * E
C_END = C_XI + EXTRA * E


def constants():
    c = np.zeros((P, C_END), np.float32)
    r = np.arange(P)
    c[:, C_ID:C_ID + P] = np.eye(P)
    c[:, C_HEAD:C_HEAD + P] = r[:, None] // HD == r[None, :] // HD
    c[:, C_ONES:C_ONES + P] = 1.0
    for d in range(P):
        if d % HD < HD // 2:
            c[d + HD // 2, C_ROT + d] = -1.0
        else:
            c[d - HD // 2, C_ROT + d] = 1.0
    c[:, C_SUF:C_SUF + P] = r[:, None] > r[None, :]
    c[:, C_TRI:C_TRI + P] = r[:, None] <= r[None, :]
    inv = (np.float32(1.0) / (np.float32(10000.0) ** (np.arange(0, HD, 2, dtype=np.float32) / np.float32(HD))))
    ang = np.arange(T, dtype=np.float32)[:, None] * inv[None, :].astype(np.float32)
    ang = np.concatenate([ang, ang], -1).T
    c[:, C_COS:C_COS + T] = np.tile(np.cos(ang), (2, 1))
    c[:, C_SIN:C_SIN + T] = np.tile(np.sin(ang), (2, 1))
    c[:, C_FOXM:C_FOXM + P] = np.where(r[None, :] <= r[:, None], 0.0, NEG)
    c[:, C_DIFM:C_DIFM + P] = np.where(r[None, :] // 64 <= r[:, None] // 64, 0.0, NEG)
    c[:, C_SBM:C_SBM + P] = r[None, :] > r[:, None]
    c[:, C_IOTA:C_IOTA + CAP] = np.arange(CAP)[None, :]
    c[:, C_SID] = r
    c[:, C_EI:C_EI + E] = np.arange(E)[None, :]
    e = np.arange(E)
    c[:, C_LT:C_LT + E * E] = (e[None, :] < e[:, None]).reshape(1, -1)
    c[:, C_XI:C_XI + EXTRA * E] = np.repeat(np.arange(EXTRA), E)[None, :]
    return c


V_MIX, V_MEM, V_FFN = 0, 16, 32
V_CB, V_DWB, V_LNG, V_LNB = 48, 60, 66, 72
V_MIX2, V_FFN2, V_FIN2, V_C = 78, 86, 94, 102
V_SUB, V_FGQ, V_FGK, V_GMQ, V_GMK, V_LQ, V_LK = 110, 111, 112, 113, 115, 117, 118
V_ADA = 119
V_TAP = V_ADA + 48
V_BF = V_TAP + TAPS * CT
V_WF = V_BF + FOX_HEADS
V_RT = V_WF + KT * FOX_HEADS
V_END = V_RT + KT * E

FF0_CH = FF0 // T
FF2_CH = FF2 // T
MOE_CH = EFF // 512
ADA_UNITS = 6 * D // T


def ffn_order(n, ins, out):
    order = []
    for c in range(n):
        order += [f"{name}{c}" for name in ins]
        if c:
            order.append(f"{out}{c - 1}")
    return order + [f"{out}{n - 1}"]


UNITS_A = (["mk0", "mv0", "mq0"] + [f"{w}{j}" for w in ("fq", "fk", "fv") for j in range(3)]
           + [f"fo{j}" for j in range(4)] + ffn_order(FF0_CH, ("g", "u"), "d") + ["mk1", "mv1"]
           + [f"ci{j}" for j in range(6)] + ["mq1"] + [f"ada{j}" for j in range(ADA_UNITS)]
           + [f"co{j}" for j in range(4)])
UNITS_B = ([f"{w}{j}" for w in ("dq", "dk", "dv", "sq", "sk", "sv") for j in range(2)] + [f"wo{j}" for j in range(4)]
           + ffn_order(FF2_CH, ("a",), "b"))
UNITS = UNITS_A + UNITS_B
NUMBER = {name: n for n, name in enumerate(UNITS)}
SPLIT = [name for name in UNITS if not name.startswith("ada")]
POS = {name: p for p, name in enumerate(SPLIT)}
U0 = len(UNITS_A)
POS0 = len([name for name in UNITS_A if name in POS])

MOE_ORDER = [(name[0], int(name[1:]), half) for name in ffn_order(MOE_CH, ("g", "u"), "d") for half in range(2)]
MOE_UNITS = len(MOE_ORDER)
assert MOE_UNITS % RAW == 0 and MOE_UNITS % SPL == 0
MOE_USES = {6: ["S0", "T0", "S2", "T2", "T4", "T6", "G1"], 7: ["S1", "S3", "T1", "T3", "T5", "G0"]}
MOE_BANK = {use: (b, len(uses), j) for b, uses in MOE_USES.items() for j, use in enumerate(uses)}


class Sessions:

    def __init__(self):
        self.fills, self.drains, self.at = [0] * 8, [0] * 8, {}

    def add(self, name, bank, own_signal=False):
        assert name not in self.at, name
        self.at[name] = (bank, self.fills[bank] + 1, self.drains[bank])
        self.drains[bank] += 1
        if not own_signal:
            self.fills[bank] += 1


def build(nc, x_dram, mem_dram, cst_dram, cols_dram, main_dram, moe_dram, out):
    ctx = ExitStack()
    with ctx:
        def sb(name, shape, dt=F32):
            return ctx.enter_context(nc.sbuf_tensor(name, shape, dt))

        sems = {}

        def sem(name):
            if name not in sems:
                sems[name] = ctx.enter_context(nc.semaphore(name))
            return sems[name]

        raw = sb("raw", [P, RAW, UW])
        wh = sb("wh", [P, SPL, UW], F32R)
        wl = sb("wl", [P, SPL, UW], F32R)
        xh = sb("xh", [P, KT, T], F32R)
        xl = sb("xl", [P, KT, T], F32R)
        ah = sb("ah", [P, 2, 512], F32R)
        al = sb("al", [P, 2, 512], F32R)
        hT = sb("hT", [P, KT, T])
        big = sb("big", [P, 8192])
        sqz = sb("sqz", [P, 2048])
        cst = sb("cst", [P, C_END])
        cols = sb("cols", [P, V_END])
        att_p = sb("att_p", [P, 3, 512])
        att_pT = sb("att_pT", [P, 2, 512])
        rn = sb("rn", [P, T])
        rn_mem = sb("rn_mem", [P, T])
        lsf = sb("lsf", [P, 2, TT, FOX_HEADS])
        ctok = sb("ctok", [P, TT, FOX_HEADS])
        nmx = sb("nmx", [P, 3, TT])
        ssum = sb("ssum", [P, 3, TT])
        rsum = sb("rsum", [P, 3, TT])
        gq8 = sb("gq8", [P, 3])
        ccol = sb("ccol", [P, KT])
        mod = sb("mod", [P, 48])
        gs = sb("gs", [P, 2, KT])
        lam = sb("lam", [P, 8])
        mx8 = sb("mx8", [P, TT, 8])
        ix8 = sb("ix8", [P, TT, 8], U32)
        lg = sb("lg", [P, TT, E])
        ixf = sb("ixf", [P, TT, 2])
        oh = sb("oh", [P, 2, TT, E])
        plan_f = sb("plan_f", [P, 16, 16])
        lt8 = sb("lt8", [P, E, E])
        kcol = sb("kcol", [P, 2, TT])
        gcol = sb("gcol", [P, 2, TT])
        pexp = sb("pexp", [P, 32])
        etab = sb("etab", [1, 16], I32)
        nbt = sb("nbt", [1, 2], I32)

        def cc(at, n=P):
            return cst[:, at:at + n]

        ident, headones, ones, rot = cc(C_ID), cc(C_HEAD), cc(C_ONES), cc(C_ROT)
        sufx, tri = cc(C_SUF), cc(C_TRI)

        def flat(t):
            return t[:, :, :].rearrange("p a b -> p (a b)")

        def view(at, a, b, base=None):
            return (big if base is None else base)[:, at:at + a * b].rearrange("p (a b) -> p a b", a=a)

        qT = view(0, 8, T)
        kz = view(2048, 16, T)
        vv = view(6144, TT, 1024)
        mem0 = view(0, KT, T)
        x_sq = big[:, 6144:8192]
        upad = view(0, CT, PAD + T)
        cacc = view(1792, CT, T)
        abuf = view(3328, CT, T)
        mem1 = view(3328, KT, T)
        q1 = view(4864, 2, T)
        mkz1 = view(5376, MEM_HEADS, T)
        mv1 = view(6400, TT, MEM)
        z_tok = view(0, TT, D)
        y_tok = big[:, 2048:3072]
        krow = view(4096, 4, T)
        sel = view(5120, TT, CAP)
        scat = big[:, 5376:5376 + T]
        scat_b = big[:, 5632:5632 + T]
        normed = view(0, KT, T, sqz)
        selh = sqz[:, 0:FOX_HEADS * P].rearrange("p (h m) -> p h m", h=FOX_HEADS)
        negc = sqz[:, FOX_HEADS * P:FOX_HEADS * P + T]
        xgh = flat(xh)[:, 0:KT * CAP].rearrange("p (a b) -> p a b", a=KT)
        xgl = flat(xl)[:, 0:KT * CAP].rearrange("p (a b) -> p a b", a=KT)
        sg = att_p
        sb_l = sqz[:, 0:768].rearrange("p (a b) -> p a b", a=2)
        sb_b = sqz[:, 768:1536].rearrange("p (a b) -> p a b", a=2)
        att_flat = flat(att_p)
        sb_m = att_flat[:, 0:768].rearrange("p (a b) -> p a b", a=2)
        sb_a = att_flat[:, 768:1536].rearrange("p (a b) -> p a b", a=2)

        def pair_of(t, j):
            return t[:, 2 * j:2 * j + 2, :].rearrange("p a b -> p (a b)")

        def four_of(t, j):
            return t[:, 4 * j:4 * j + 4, :].rearrange("p a b -> p (a b)")

        ps = ctx.enter_context(nc.psum_tensor("ps", [P, 8, 512], F32))

        S = Sessions()

        def product(name, b):
            S.add(name, b, own_signal=True)

        S.add("nsum0", 6)
        S.add("nsum1", 7)
        product("mk0", 0)
        S.add("lam", 2)
        product("mv0", 1)
        S.add("qsum0", 4)
        S.add("foxf", 2)
        product("mq0", 3)
        product("fq0", 0)
        S.add("qsum1", 5)
        S.add("cum", 6)
        for j in range(1, 6):
            product(f"{'fq' if j < 3 else 'fk'}{j % 3}", j % 4)
            S.add(f"qsum{1 + j}", 4 + (1 + j) % 2)
        product("fv0", 2)
        S.add("qsum7", 5)
        product("fv1", 3)
        product("fv2", 0)

        maps = []

        def add_maps(kinds):
            first = len(maps)
            maps.extend(kinds)
            return range(first, len(maps))

        fox_maps = add_maps([
            dict(kind="fox" if h < FOX_HEADS else "mem", head=h, q=qT[:, h // 2, :], k=kz[:, h, :],
                 v=[vv[:, t, HD * h:HD * h + HD] for t in range(TT)], row=HD * (h % 2), m=HD, to=h // 2)
            for h in range(FOX_HEADS + MEM_HEADS)])
        mem_maps = add_maps([
            dict(kind="mem", head=h, q=q1[:, h // 2, :], k=mkz1[:, h, :],
                 v=[mv1[:, t, HD * h:HD * h + HD] for t in range(TT)], row=HD * (h % 2), m=HD, to=CT + h // 2)
            for h in range(MEM_HEADS)])
        diff_maps = add_maps([
            dict(kind="diff", head=m, q=qT[:, m // 2, :], k=kz[:, m, :],
                 v=[vv[:, t, P * (m // 2):P * (m // 2) + P] for t in range(TT)], row=0, m=P, to=m // 2)
            for m in range(8)])

        T_LAG, PV_LAG = 2, 3

        def add_attention(rng):
            n, a0 = len(rng), rng[0]
            for i in range(n + PV_LAG):
                if i < n:
                    S.add(f"sc{a0 + i}", (a0 + i) % 2)
                if 0 <= i - T_LAG < n:
                    S.add(f"pT{a0 + i - T_LAG}", 2 + (a0 + i) % 2)
                if 0 <= i - PV_LAG < n and (i - PV_LAG) % 2 == 0:
                    g = (a0 + i - PV_LAG) // 2
                    S.add(f"pv{g}", 4 + g % 2, own_signal=True)

        add_attention(fox_maps)
        for j in range(4):
            product(f"fo{j}", j)
        S.add("nsum2", 6)
        for c in range(FF0_CH):
            product(f"g{c}", 2 * (c % 2))
            product(f"u{c}", 2 * (c % 2) + 1)
        for j in range(4):
            product(f"down0_{j}", 4 + j)
        product("mk1", 2)
        product("mv1", 3)
        S.add("qsum8", 0)
        S.add("nsum3", 1)
        for j in range(6):
            product(f"ci{j}", j % 4)
        product("mq1", 2)
        S.add("qsum9", 4)
        add_attention(mem_maps)
        product("ada", 6)
        S.add("lnsum", 7)
        S.add("lnvar", 7)
        for j in range(4):
            product(f"co{j}", j)
        S.add("nsum4", 4)
        S.add("router", 5)
        for j in range(4):
            S.add(f"ztok{j}", j)
        S.add("mcum", 5)
        S.add("krow", 6)
        S.add("grow", 7)
        for j in range(2):
            S.add(f"gather{j}", 4 + j)
        before_moe = list(S.drains)
        for j in range(4):
            S.add(f"scat{j}", 4 + j)
        S.add("nsum5", 0)
        ROPED = ("dq0", "dq1", "dk0", "dk1")
        WIN = UNITS_B[:12]
        for j, name in enumerate(WIN):
            product(name, (1 + j) % 4)
            if 1 <= j <= 4:
                S.add(f"rot{j - 1}", 4 + (j - 1) % 2)
        add_attention(diff_maps)
        SBH = 8
        for i in range(SBH + 2):
            if i < SBH:
                S.add(f"sbs{i}", i % 2)
            if 0 <= i - 1 < SBH:
                S.add(f"sbx{i - 1}", 2 + (i - 1) % 2)
            if 0 <= i - 2 < SBH and i % 2 == 0:
                S.add(f"sbo{(i - 2) // 2}", 4 + (i // 2) % 2, own_signal=True)
        S.add("sub0", 6)
        S.add("sub1", 7)
        for j in range(4):
            product(f"wo{j}", j)
        S.add("nsum6", 4)
        for c in range(FF2_CH):
            product(f"a{c}", c % 4)
        for j in range(4):
            product(f"down2_{j}", 4 + j)
        S.add("nsum7", 0)

        def bank(name):
            return ps[:, S.at[name][0], :]

        def claim(pe, name):
            b, _, k = S.at[name]
            if k:
                pe.wait_ge(sem(f"drained{b}"), k)

        def wait_filled(eng, name):
            b, k, _ = S.at[name]
            eng.wait_ge(sem(f"filled{b}"), k)

        def wait_drained(eng, name):
            b, _, k = S.at[name]
            eng.wait_ge(sem(f"drained{b}"), k + 1)

        def filled(name):
            return sem(f"filled{S.at[name][0]}")

        def drained(name):
            return sem(f"drained{S.at[name][0]}")

        def past_moe(count, nb):
            return count if nb is None else nb * MOE_UNITS + count

        def wait_done(eng, name, nb=None):
            eng.wait_ge(sem("unit_done"), past_moe(NUMBER[name] + 1, nb))

        def wait_loaded(eng, n, nb=None):
            turns = 16 * (n // RAW + 1)
            eng.wait_ge(sem(f"ring_loaded{n % RAW}"), turns if nb is None else nb * (16 * MOE_UNITS // RAW) + turns)

        RAW_STREAM = {name: r for r, name in enumerate(
            ("mem0", "x", "ffn0", "mem1", "mix1", "ffn1", "mix2", "ffn2", "final"))}
        SPLIT_STREAM = {name: s for s, name in enumerate(("mem0", "x", "ffn0", "mem1", "mix1", "mix2", "ffn2"))}

        def wait_raw(eng, name, k=KT - 1):
            eng.wait_ge(sem("norm_raw"), KT * RAW_STREAM[name] + k + 1)

        def wait_hi(eng, name, k=KT - 1):
            eng.wait_ge(sem("norm_hi"), KT * SPLIT_STREAM[name] + k + 1)

        def wait_lo(eng, name, k=KT - 1):
            eng.wait_ge(sem("norm_lo"), KT * SPLIT_STREAM[name] + k + 1)

        block = ctx.enter_context(nc.Block())

        @block.sync
        def _(sp):
            def load(n, nb=None):
                if n >= RAW:
                    before = UNITS[n - RAW]
                    if n >= U0 + RAW or n < U0 and before in POS:
                        sp.wait_ge(sem("lo_ready"), past_moe(POS[before] + 1, nb))
                    elif n < U0:
                        sp.wait_ge(sem("unit_done"), n - RAW + 1)
                    else:
                        sp.wait_ge(sem("lo_ready"), past_moe(POS0 + n - U0 - RAW + 1, nb))
                src = main_dram[n:n + 1, :, :].rearrange("a p f -> p (a f)")
                sp.dma_start(raw[:, n % RAW, :], src).then_inc(sem(f"ring_loaded{n % RAW}"), 16)

            def load_expert(j, e):
                s = (U0 + j) % RAW
                src = moe_dram[e, j:j + 1, :, :].rearrange("a b p f -> p (a b f)")
                sp.dma_start(raw[:, s, :], src).then_inc(sem(f"ring_loaded{s}"), 16)

            for n in range(U0):
                load(n)
            for j in range(MOE_UNITS):
                before = UNITS[U0 + j - RAW] if j < RAW else None
                if before is not None and before not in POS:
                    sp.wait_ge(sem("unit_done"), U0 + j - RAW + 1)
                else:
                    sp.wait_ge(sem("lo_ready"), POS0 + j - RAW + 1)
                load_expert(j, slice(0, 1))
            sp.wait_ge(sem("moe_plan"), 2)
            nb = sp.value_load(nbt[0:1, 0:1], min_val=E, max_val=MAXBLK)
            last = sp.value_load(nbt[0:1, 1:2], min_val=E - 1, max_val=MAXBLK - 1)
            with sp.Fori(0, last) as i:
                e = sp.value_load(etab[0:1, bass.ds(i + 1, 1)], min_val=0, max_val=E - 1)
                for j in range(MOE_UNITS):
                    sp.wait_ge(sem("lo_ready"), i * MOE_UNITS + POS0 + MOE_UNITS + j - RAW + 1)
                    load_expert(j, bass.ds(e, 1))
            for n in range(U0, len(UNITS)):
                load(n, nb)
            for half in range(2):
                k = KT // 2 * half
                wait_raw(sp, "final", k + KT // 2 - 1)
                sp.dma_start(out[:, T * k:T * (k + KT // 2)],
                             sqz[:, T * k:T * (k + KT // 2)]).then_inc(sem("stored"), 16)
            sp.wait_ge(sem("stored"), 32)

        @block.gpsimd
        def _(pool):
            def zero_keys(keys, name):
                pool.memset(keys[:, :, :], 0.0).then_inc(sem(name), 1)

            def subtract_hi(name):
                for k in range(KT):
                    wait_hi(pool, name, k)
                    pool.tensor_tensor(xl[:, k, :], normed[:, k, :], xh[:, k, :].bitcast(F32),
                                       ALU.subtract).then_inc(sem("norm_lo"), 1)

            zero_keys(kz, "keys_zeroed")
            subtract_hi("mem0")
            subtract_hi("x")
            wait_filled(pool, "foxf")
            wait_lo(pool, "x")
            pool.memset(negc, 0.0).then_inc(sem("negc_zeroed"), 1)

            def normalise(rng):
                for a in rng:
                    w0, w1 = (P, 3 * P) if maps[a]["kind"] != "mem" else (T, 2 * T)
                    pool.wait_ge(sem("att_rsum"), a + 1)
                    pool.tensor_scalar(att_p[:, a % 3, 0:w0], att_p[:, a % 3, 0:w0], rsum[:, a % 3, 0:1], None,
                                       ALU.mult).then_inc(sem("att_probs"), 1)
                    pool.tensor_scalar(att_p[:, a % 3, w0:w1], att_p[:, a % 3, w0:w1], rsum[:, a % 3, 1:2], None,
                                       ALU.mult).then_inc(sem("att_probs"), 1)

            normalise(fox_maps)
            pool.wait_ge(sem("att_pv"), len(fox_maps))
            pool.dma_start(big[:, 3328:3328 + KT * T], mem_dram).then_inc(sem("ld_mem1"), 16)
            zero_keys(mkz1, "keys1_zeroed")
            pool.memset(upad[:, :, 0:PAD], 0.0).then_inc(sem("upad_zeroed"), 1)
            subtract_hi("ffn0")

            def hidden_lo(c, count):
                pool.wait_ge(sem("hid_hi"), count)
                pool.tensor_tensor(al[:, c % 2, :], sg[:, c % 2, :], ah[:, c % 2, :].bitcast(F32),
                                   ALU.subtract).then_inc(sem("hid_lo"), 1)

            for c in range(FF0_CH):
                hidden_lo(c, c + 1)
            subtract_hi("mem1")
            subtract_hi("mix1")
            normalise(mem_maps)
            for c in range(CT):
                pool.wait_ge(sem("conv_hi"), c + 1)
                pool.tensor_tensor(xl[:, c, :], cacc[:, c, :], xh[:, c, :].bitcast(F32),
                                   ALU.subtract).then_inc(sem("conv_lo"), 1)
            wait_done(pool, "co3")
            pool.memset(y_tok, 0.0).then_inc(sem("moe_zeroed"), 1)
            pool.memset(scat, 0.0).then_inc(sem("moe_zeroed"), 1)
            for j in range(4):
                wait_drained(pool, f"scat{j}")
            zero_keys(kz, "keys_zeroed")
            normalise(diff_maps)

            sbm = cc(C_SBM)
            for i in range(SBH + 1):
                if i < SBH:
                    b = i % 2
                    pool.wait_ge(sem("sb_m"), i + 1)
                    for at in (0, 2 * P):
                        pool.tensor_tensor(sb_m[:, b, at:at + P], sb_m[:, b, at:at + P], sbm,
                                           ALU.mult).then_inc(sem("sb_masked"), 1)
                if i >= 1:
                    b = (i - 1) % 2
                    pool.wait_ge(sem("sb_exp"), i)
                    for at in (0, 2 * P):
                        pool.tensor_tensor(sb_a[:, b, at:at + P], sb_a[:, b, at:at + P], sbm,
                                           ALU.mult).then_inc(sem("sb_probs"), 1)
            for c in range(FF2_CH):
                hidden_lo(c, FF0_CH + c + 1)

        @block.scalar
        def _(act):
            act.dma_start(flat(mem0), mem_dram).then_inc(sem("ld_mem"), 16)
            act.dma_start(cst[:, :], cst_dram).then_inc(sem("ld_cst"), 16)
            act.dma_start(flat(hT), x_dram).then_inc(sem("ld_x"), 16)
            act.dma_start(cols[:, :], cols_dram).then_inc(sem("ld_cols"), 16)

            step = [0]

            def link(ins):
                step[0] += 1
                ins.then_inc(sem("act_step"), 1)
                act.wait_ge(sem("act_step"), step[0])

            def split_hi(p, nb=None):
                n = NUMBER[SPLIT[p]]
                wait_loaded(act, n, nb)
                if p >= SPL:
                    wait_done(act, SPLIT[p - SPL], nb)
                act.activation(wh[:, p % SPL, :], raw[:, n % RAW, :], ACT.Copy).then_inc(sem("hi_ready"), 1)

            def split_after(name, nb=None):
                p = POS[name] + SPL
                if p >= len(SPLIT):
                    return
                if nb is None and p >= POS0:
                    wait_loaded(act, U0 + p - POS0)
                    wait_done(act, name)
                    act.activation(wh[:, p % SPL, :], raw[:, (U0 + p - POS0) % RAW, :],
                                   ACT.Copy).then_inc(sem("hi_ready"), 1)
                else:
                    split_hi(p, nb)

            def square(src, dst, j):
                act.activation(dst[:, 512 * j:512 * j + 512], pair_of(src, j), ACT.Square).then_inc(sem("norm_sq"), 1)

            def norm_sd(k, scale):
                wait_drained(act, f"nsum{k}")
                act.activation(scale[:, :], scale[:, :], ACT.Sqrt).then_inc(sem("norm_sd"), 1)

            def norm_hi(name):
                for k in range(KT):
                    wait_raw(act, name, k)
                    act.activation(xh[:, k, :], normed[:, k, :], ACT.Copy).then_inc(sem("norm_hi"), 1)

            def norm_hi_shifted(name, at):
                for k in range(KT):
                    wait_raw(act, name, k)
                    act.activation(xh[:, k, :], normed[:, k, :], ACT.Identity,
                                   bias=mod[:, at + k:at + k + 1]).then_inc(sem("norm_hi"), 1)

            def qk_square(k, name):
                wait_done(act, name)
                if k >= 2:
                    wait_filled(act, f"qsum{k - 2}")
                act.activation(att_pT[:, k % 2, :], bank(name), ACT.Square).then_inc(sem("qk_sq"), 1)

            def qk_sd(k):
                wait_drained(act, f"qsum{k}")
                act.activation(att_p[:, k % 2, :], att_p[:, k % 2, :], ACT.Sqrt).then_inc(sem("qk_sd"), 1)

            def values_out(name, dst, nb=None):
                wait_done(act, name, nb)
                act.activation(dst, bank(name).rearrange("p (a b) -> p a b", a=TT), ACT.Copy).then_inc(drained(name), 1)

            act.wait_ge(sem("ld_mem"), 16)
            for j in range(4):
                square(mem0, sqz, j)
            act.wait_ge(sem("ld_x"), 16)
            for j in range(4):
                square(hT, x_sq, j)
            norm_sd(0, rn_mem)
            norm_sd(1, rn)
            for p in range(SPL):
                split_hi(p)
            norm_hi("mem0")
            qk_square(0, "mk0")
            split_after("mk0")
            wait_filled(act, "nsum1")
            values_out("mv0", vv[:, :, FOX:D])
            split_after("mv0")
            norm_hi("x")
            qk_sd(0)
            act.wait_ge(sem("ld_cols"), 16)
            act.activation(ccol[:, :], cols[:, V_C:V_C + KT], ACT.Silu).then_inc(sem("ccol_ready"), 1)
            wait_filled(act, "lam")
            act.activation(lam[:, 2:4], bank("lam")[:, 0:2], ACT.Exp).then_inc(drained("lam"), 1)
            act.wait_ge(sem("fox_negabs"), 1)
            link(act.activation(lsf[:, 1, :, :], lsf[:, 1, :, :], ACT.Exp))
            act.activation(lsf[:, 1, :, :], lsf[:, 1, :, :], ACT.Ln, bias=1.0).then_inc(sem("fox_log1p"), 1)
            qk_square(1, "mq0")
            split_after("mq0")
            for j in range(6):
                name = UNITS_A[3 + j]
                qk_square(2 + j, name)
                split_after(name)
                qk_sd(1 + j)
                if j == 0:
                    act.wait_ge(sem("negc_zeroed"), 1)
                    wait_filled(act, "cum")
                    act.activation(negc[0:FOX_HEADS, :], bank("cum")[0:FOX_HEADS, 0:T], ACT.Copy,
                                   scale=-1.0).then_inc(sem("negc_ready"), 1)
            for j in range(3):
                values_out(f"fv{j}", vv[:, :, T * j:T * j + T])
                split_after(f"fv{j}")
                if j == 0:
                    qk_sd(7)

            def attention(rng):
                n, a0 = len(rng), rng[0]
                for i in range(n + PV_LAG + 1):
                    if i < n:
                        a = a0 + i
                        w0, w1 = (P, 3 * P) if maps[a]["kind"] != "mem" else (T, 2 * T)
                        act.wait_ge(sem("att_max"), 2 * (a + 1))
                        for t, (lo, hi) in enumerate(((0, w0), (w0, w1))):
                            act.activation(att_p[:, a % 3, lo:hi], att_p[:, a % 3, lo:hi], ACT.Exp,
                                           bias=nmx[:, a % 3, t:t + 1],
                                           accum_out=ssum[:, a % 3, t:t + 1]).then_inc(sem("att_exp"), 1)
                    if 0 <= i - T_LAG < n:
                        a = a0 + i - T_LAG
                        w = 3 * P if maps[a]["kind"] != "mem" else 4 * P
                        wait_filled(act, f"pT{a}")
                        if a >= 2:
                            act.wait_ge(sem("att_pv"), a - 1)
                        act.activation(att_pT[:, a % 2, 0:w], bank(f"pT{a}")[:, 0:w],
                                       ACT.Copy).then_inc(drained(f"pT{a}"), 1)
                    if 0 <= i - PV_LAG - 1 < n and (i - PV_LAG - 1) % 2 == 1 and maps[a0]["kind"] != "diff":
                        g = (a0 + i - PV_LAG - 1) // 2
                        act.wait_ge(sem("att_pv"), 2 * (g + 1))
                        act.activation(xh[:, maps[2 * g]["to"], :], bank(f"pv{g}")[:, 0:T],
                                       ACT.Copy).then_inc(sem("mix_hi"), 1)

            attention(fox_maps)

            for j in range(4):
                wait_drained(act, f"fo{j}")
                square(hT, sqz, j)
                split_after(f"fo{j}")
            norm_sd(2, rn)
            norm_hi("ffn0")

            def hidden_hi(c, name):
                wait_drained(act, name)
                act.activation(ah[:, c % 2, :], sg[:, c % 2, :], ACT.Copy).then_inc(sem("hid_hi"), 1)

            for name in ffn_order(FF0_CH, ("g", "u"), "d"):
                c = int(name[1:])
                if name[0] == "g":
                    wait_done(act, name)
                    if c >= 2:
                        act.wait_ge(sem("hid_lo"), c - 1)
                    act.activation(sg[:, c % 2, :], bank(name), ACT.Silu).then_inc(drained(name), 1)
                split_after(name)
                if name[0] == "u":
                    hidden_hi(c, name)
                if name == f"u{FF0_CH - 1}":
                    norm_hi("mem1")
            wait_lo(act, "mem1")
            for j in range(4):
                wait_drained(act, f"down0_{j}")
                square(hT, sqz, j)
            qk_square(8, "mk1")
            split_after("mk1")
            values_out("mv1", mv1)
            split_after("mv1")
            qk_sd(8)
            norm_sd(3, rn)
            norm_hi("mix1")

            for j in range(6):
                wait_done(act, f"ci{j}")
                for t in range(2):
                    c = 2 * j + t
                    if j < 3:
                        ins = act.activation(abuf[:, c, :], bank(f"ci{j}")[:, T * t:T * t + T], ACT.Identity,
                                             bias=cols[:, V_CB + c:V_CB + c + 1])
                    else:
                        ins = act.activation(cacc[:, c - CT, :], bank(f"ci{j}")[:, T * t:T * t + T], ACT.Sigmoid,
                                             bias=cols[:, V_CB + c:V_CB + c + 1])
                ins.then_inc(drained(f"ci{j}"), 1)
                if j < 4:
                    split_after(f"ci{j}")
            qk_square(9, "mq1")
            qk_sd(9)
            attention(mem_maps)
            for name in ("ci4", "ci5", "mq1"):
                split_after(name)
            act.wait_ge(sem("ln_centred"), 1)
            act.activation(sqz[:, 0:CT * T], flat(cacc), ACT.Square).then_inc(sem("ln_sq"), 1)
            wait_drained(act, "lnvar")
            act.activation(rn[:, :], rn[:, :], ACT.Sqrt).then_inc(sem("ln_sd"), 1)
            act.wait_ge(sem("ln_scaled"), 1)
            for c in range(CT):
                act.activation(cacc[:, c, :], cacc[:, c, :], ACT.Silu, bias=cols[:, V_LNB + c:V_LNB + c + 1],
                               scale=cols[:, V_LNG + c:V_LNG + c + 1]).then_inc(sem("conv_silu"), 1)
            for c in range(CT):
                act.wait_ge(sem("conv_silu"), c + 1)
                act.activation(xh[:, c, :], cacc[:, c, :], ACT.Copy).then_inc(sem("conv_hi"), 1)
            for j in range(4):
                wait_drained(act, f"co{j}")
                square(hT, sqz, j)
                split_after(f"co{j}")
            norm_sd(4, rn)
            for j in range(4):
                wait_filled(act, f"ztok{j}")
                act.activation(z_tok[:, j // 2, 512 * (j % 2):512 * (j % 2) + 512], bank(f"ztok{j}"),
                               ACT.Copy).then_inc(drained(f"ztok{j}"), 1)
            act.wait_ge(sem("gate_diff"), 1)
            act.activation(pexp[:, 0:2], pexp[:, 0:2], ACT.Exp).then_inc(sem("gate_exp"), 1)
            for j in range(2):
                wait_filled(act, f"gather{j}")
                act.activation(four_of(xgh, j), bank(f"gather{j}"), ACT.Copy).then_inc(sem("gather_hi"), 1)

            act.wait_ge(sem("moe_plan"), 2)
            nb = act.value_load(nbt[0:1, 0:1], min_val=E, max_val=MAXBLK)
            with act.Fori(0, nb) as i:
                def split_next(j):
                    n, p = U0 + j + SPL, POS0 + j + SPL
                    act.wait_ge(sem(f"ring_loaded{n % RAW}"), i * (16 * MOE_UNITS // RAW) + 16 * (n // RAW + 1))
                    act.wait_ge(sem("unit_done"), i * MOE_UNITS + U0 + j + 1)
                    act.activation(wh[:, p % SPL, :], raw[:, n % RAW, :], ACT.Copy).then_inc(sem("hi_ready"), 1)

                def turned_hi(c):
                    b, per, use = MOE_BANK[f"T{c}"]
                    act.wait_ge(sem(f"moe_filled{b}"), i * per + use + 1)
                    act.activation(ah[:, c % 2, :], ps[:, b, :], ACT.Copy).then_inc(sem("moe_hid_hi"), 1)

                for j, (kind, c, half) in enumerate(MOE_ORDER):
                    if kind == "g" and half == 1:
                        act.wait_ge(sem("unit_done"), i * MOE_UNITS + U0 + j + 1)
                        act.activation(sg[:, c % 2, :], ps[:, 2 * (c % 2), :], ACT.Silu).then_inc(sem("moe_silu"), 1)
                    split_next(j)
                    if kind == "g" and half == 1 and c >= 1:
                        turned_hi(c - 1)
                    if (kind, c, half) == ("d", MOE_CH - 2, 1):
                        turned_hi(MOE_CH - 1)
                        for g in range(2):
                            b, per, use = MOE_BANK[f"G{g}"]
                            act.wait_ge(sem(f"moe_filled{b}"), i * per + use + 1)
                            act.activation(four_of(xgh, g), ps[:, b, :], ACT.Copy).then_inc(sem("gather_hi"), 1)
                for g in range(2):
                    act.activation(y_tok[:, 512 * g:512 * g + 512], ps[:, 4 + g, :],
                                   ACT.Copy).then_inc(sem("moe_y"), 1)

            for j in range(4):
                wait_drained(act, f"scat{j}")
                square(hT, sqz, j)
            norm_sd(5, rn)
            norm_hi_shifted("mix2", 0)
            for j, name in enumerate(ROPED):
                wait_done(act, name, nb)
                if j >= 2:
                    act.wait_ge(sem("rope_done"), rope_count(j - 1))
                act.activation(att_pT[:, j % 2, :], bank(name), ACT.Copy).then_inc(drained(name), 1)
                split_after(name, nb)
            for j in range(2):
                values_out(f"dv{j}", vv[:, :, T * j:T * j + T], nb)
                split_after(f"dv{j}", nb)
            for j in range(2):
                wait_done(act, f"sq{j}", nb)
                act.activation(pair_of(qT, 2 + j), bank(f"sq{j}"), ACT.Copy, scale=SCALE).then_inc(drained(f"sq{j}"), 1)
                split_after(f"sq{j}", nb)
            act.wait_ge(sem("keys_zeroed"), 2)
            for j in range(2):
                wait_done(act, f"sk{j}", nb)
                src = bank(f"sk{j}").rearrange("p (a b) -> p a b", a=2)
                act.activation(kz[0:HD, 8 + 4 * j:12 + 4 * j:2, :], src[0:HD, :, :], ACT.Copy)
                act.activation(kz[HD:P, 9 + 4 * j:12 + 4 * j:2, :], src[HD:P, :, :],
                               ACT.Copy).then_inc(drained(f"sk{j}"), 1)
                split_after(f"sk{j}", nb)
            for j in range(2):
                values_out(f"sv{j}", vv[:, :, 512 + T * j:512 + T * j + T], nb)
                split_after(f"sv{j}", nb)
            act.wait_ge(sem("rope_done"), rope_count(4))
            attention(diff_maps)

            for i in range(SBH + 2):
                if i < SBH:
                    b = i % 2
                    wait_filled(act, f"sbs{i}")
                    if i >= 2:
                        wait_drained(act, f"sbs{i - 2}")
                    link(act.activation(sb_l[:, b, :], bank(f"sbs{i}")[:, 0:384], ACT.Abs))
                    link(act.activation(sb_l[:, b, :], sb_l[:, b, :], ACT.Exp, scale=-1.0))
                    act.activation(sb_l[:, b, :], sb_l[:, b, :], ACT.Ln, bias=1.0).then_inc(sem("sb_log1p"), 1)
                if 0 <= i - 1 < SBH:
                    j = i - 1
                    wait_drained(act, f"sbx{j}")
                    if j >= 2:
                        act.wait_ge(sem("sb_pv"), j - 1)
                    act.activation(sb_a[:, j % 2, :], sb_b[:, j % 2, :], ACT.Exp).then_inc(sem("sb_exp"), 1)
                if 0 <= i - 2 < SBH and i % 2 == 1:
                    g = (i - 2) // 2
                    act.wait_ge(sem("sb_pv"), 2 * (g + 1))
                    act.activation(xh[:, 4 + g, :], bank(f"sbo{g}")[:, 0:T], ACT.Copy).then_inc(sem("sb_hi"), 1)

            act.wait_ge(sem("att_pv"), len(maps))
            for j in range(2):
                for g in range(2):
                    wait_drained(act, f"pv{diff_maps[0] // 2 + 2 * j + g}")
                act.activation(att_pT[:, j, :], pair_of(qT, j), ACT.Square).then_inc(sem("sub_sq"), 1)
            for j in range(2):
                wait_drained(act, f"sub{j}")
                act.activation(att_p[:, j, :], att_p[:, j, :], ACT.Sqrt).then_inc(sem("sub_sd"), 1)
            for j in range(2):
                act.wait_ge(sem("sub_out"), j + 1)
                act.activation(pair_of(xh, j), pair_of(qT, j), ACT.Copy).then_inc(sem("sub_hi"), 1)

            for j in range(4):
                wait_drained(act, f"wo{j}")
                square(hT, sqz, j)
                split_after(f"wo{j}", nb)
            norm_sd(6, rn)
            norm_hi_shifted("ffn2", 24)
            for name in ffn_order(FF2_CH, ("a",), "b"):
                c = int(name[1:])
                split_after(name, nb)
                if name[0] == "a":
                    hidden_hi(c, name)
            for j in range(4):
                wait_drained(act, f"down2_{j}")
                square(hT, sqz, j)
            norm_sd(7, rn)

        @block.tensor
        def _(pe):
            mm = nc.tensor.matmul
            pe.wait_ge(sem("ld_cst"), 16)

            def exact(out_, left, right, start, stop, **kw):
                (lh, ll), (rh, rl) = left, right
                mm(out_, lh, rh, start=start, stop=False, **kw)
                mm(out_, lh, rl, start=False, stop=False, **kw)
                return mm(out_, ll, rh, start=False, stop=stop, **kw)

            def weights(name, k, nb=None):
                pe.wait_ge(sem("lo_ready"), past_moe(POS[name] + 1, nb))
                s = POS[name] % SPL
                return [w[:, s, :].rearrange("p (k n) -> p k n", k=k) for w in (wh, wl)]

            def turn(name, pieces):
                claim(pe, name)
                for at, src in pieces:
                    ins = pe.transpose(bank(name)[:, at:at + P], src, ident)
                ins.then_inc(filled(name), 1)

            def norm_sum(k, src=sqz):
                claim(pe, f"nsum{k}")
                for j in range(KT):
                    if j % 2 == 0:
                        pe.wait_ge(sem("norm_sq"), 4 * k + j // 2 + 1)
                    ins = mm(bank(f"nsum{k}")[:, 0:T], ones, src[:, T * j:T * j + T], start=(j == 0), stop=(j == KT - 1))
                ins.then_inc(filled(f"nsum{k}"), 1)

            def head_sum(k):
                pe.wait_ge(sem("qk_sq"), k + 1)
                claim(pe, f"qsum{k}")
                mm(bank(f"qsum{k}"), headones, att_pT[:, k % 2, :], start=True, stop=True).then_inc(filled(f"qsum{k}"), 1)

            def by_channels(name, nb=None, stream=None):
                h, l = weights(name, KT, nb)
                claim(pe, name)
                for t in range(2):
                    for k in range(KT):
                        if stream and t == 0:
                            wait_lo(pe, stream, k)
                        c = slice(P * t, P * t + P)
                        ins = exact(bank(name)[:, T * t:T * t + T], (h[:, k, c], l[:, k, c]), (xh[:, k, :], xl[:, k, :]),
                                    k == 0, k == KT - 1)
                ins.then_inc(sem("unit_done"), 1)

            def by_tokens(name, nb=None):
                h, l = weights(name, KT, nb)
                claim(pe, name)
                for t in range(TT):
                    for k in range(KT):
                        c = slice(P * t, P * t + P)
                        ins = exact(bank(name)[:, T * t:T * t + T], (xh[:, k, c], xl[:, k, c]), (h[:, k, :], l[:, k, :]),
                                    k == 0, k == KT - 1)
                ins.then_inc(sem("unit_done"), 1)

            def narrow(name, w, n):
                claim(pe, name)
                for t in range(TT):
                    for k in range(KT):
                        ins = mm(bank(name)[:, n * t:n * t + n], normed[:, k, P * t:P * t + P], w[:, k, :],
                                 start=(k == 0), stop=(k == KT - 1))
                ins.then_inc(filled(name), 1)

            def down(name, acc, c, last, count, nb=None):
                if c == 0:
                    for j in range(4):
                        claim(pe, f"{acc}{j}")
                h, l = weights(name, 2, nb)
                pe.wait_ge(sem("hid_lo"), count)
                a = [t[:, c % 2, :].rearrange("p (k n) -> p k n", k=2) for t in (ah, al)]
                for o in range(KT):
                    for k in range(2):
                        n = slice(P * o, P * o + P)
                        ins = exact(bank(f"{acc}{o // 2}")[:, T * (o % 2):T * (o % 2) + T], (h[:, k, n], l[:, k, n]),
                                    (a[0][:, k, :], a[1][:, k, :]), c == 0 and k == 0 and o % 2 == 0,
                                    c == last and k == 1, skip_group_check=True)
                ins.then_inc(sem("unit_done"), 1)

            norm_sum(0)
            norm_sum(1, x_sq)
            by_channels("mk0", stream="mem0")
            pe.wait_ge(sem("lam_prod"), 2)
            claim(pe, "lam")
            mm(bank("lam")[:, 0:2], ones, lam[:, 0:2], start=True, stop=True).then_inc(filled("lam"), 1)
            by_tokens("mv0")
            head_sum(0)

            pe.wait_ge(sem("ld_cols"), 16)
            wait_raw(pe, "x")
            narrow("foxf", cols[:, V_WF:V_RT].rearrange("p (k n) -> p k n", k=KT), FOX_HEADS)
            by_channels("mq0", stream="x")
            for j in range(6):
                by_channels(UNITS_A[3 + j])
                head_sum(1 + j)
                if j == 0:
                    pe.wait_ge(sem("fox_logf"), 1)
                    claim(pe, "cum")
                    lf = lsf[:, 0, :, :]
                    cum = bank("cum")
                    mm(cum[0:FOX_HEADS, 0:P], lf[:, 0, :], tri, start=True, stop=True)
                    mm(cum[0:FOX_HEADS, P:T], lf[:, 0, :], ones, start=True, stop=False)
                    mm(cum[0:FOX_HEADS, P:T], lf[:, 1, :], tri, start=False, stop=True)
                    mm(cum[:, T:T + FOX_HEADS], tri, lf[:, 0, :], start=True, stop=True)
                    mm(cum[:, T + FOX_HEADS:T + 2 * FOX_HEADS], ones, lf[:, 0, :], start=True, stop=False)
                    mm(cum[:, T + FOX_HEADS:T + 2 * FOX_HEADS], tri, lf[:, 1, :], start=False,
                       stop=True).then_inc(filled("cum"), 1)
            by_tokens("fv0")
            head_sum(7)
            by_tokens("fv1")
            by_tokens("fv2")

            def attention(rng):
                n, a0 = len(rng), rng[0]
                for i in range(n + PV_LAG):
                    if i < n:
                        a = a0 + i
                        m, s = maps[a], bank(f"sc{a}")
                        full = m["kind"] == "mem"
                        claim(pe, f"sc{a}")
                        for t, (at, nk) in enumerate(((0, T), (T, T)) if full else ((0, P), (P, T))):
                            fox = m["kind"] == "fox"
                            ins = mm(s[:, at:at + nk], m["q"][:, P * t:P * t + P], m["k"][:, 0:nk],
                                     start=True, stop=not fox)
                            if fox:
                                ins = mm(s[:, at:at + nk], selh[:, m["head"], :], negc[:, 0:nk],
                                         start=False, stop=True)
                        ins.then_inc(filled(f"sc{a}"), 1)
                    if 0 <= i - T_LAG < n:
                        a = a0 + i - T_LAG
                        pe.wait_ge(sem("att_probs"), 2 * (a + 1))
                        order = (0, 2, 1, 3) if maps[a]["kind"] == "mem" else (0, 1, 2)
                        turn(f"pT{a}", [(P * c, att_p[:, a % 3, P * o:P * o + P]) for c, o in enumerate(order)])
                    if 0 <= i - PV_LAG < n:
                        a = a0 + i - PV_LAG
                        m, g = maps[a], a // 2
                        if a % 2 == 0:
                            claim(pe, f"pv{g}")
                        o = bank(f"pv{g}")[m["row"]:m["row"] + m["m"], :]
                        wait_drained(pe, f"pT{a}")
                        pT = att_pT[:, a % 2, :]
                        second = m["kind"] == "diff" and a % 2 == 1
                        last = m["kind"] != "diff" or a % 2 == 1
                        mm(o[:, 0:T], m["v"][0], pT[:, 0:T], start=not second, stop=False, skip_group_check=True)
                        if m["kind"] == "mem":
                            ins = mm(o[:, 0:T], m["v"][1], pT[:, T:2 * T], start=False, stop=last,
                                     skip_group_check=True)
                        else:
                            ins = mm(o[:, P:T], m["v"][1], pT[:, T:T + P], start=False, stop=last,
                                     skip_group_check=True)
                        ins.then_inc(sem("att_pv"), 1)

            pe.wait_ge(sem("keys_zeroed"), 1)
            for name in ["mk0", "mv0", "mq0"] + UNITS_A[3:12]:
                wait_drained(pe, name)
            pe.wait_ge(sem("negc_ready"), 1)
            pe.wait_ge(sem("selh_ready"), 1)
            attention(fox_maps)

            for g in range(8):
                wait_drained(pe, f"pv{g}")
            for j in range(4):
                by_channels(f"fo{j}")
            norm_sum(2)

            for name in ffn_order(FF0_CH, ("g", "u"), "d"):
                c = int(name[1:])
                if name[0] == "d":
                    down(name, "down0_", c, FF0_CH - 1, c + 1)
                else:
                    by_channels(name, stream="ffn0" if name == "g0" else None)

            by_channels("mk1", stream="mem1")
            by_tokens("mv1")
            head_sum(8)
            norm_sum(3)
            for j in range(6):
                by_channels(f"ci{j}", stream="mix1" if j == 0 else None)
            by_channels("mq1")
            head_sum(9)
            for name in ("mk1", "mv1", "mq1"):
                wait_drained(pe, name)
            attention(mem_maps)
            pe.wait_ge(sem("ccol_ready"), 1)
            claim(pe, "ada")
            for j in range(ADA_UNITS):
                n = NUMBER[f"ada{j}"]
                wait_loaded(pe, n)
                w = raw[:, n % RAW, :].rearrange("p (k n) -> p k n", k=KT)
                for c in range(2):
                    for k in range(KT):
                        ins = mm(bank("ada")[:, 2 * j + c:2 * j + c + 1], w[:, k, P * c:P * c + P], ccol[:, k:k + 1],
                                 start=(k == 0), stop=(k == KT - 1))
                ins.then_inc(sem("unit_done"), 1)

            def channel_sum(name, src):
                claim(pe, name)
                for c in range(CT):
                    ins = mm(bank(name)[:, 0:T], ones, src(c), start=(c == 0), stop=(c == CT - 1))
                ins.then_inc(filled(name), 1)

            pe.wait_ge(sem("conv_done"), CT)
            channel_sum("lnsum", lambda c: cacc[:, c, :])
            pe.wait_ge(sem("ln_sq"), 1)
            channel_sum("lnvar", lambda c: sqz[:, T * c:T * c + T])
            pe.wait_ge(sem("conv_lo"), CT)
            for g in range(mem_maps[0] // 2, mem_maps[0] // 2 + 2):
                wait_drained(pe, f"pv{g}")
            for j in range(4):
                by_channels(f"co{j}")
            norm_sum(4)

            wait_raw(pe, "ffn1")
            narrow("router", cols[:, V_RT:V_END].rearrange("p (k n) -> p k n", k=KT), E)
            for j in range(4):
                t = j // 2
                turn(f"ztok{j}", [(P * c, normed[:, 4 * (j % 2) + c, P * t:P * t + P]) for c in range(4)])
            pe.wait_ge(sem("moe_marks"), 1)
            claim(pe, "mcum")
            b = bank("mcum")
            M = [plan_f[:, 0, E * t:E * t + E] for t in range(TT)]
            mm(b[:, 0:E], tri, M[0], start=True, stop=True)
            mm(b[:, E:2 * E], ones, M[0], start=True, stop=False)
            mm(b[:, E:2 * E], tri, M[1], start=False, stop=True)
            mm(b[:, 2 * E:3 * E], ones, M[0], start=True, stop=False)
            mm(b[:, 2 * E:3 * E], ones, M[1], start=False, stop=True).then_inc(filled("mcum"), 1)

            def as_rows(name, src):
                claim(pe, name)
                for a in range(2):
                    for t in range(TT):
                        ins = mm(bank(name)[:, T * a + P * t:T * a + P * t + P],
                                 src[:, a, t:t + 1].broadcast_to([P, P]), ident, start=True, stop=True)
                ins.then_inc(filled(name), 1)

            pe.wait_ge(sem("moe_keys"), 1)
            as_rows("krow", kcol)
            pe.wait_ge(sem("moe_gates"), 2)
            as_rows("grow", gcol)

            def gather(psum, j):
                for c in range(4):
                    for t in range(TT):
                        ins = mm(psum[:, CAP * c:CAP * c + CAP], z_tok[:, t, P * (4 * j + c):P * (4 * j + c) + P],
                                 sel[:, t, :], start=(t == 0), stop=(t == TT - 1))
                return ins

            for j in range(4):
                wait_drained(pe, f"ztok{j}")
            pe.wait_ge(sem("moe_sel"), TT)
            for j in range(2):
                claim(pe, f"gather{j}")
                gather(bank(f"gather{j}"), j).then_inc(filled(f"gather{j}"), 1)

            def scatter(psum, j):
                for c in range(2):
                    o = 2 * j + c
                    ins = mm(psum[:, T * c:T * c + T], y_tok[:, P * o:P * o + P], scat, start=True, stop=True)
                return ins

            pe.wait_ge(sem("moe_plan"), 2)
            nb = pe.value_load(nbt[0:1, 0:1], min_val=E, max_val=MAXBLK)
            for b in range(8):
                pe.wait_ge(sem(f"drained{b}"), before_moe[b])
            pe.wait_ge(sem("moe_zeroed"), 2)
            with pe.Fori(0, nb) as i:
                def unit(j, k):
                    p = POS0 + j
                    pe.wait_ge(sem("lo_ready"), i * MOE_UNITS + p + 1)
                    return [w[:, p % SPL, :].rearrange("p (k n) -> p k n", k=k) for w in (wh, wl)]

                def spare(use):
                    b, per, at = MOE_BANK[use]
                    pe.wait_ge(sem(f"moe_drained{b}"), i * per + at)
                    return ps[:, b, :], sem(f"moe_filled{b}")

                def spare_drained(use):
                    b, per, at = MOE_BANK[use]
                    pe.wait_ge(sem(f"moe_drained{b}"), i * per + at + 1)

                def turned(c):
                    pe.wait_ge(sem("moe_prod"), i * MOE_CH + c + 1)
                    psum, done = spare(f"T{c}")
                    for f in range(4):
                        ins = pe.transpose(psum[:, P * f:P * f + P], sg[:, c % 2, P * f:P * f + P], ident)
                    ins.then_inc(done, 1)

                def scattered(j):
                    psum, done = spare(f"S{j}")
                    scatter(psum, j).then_inc(done, 1)

                for g, b in ((0, 7), (1, 6)):
                    pe.wait_ge(sem(f"moe_drained{b}"), i * len(MOE_USES[b]))
                for j, (kind, c, half) in enumerate(MOE_ORDER):
                    if kind in "gu":
                        b = 2 * (c % 2) + (kind == "u")
                        w = unit(j, 4)
                        if half == 0:
                            pe.wait_ge(sem("moe_silu" if kind == "g" else "moe_prod"),
                                       i * MOE_CH + max(0, c - 1))
                        for k in range(4):
                            x = [t[:, 4 * half + k, :] for t in (xgh, xgl)]
                            ins = exact(ps[:, b, :], x, (w[0][:, k, :], w[1][:, k, :]), half == 0 and k == 0,
                                        half == 1 and k == 3)
                    else:
                        w = unit(j, 2)
                        if half == 0:
                            spare_drained(f"T{c}")
                            if c == 0:
                                pe.wait_ge(sem("moe_y"), i * 2)
                        for k in range(2):
                            s = slice(P * (2 * half + k), P * (2 * half + k) + P)
                            for o in range(2):
                                n = slice(512 * o, 512 * o + 512)
                                ins = exact(ps[:, 4 + o, :], (ah[:, c % 2, s], al[:, c % 2, s]),
                                            (w[0][:, k, n], w[1][:, k, n]), c == 0 and half == 0 and k == 0,
                                            c == MOE_CH - 1 and half == 1 and k == 1)
                    ins.then_inc(sem("unit_done"), 1)
                    if (kind, half) == ("g", 1) and c >= 1:
                        turned(c - 1)
                    if (kind, half) == ("u", 1) and c <= 1:
                        if c == 0:
                            pe.wait_ge(sem("moe_y"), i * 2)
                            pe.wait_ge(sem("moe_scat"), i)
                        scattered(2 * c)
                        scattered(2 * c + 1)
                    if (kind, c, half) == ("d", MOE_CH - 2, 1):
                        turned(MOE_CH - 1)
                        pe.wait_ge(sem("moe_sel"), i * TT + 2 * TT)
                        for g in range(2):
                            psum, done = spare(f"G{g}")
                            gather(psum, g).then_inc(done, 1)
            pe.wait_ge(sem("moe_y"), nb * 2)
            pe.wait_ge(sem("moe_scat"), nb)
            for b in (6, 7):
                pe.wait_ge(sem(f"moe_drained{b}"), nb * len(MOE_USES[b]))
            for j in range(4):
                claim(pe, f"scat{j}")
                scatter(bank(f"scat{j}"), j).then_inc(filled(f"scat{j}"), 1)

            pe.wait_ge(sem("moe_silu"), nb * MOE_CH)
            pe.wait_ge(sem("moe_prod"), nb * MOE_CH)
            norm_sum(5)
            for j, name in enumerate(WIN):
                if name[1] == "v":
                    by_tokens(name, nb)
                else:
                    by_channels(name, nb, "mix2" if j == 0 else None)
                if 1 <= j <= 4:
                    wait_drained(pe, ROPED[j - 1])
                    claim(pe, f"rot{j - 1}")
                    mm(bank(f"rot{j - 1}"), rot, att_pT[:, (j - 1) % 2, :], start=True,
                       stop=True).then_inc(filled(f"rot{j - 1}"), 1)
            pe.wait_ge(sem("rope_done"), rope_count(4))
            for name in WIN[4:]:
                wait_drained(pe, name)
            attention(diff_maps)

            for i in range(SBH + 2):
                if i < SBH:
                    s, k, q = bank(f"sbs{i}"), kz[:, 8 + i, :], qT[:, 4 + i // 2, :]
                    claim(pe, f"sbs{i}")
                    mm(s[:, 0:T], k[:, 0:P], q, start=True, stop=True)
                    mm(s[:, T:T + P], k[:, P:T], q[:, P:T], start=True, stop=True).then_inc(filled(f"sbs{i}"), 1)
                if 0 <= i - 1 < SBH:
                    j = i - 1
                    x, m = bank(f"sbx{j}"), sb_m[:, j % 2, :]
                    pe.wait_ge(sem("sb_masked"), 2 * (j + 1))
                    claim(pe, f"sbx{j}")
                    mm(x[:, 0:T], sufx, m[:, 0:T], start=True, stop=False, skip_group_check=True)
                    mm(x[:, P:T], ones, m[:, T:T + P], start=False, stop=True, skip_group_check=True)
                    mm(x[:, T:T + P], sufx, m[:, T:T + P], start=True, stop=True,
                       skip_group_check=True).then_inc(filled(f"sbx{j}"), 1)
                if 0 <= i - 2 < SBH:
                    j = i - 2
                    if j % 2 == 0:
                        claim(pe, f"sbo{j // 2}")
                    o = bank(f"sbo{j // 2}")[HD * (j % 2):HD * (j % 2) + HD, :]
                    pe.wait_ge(sem("sb_probs"), 2 * (j + 1))
                    v = [vv[:, t, 512 + HD * j:512 + HD * j + HD] for t in range(TT)]
                    mm(o[:, 0:T], v[0], sb_a[:, j % 2, 0:T], start=True, stop=False, skip_group_check=True)
                    mm(o[:, P:T], v[1], sb_a[:, j % 2, T:T + P], start=False, stop=True,
                       skip_group_check=True).then_inc(sem("sb_pv"), 1)
            for j in range(2):
                pe.wait_ge(sem("sub_sq"), j + 1)
                claim(pe, f"sub{j}")
                mm(bank(f"sub{j}"), ones, att_pT[:, j, :], start=True, stop=True).then_inc(filled(f"sub{j}"), 1)
            pe.wait_ge(sem("sub_lo"), 2)
            for j in range(SBH // 2):
                wait_drained(pe, f"sbo{j}")
            for j in range(4):
                by_channels(f"wo{j}", nb)
            norm_sum(6)
            for name in ffn_order(FF2_CH, ("a",), "b"):
                c = int(name[1:])
                if name[0] == "b":
                    down(name, "down2_", c, FF2_CH - 1, FF0_CH + c + 1, nb)
                else:
                    by_channels(name, nb, "ffn2" if name == "a0" else None)
            norm_sum(7)

        @block.vector
        def _(dve):
            V = nc.vector
            step = [0]

            def link(ins):
                step[0] += 1
                ins.then_inc(sem("dve_step"), 1)
                dve.wait_ge(sem("dve_step"), step[0])

            def stt(out_, in0, scalar, in1, op0, op1):
                return V.scalar_tensor_tensor(out=out_, in0=in0, scalar=scalar, in1=in1, op0=op0, op1=op1)

            def col(at):
                return cols[:, at:at + 1]

            def rest(out_, whole, leading):
                return V.tensor_tensor(out_, whole, leading.bitcast(F32), ALU.subtract)

            def split_lo(p, nb=None):
                n = NUMBER[SPLIT[p]]
                dve.wait_ge(sem("hi_ready"), past_moe(p + 1, nb))
                rest(wl[:, p % SPL, :], raw[:, n % RAW, :], wh[:, p % SPL, :]).then_inc(sem("lo_ready"), 1)

            def split_after(name, nb=None):
                p = POS[name] + SPL
                if p >= len(SPLIT):
                    return
                if nb is None and p >= POS0:
                    dve.wait_ge(sem("hi_ready"), p + 1)
                    rest(wl[:, p % SPL, :], raw[:, (U0 + p - POS0) % RAW, :],
                         wh[:, p % SPL, :]).then_inc(sem("lo_ready"), 1)
                else:
                    split_lo(p, nb)

            def gains(at):
                return cols[:, at:at + KT]

            def norm_rms(k, scale):
                wait_filled(dve, f"nsum{k}")
                V.tensor_scalar(scale[:, :], bank(f"nsum{k}")[:, 0:T], 1.0 / D, EPS, ALU.mult,
                                ALU.add).then_inc(drained(f"nsum{k}"), 1)
                dve.wait_ge(sem("norm_sd"), k + 1)
                link(V.reciprocal(scale[:, :], scale[:, :]))

            def norm_raw(src, gain, scale):
                for k in range(KT):
                    stt(normed[:, k, :], src[:, k, :], gain[:, k:k + 1], scale[:, :], ALU.mult,
                        ALU.mult).then_inc(sem("norm_raw"), 1)

            def norm_lo_shifted(name, at):
                for k in range(KT):
                    wait_hi(dve, name, k)
                    stt(xl[:, k, :], normed[:, k, :], mod[:, at + k:at + k + 1], xh[:, k, :].bitcast(F32), ALU.add,
                        ALU.subtract).then_inc(sem("norm_lo"), 1)

            qk_names = []

            def qk_scale(name, outs):
                k = len(qk_names)
                qk_names.append(name)
                r = att_p[:, k % 2, :]
                wait_filled(dve, f"qsum{k}")
                if k >= 2:
                    wait_drained(dve, qk_names[k - 2])
                V.tensor_scalar(r, bank(f"qsum{k}"), 1.0 / HD, EPS, ALU.mult, ALU.add).then_inc(drained(f"qsum{k}"), 1)
                dve.wait_ge(sem("qk_sd"), k + 1)
                link(V.reciprocal(r, r))
                heads = bank(name).rearrange("p (a b) -> p a b", a=2)
                r2 = r.rearrange("p (a b) -> p a b", a=2)
                for dst, lo, hi, gain in outs:
                    ins = stt(dst, heads[lo:hi, :, :], gain[lo:hi, :], r2[lo:hi, :, :], ALU.mult, ALU.mult)
                ins.then_inc(drained(name), 1)

            def keys(name, keys_, at, gain):
                qk_scale(name, [(keys_[0:HD, at:at + 4:2, :], 0, HD, gain),
                                (keys_[HD:P, at + 1:at + 4:2, :], HD, P, gain)])

            dve.wait_ge(sem("ld_cols"), 16)
            V.tensor_scalar(gq8[:, 0:1], col(V_FGQ), SCALE, None, ALU.mult)
            V.tensor_scalar(gq8[:, 1:3], cols[:, V_GMQ:V_GMQ + 2], SCALE, None, ALU.mult)
            dve.wait_ge(sem("ld_cst"), 16)
            link(V.tensor_tensor(lam[:, 4:5], col(V_LQ), col(V_LK), ALU.mult))
            V.tensor_tensor(lam[:, 0:1], lam[:, 4:5], headones[:, 0:1], ALU.mult).then_inc(sem("lam_prod"), 1)
            V.tensor_tensor(lam[:, 1:2], lam[:, 4:5], headones[:, HD:HD + 1], ALU.mult).then_inc(sem("lam_prod"), 1)

            norm_rms(0, rn_mem)
            norm_raw(mem0, gains(V_MEM), rn_mem)
            norm_rms(1, rn)
            for p in range(SPL):
                split_lo(p)
            wait_lo(dve, "mem0")
            norm_raw(hT, gains(V_MIX), rn)
            split_after("mk0")
            split_after("mv0")
            dve.wait_ge(sem("keys_zeroed"), 1)
            keys("mk0", kz, FOX_HEADS, col(V_GMK))
            wait_filled(dve, "foxf")
            V.tensor_tensor(lsf[:, 0, :, :], bank("foxf")[:, 0:2 * FOX_HEADS].rearrange("p (a b) -> p a b", a=2),
                            cols[:, V_BF:V_BF + FOX_HEADS].unsqueeze(1).broadcast_to([P, TT, FOX_HEADS]),
                            ALU.add).then_inc(drained("foxf"), 1)
            wait_drained(dve, "foxf")
            stt(lsf[:, 1, :, :], lsf[:, 0, :, :], -1.0, lsf[:, 0, :, :], ALU.mult,
                ALU.min).then_inc(sem("fox_negabs"), 1)
            dve.wait_ge(sem("fox_log1p"), 1)
            stt(lsf[:, 0, :, :], lsf[:, 0, :, :], 0.0, lsf[:, 1, :, :], ALU.min,
                ALU.subtract).then_inc(sem("fox_logf"), 1)
            split_after("mq0")
            for j in range(6):
                split_after(UNITS_A[3 + j])
                if j == 0:
                    qk_scale("mq0", [(qT[:, 6:8, :], 0, P, gq8[:, 1:2])])
                    wait_lo(dve, "x")
                    V.tensor_copy(selh, ident[:, 0:FOX_HEADS].unsqueeze(2).broadcast_to([P, FOX_HEADS, P])).then_inc(
                        sem("selh_ready"), 1)
                    wait_filled(dve, "cum")
                    dve.wait_ge(sem("negc_ready"), 1)
                    V.tensor_copy(flat(ctok), bank("cum")[:, T:T + 2 * FOX_HEADS]).then_inc(drained("cum"), 1)
                    wait_drained(dve, "cum")
                elif j < 4:
                    qk_scale(f"fq{j - 1}", [(qT[:, 2 * j - 2:2 * j, :], 0, P, gq8[:, 0:1])])
                else:
                    keys(f"fk{j - 4}", kz, 4 * (j - 4), col(V_FGK))
            split_after("fv0")
            keys("fk2", kz, 8, col(V_FGK))
            split_after("fv1")
            split_after("fv2")

            def attention(rng):
                n, a0 = len(rng), rng[0]
                for i in range(n + PV_LAG + 1):
                    if i < n:
                        a = a0 + i
                        m, s, p = maps[a], bank(f"sc{a}"), att_p[:, a % 3, :]
                        wait_filled(dve, f"sc{a}")
                        if a >= 3:
                            wait_filled(dve, f"pT{a - 3}")
                        if m["kind"] == "fox":
                            h = m["head"]
                            c0, c1 = ctok[:, 0, h:h + 1], ctok[:, 1, h:h + 1]
                            stt(p[:, 0:P], s[:, 0:P], c0, cc(C_FOXM), ALU.add, ALU.add)
                            V.tensor_scalar(p[:, P:2 * P], s[:, P:2 * P], c1, None, ALU.add)
                            stt(p[:, 2 * P:3 * P], s[:, 2 * P:3 * P], c1, cc(C_FOXM), ALU.add,
                                ALU.add).then_inc(drained(f"sc{a}"), 1)
                            w0, w1 = P, 3 * P
                        elif m["kind"] == "diff":
                            V.tensor_tensor(p[:, 0:P], s[:, 0:P], cc(C_DIFM), ALU.add)
                            V.tensor_copy(p[:, P:2 * P], s[:, P:2 * P])
                            V.tensor_tensor(p[:, 2 * P:3 * P], s[:, 2 * P:3 * P], cc(C_DIFM),
                                            ALU.add).then_inc(drained(f"sc{a}"), 1)
                            w0, w1 = P, 3 * P
                        else:
                            V.tensor_copy(p, s).then_inc(drained(f"sc{a}"), 1)
                            w0, w1 = T, 2 * T
                        wait_drained(dve, f"sc{a}")
                        for t, (lo, hi) in enumerate(((0, w0), (w0, w1))):
                            V.tensor_reduce(nmx[:, a % 3, t:t + 1], p[:, lo:hi], AX_X, ALU.max,
                                            negate=True).then_inc(sem("att_max"), 1)
                    if 0 <= i - 1 < n:
                        a = a0 + i - 1
                        dve.wait_ge(sem("att_exp"), 2 * (a + 1))
                        ins = V.reciprocal(rsum[:, a % 3, :], ssum[:, a % 3, :])
                        if maps[a]["kind"] == "diff" and a % 2 == 1:
                            link(ins)
                            ins = V.tensor_scalar(rsum[:, a % 3, :], rsum[:, a % 3, :], lam[:, 6:7], None, ALU.mult)
                        ins.then_inc(sem("att_rsum"), 1)
                    if 0 <= i - PV_LAG - 1 < n and (i - PV_LAG - 1) % 2 == 1:
                        g = (a0 + i - PV_LAG - 1) // 2
                        o, to = bank(f"pv{g}")[:, 0:T], maps[2 * g]["to"]
                        if maps[a0]["kind"] == "diff":
                            dve.wait_ge(sem("att_pv"), 2 * (g + 1))
                            V.tensor_copy(qT[:, to, :], o).then_inc(drained(f"pv{g}"), 1)
                        else:
                            dve.wait_ge(sem("mix_hi"), g + 1)
                            rest(xl[:, to, :], o, xh[:, to, :]).then_inc(drained(f"pv{g}"), 1)

            attention(fox_maps)

            def residual(name, j):
                h2 = pair_of(hT, j)
                V.tensor_tensor(h2, h2, bank(name), ALU.add).then_inc(drained(name), 1)

            for j in range(4):
                wait_done(dve, f"fo{j}")
                residual(f"fo{j}", j)
                split_after(f"fo{j}")
            norm_rms(2, rn)
            norm_raw(hT, gains(V_FFN), rn)
            for name in ffn_order(FF0_CH, ("g", "u"), "d"):
                c = int(name[1:])
                if name[0] == "u":
                    wait_done(dve, name)
                    wait_drained(dve, f"g{c}")
                    V.tensor_tensor(sg[:, c % 2, :], sg[:, c % 2, :], bank(name), ALU.mult).then_inc(drained(name), 1)
                split_after(name)
                if name == "d0":
                    dve.wait_ge(sem("ld_mem1"), 16)
                    wait_lo(dve, "ffn0")
                    norm_raw(mem1, gains(V_MEM + 8), rn_mem)
            for j in range(4):
                wait_done(dve, f"d{FF0_CH - 1}")
                residual(f"down0_{j}", j)
            split_after("mk1")
            split_after("mv1")
            dve.wait_ge(sem("keys1_zeroed"), 1)
            keys("mk1", mkz1, 0, col(V_GMK + 1))
            norm_rms(3, rn)
            norm_raw(hT, gains(V_MIX + 8), rn)

            dve.wait_ge(sem("upad_zeroed"), 1)
            for j in range(6):
                if j >= 3:
                    wait_drained(dve, f"ci{j}")
                    V.tensor_tensor(upad[:, 2 * j - 6:2 * j - 4, PAD:PAD + T], abuf[:, 2 * j - 6:2 * j - 4, :],
                                    cacc[:, 2 * j - 6:2 * j - 4, :], ALU.mult).then_inc(sem("glu"), 1)
                if j < 4:
                    split_after(f"ci{j}")
            qk_scale("mq1", [(q1[:, :, :], 0, P, gq8[:, 2:3])])
            attention(mem_maps)
            dve.wait_ge(sem("glu"), 3)
            for tap in range(TAPS):
                for c in range(CT):
                    if tap:
                        dve.wait_ge(sem("conv_tap"), CT * (tap - 1) + c + 1)
                    w = col(V_TAP + CT * tap + c)
                    u = upad[:, c, tap:tap + T]
                    if tap == 0:
                        ins = V.tensor_scalar(cacc[:, c, :], u, w, col(V_DWB + c), ALU.mult, ALU.add)
                    else:
                        ins = stt(cacc[:, c, :], u, w, cacc[:, c, :], ALU.mult, ALU.add)
                    ins.then_inc(sem("conv_tap") if tap < TAPS - 1 else sem("conv_done"), 1)
            for name in ("ci4", "ci5", "mq1"):
                split_after(name)
            wait_done(dve, f"ada{ADA_UNITS - 1}")
            V.tensor_tensor(mod[:, :], bank("ada")[:, 0:48], cols[:, V_ADA:V_ADA + 48], ALU.add).then_inc(drained("ada"), 1)
            wait_drained(dve, "ada")
            stt(gs[:, 0, :], mod[:, 8:16], 1.0, gains(V_MIX2), ALU.add, ALU.mult)
            stt(gs[:, 1, :], mod[:, 32:40], 1.0, gains(V_FFN2), ALU.add, ALU.mult).then_inc(sem("gs_ready"), 1)
            wait_drained(dve, "lam")
            link(V.tensor_tensor(lam[:, 5:6], lam[:, 3:4], lam[:, 2:3], ALU.subtract))
            link(V.tensor_scalar(lam[:, 6:7], lam[:, 5:6], LAMBDA_INIT, None, ALU.subtract))
            link(V.tensor_scalar(lam[:, 7:8], col(V_SUB), 1.0 - LAMBDA_INIT, None, ALU.mult))
            wait_filled(dve, "lnsum")
            wait_raw(dve, "mix1")
            V.tensor_scalar(rn[:, :], bank("lnsum")[:, 0:T], 1.0 / CONV, None, ALU.mult).then_inc(drained("lnsum"), 1)
            wait_drained(dve, "lnsum")
            rn_all = rn[:, :].unsqueeze(1).broadcast_to([P, CT, T])
            V.tensor_tensor(cacc, cacc, rn_all, ALU.subtract).then_inc(sem("ln_centred"), 1)
            wait_filled(dve, "lnvar")
            dve.wait_ge(sem("ln_centred"), 1)
            V.tensor_scalar(rn[:, :], bank("lnvar")[:, 0:T], 1.0 / CONV, EPS, ALU.mult, ALU.add).then_inc(drained("lnvar"), 1)
            dve.wait_ge(sem("ln_sd"), 1)
            link(V.reciprocal(rn[:, :], rn[:, :]))
            V.tensor_tensor(cacc, cacc, rn_all, ALU.mult).then_inc(sem("ln_scaled"), 1)
            for j in range(4):
                wait_done(dve, f"co{j}")
                residual(f"co{j}", j)
                split_after(f"co{j}")
            norm_rms(4, rn)
            norm_raw(hT, gains(V_FFN + 8), rn)

            ei = cc(C_EI, E)
            wait_filled(dve, "router")
            V.tensor_copy(flat(lg), bank("router")[:, 0:TT * E]).then_inc(drained("router"), 1)
            wait_drained(dve, "router")
            for t in range(TT):
                link(V.max(mx8[:, t, :], lg[:, t, :]))
                link(V.max_index(ix8[:, t, :], mx8[:, t, :], lg[:, t, :]))
            link(V.tensor_copy(ixf[:, :, :], ix8[:, :, 0:2]))
            for a in range(2):
                for t in range(TT):
                    link(V.tensor_scalar(oh[:, a, t, :], ei, ixf[:, t, a:a + 1], None, ALU.is_equal))
            marks = plan_f[:, 0, :]
            V.tensor_tensor(marks, oh[:, 0, :, :].rearrange("p a b -> p (a b)"),
                            oh[:, 1, :, :].rearrange("p a b -> p (a b)"), ALU.add).then_inc(sem("moe_marks"), 1)
            V.tensor_tensor(pexp[:, 0:2].unsqueeze(2), mx8[:, :, 1:2], mx8[:, :, 0:1],
                            ALU.subtract).then_inc(sem("gate_diff"), 1)
            wait_filled(dve, "mcum")
            dve.wait_ge(sem("moe_marks"), 1)
            link(V.tensor_tensor(plan_f[:, 1, :], bank("mcum")[:, 0:2 * E], marks, ALU.subtract))
            pos = plan_f[:, 1, :]
            V.tensor_copy(plan_f[:, 2, 0:E], bank("mcum")[:, 2 * E:3 * E]).then_inc(drained("mcum"), 1)
            wait_drained(dve, "mcum")
            cnt = plan_f[:, 2, 0:E]
            link(V.tensor_scalar(plan_f[:, 3, 0:E], cnt, float(CAP), None, ALU.is_gt))
            link(stt(plan_f[:, 4, 0:E], cnt, float(2 * CAP), plan_f[:, 3, 0:E], ALU.is_gt, ALU.add))
            extra = plan_f[:, 4, 0:E]
            link(V.tensor_tensor(lt8[:, :, :], cc(C_LT, E * E).rearrange("p (a b) -> p a b", a=E),
                                 extra.unsqueeze(1).broadcast_to([P, E, E]), ALU.mult))
            link(V.tensor_reduce(plan_f[:, 5, 0:E], lt8[:, :, :], AX_X, ALU.add))
            before = plan_f[:, 5, 0:E]
            link(stt(plan_f[:, 6, 0:E], before, float(E - 1), ei, ALU.add, ALU.subtract))
            link(V.tensor_scalar(plan_f[:, 7, 0:E], plan_f[:, 6, 0:E], float(CAP), None, ALU.mult))
            link(V.tensor_scalar(plan_f[:, 8, :], pos, float(CAP), None, ALU.is_ge))
            two = lambda r: plan_f[:, r, :].rearrange("p (a b) -> p a b", a=TT)
            link(V.tensor_tensor(two(9), two(8), plan_f[:, 7, 0:E].unsqueeze(1).broadcast_to([P, TT, E]), ALU.mult))
            link(V.tensor_tensor(plan_f[:, 10, :], plan_f[:, 9, :], pos, ALU.add))
            link(V.tensor_scalar(plan_f[:, 11, 0:E], ei, float(CAP), None, ALU.mult))
            link(V.tensor_tensor(two(12), two(10), plan_f[:, 11, 0:E].unsqueeze(1).broadcast_to([P, TT, E]), ALU.add))
            for a in range(2):
                r = plan_f[:, 13 + a, :].rearrange("p (a b) -> p a b", a=TT)
                link(V.tensor_tensor(r, oh[:, a, :, :], two(12), ALU.mult))
                ins = V.tensor_reduce(kcol[:, a, :], r, AX_X, ALU.add)
                if a == 0:
                    link(ins)
            ins.then_inc(sem("moe_keys"), 1)
            link(V.tensor_tensor(plan_f[0:1, 15, 0:E], plan_f[0:1, 5, 0:E], plan_f[0:1, 4, 0:E], ALU.add))
            link(V.tensor_scalar(pexp[0:1, 8:9], plan_f[0:1, 15, E - 1:E], float(E), None, ALU.add))
            link(V.tensor_tensor(lt8[0:1, 0:EXTRA, :], plan_f[0:1, 15, 0:E].unsqueeze(1).broadcast_to([1, EXTRA, E]),
                                 cst[0:1, C_XI:C_XI + EXTRA * E].rearrange("p (a b) -> p a b", a=EXTRA), ALU.is_le))
            link(V.tensor_reduce(pexp[0:1, 16:16 + EXTRA], lt8[0:1, 0:EXTRA, :], AX_X, ALU.add))
            link(V.tensor_scalar(pexp[0:1, 16:16 + EXTRA], pexp[0:1, 16:16 + EXTRA], float(E - 1), None, ALU.min))
            V.tensor_copy(etab[0:1, 0:E], cst[0:1, C_EI:C_EI + E])
            V.tensor_copy(etab[0:1, E:E + EXTRA], pexp[0:1, 16:16 + EXTRA]).then_inc(sem("moe_plan"), 1)
            V.tensor_copy(nbt[0:1, 0:1], pexp[0:1, 8:9])
            V.tensor_scalar(nbt[0:1, 1:2], pexp[0:1, 8:9], -1.0, None, ALU.add).then_inc(sem("moe_plan"), 1)
            dve.wait_ge(sem("gate_exp"), 1)
            link(V.tensor_scalar(pexp[:, 2:4], pexp[:, 0:2], 1.0, None, ALU.add))
            V.reciprocal(gcol[:, 0, :], pexp[:, 2:4]).then_inc(sem("moe_gates"), 1)
            dve.wait_ge(sem("moe_gates"), 1)
            V.tensor_tensor(gcol[:, 1, :], gcol[:, 0, :], pexp[:, 0:2], ALU.mult).then_inc(sem("moe_gates"), 1)
            wait_filled(dve, "krow")
            V.tensor_copy(krow[:, 0:2, :].rearrange("p a b -> p (a b)"), bank("krow")).then_inc(drained("krow"), 1)
            wait_filled(dve, "grow")
            V.tensor_copy(krow[:, 2:4, :].rearrange("p a b -> p (a b)"), bank("grow")).then_inc(drained("grow"), 1)
            wait_drained(dve, "krow")
            wait_drained(dve, "grow")


            iota = cc(C_IOTA, CAP)

            def select(count, first=False):
                if not first:
                    dve.wait_ge(sem("keys_moved"), count)
                for t in range(TT):
                    V.tensor_scalar(sel[:, t, :], iota, kcol[:, 0, t:t + 1], None,
                                    ALU.is_equal).then_inc(sem("sel_half"), 1)
                dve.wait_ge(sem("sel_half"), count * TT + TT)
                for t in range(TT):
                    stt(sel[:, t, :], iota, kcol[:, 1, t:t + 1], sel[:, t, :], ALU.is_equal,
                        ALU.add).then_inc(sem("moe_sel"), 1)
                dve.wait_ge(sem("moe_sel"), count * TT + TT)
                V.tensor_scalar(kcol[:, :, :], kcol[:, :, :], -float(CAP), None, ALU.add).then_inc(sem("keys_moved"), 1)

            select(0, first=True)
            for j in range(2):
                dve.wait_ge(sem("gather_hi"), j + 1)
                rest(four_of(xgl, j), bank(f"gather{j}"), four_of(xgh, j)).then_inc(drained(f"gather{j}"), 1)
            sid = cst[:, C_SID:C_SID + 1]
            dve.wait_ge(sem("moe_zeroed"), 2)
            dve.wait_ge(sem("moe_plan"), 2)
            nb = dve.value_load(nbt[0:1, 0:1], min_val=E, max_val=MAXBLK)
            with dve.Fori(0, nb) as i:
                def split_next(j):
                    n, p = U0 + j + SPL, POS0 + j + SPL
                    dve.wait_ge(sem("hi_ready"), i * MOE_UNITS + p + 1)
                    rest(wl[:, p % SPL, :], raw[:, n % RAW, :], wh[:, p % SPL, :]).then_inc(sem("lo_ready"), 1)

                def turned_lo(c):
                    b = MOE_BANK[f"T{c}"][0]
                    dve.wait_ge(sem("moe_hid_hi"), i * MOE_CH + c + 1)
                    rest(al[:, c % 2, :], ps[:, b, :], ah[:, c % 2, :]).then_inc(sem(f"moe_drained{b}"), 1)

                def add_tokens(s):
                    b, per, use = MOE_BANK[f"S{s}"]
                    dve.wait_ge(sem(f"moe_filled{b}"), i * per + use + 1)
                    h2 = pair_of(hT, s)
                    V.tensor_tensor(h2, h2, ps[:, b, :], ALU.add).then_inc(sem(f"moe_drained{b}"), 1)

                for j, (kind, c, half) in enumerate(MOE_ORDER):
                    if (kind, half) == ("u", 1):
                        dve.wait_ge(sem("unit_done"), i * MOE_UNITS + U0 + j + 1)
                        dve.wait_ge(sem("moe_silu"), i * MOE_CH + c + 1)
                        V.tensor_tensor(sg[:, c % 2, :], sg[:, c % 2, :], ps[:, 2 * (c % 2) + 1, :],
                                        ALU.mult).then_inc(sem("moe_prod"), 1)
                    split_next(j)
                    if (kind, half) == ("g", 1) and c >= 1:
                        turned_lo(c - 1)
                    if (kind, half) == ("u", 1) and c <= 1:
                        add_tokens(2 * c)
                        add_tokens(2 * c + 1)
                    if (kind, c, half) == ("g", 3, 0):
                        select(i + 1)
                    if (kind, c, half) == ("g", 4, 0):
                        stt(scat, krow[:, 0, :], sid, krow[:, 2, :], ALU.is_equal, ALU.mult).then_inc(sem("scat_half"), 1)
                        stt(scat_b, krow[:, 1, :], sid, krow[:, 3, :], ALU.is_equal,
                            ALU.mult).then_inc(sem("scat_half"), 1)
                        dve.wait_ge(sem("scat_half"), i * 3 + 2)
                        V.tensor_scalar(krow[:, 0:2, :], krow[:, 0:2, :], -float(CAP), None,
                                        ALU.add).then_inc(sem("scat_half"), 1)
                        dve.wait_ge(sem("scat_half"), i * 3 + 3)
                        V.tensor_tensor(scat, scat, scat_b, ALU.add).then_inc(sem("moe_scat"), 1)
                    if (kind, c, half) == ("d", MOE_CH - 2, 1):
                        turned_lo(MOE_CH - 1)
                        for g in range(2):
                            b = MOE_BANK[f"G{g}"][0]
                            dve.wait_ge(sem("gather_hi"), i * 2 + 2 + g + 1)
                            rest(four_of(xgl, g), ps[:, b, :], four_of(xgh, g)).then_inc(sem(f"moe_drained{b}"), 1)
            for j in range(4):
                wait_filled(dve, f"scat{j}")
                residual(f"scat{j}", j)

            wait_raw(dve, "ffn1")
            norm_rms(5, rn)
            norm_raw(hT, gs[:, 0, :], rn)
            norm_lo_shifted("mix2", 0)
            cos2 = cc(C_COS, T).unsqueeze(1).broadcast_to([P, 2, T])
            sin2 = cc(C_SIN, T).unsqueeze(1).broadcast_to([P, 2, T])
            t1 = att_p[:, 0, :].rearrange("p (a b) -> p a b", a=2)
            t2 = att_p[:, 1, :].rearrange("p (a b) -> p a b", a=2)
            dve.wait_ge(sem("keys_zeroed"), 2)

            def rope(j):
                scale = SCALE if j < 2 else 1.0
                wait_drained(dve, ROPED[j])
                plain = att_pT[:, j % 2, :].rearrange("p (a b) -> p a b", a=2)
                if j:
                    dve.wait_ge(sem("rope_done"), rope_count(j))
                link(stt(t1, plain, scale, cos2, ALU.mult, ALU.mult))
                wait_filled(dve, f"rot{j}")
                stt(t2, bank(f"rot{j}").rearrange("p (a b) -> p a b", a=2), scale, sin2, ALU.mult,
                    ALU.mult).then_inc(drained(f"rot{j}"), 1)
                wait_drained(dve, f"rot{j}")
                if j < 2:
                    V.tensor_tensor(qT[:, 2 * j:2 * j + 2, :], t1, t2, ALU.add).then_inc(sem("rope_done"), 1)
                else:
                    at = 4 * (j - 2)
                    V.tensor_tensor(kz[0:HD, at:at + 4:2, :], t1[0:HD, :, :], t2[0:HD, :, :],
                                    ALU.add).then_inc(sem("rope_done"), 1)
                    V.tensor_tensor(kz[HD:P, at + 1:at + 4:2, :], t1[HD:P, :, :], t2[HD:P, :, :],
                                    ALU.add).then_inc(sem("rope_done"), 1)

            for j, name in enumerate(WIN):
                split_after(name, nb)
                if 1 <= j <= 4:
                    rope(j - 1)
            attention(diff_maps)

            wait_filled(dve, f"pT{len(maps) - 1}")
            for i in range(SBH + 2):
                if i < SBH:
                    b, s = i % 2, bank(f"sbs{i}")[:, 0:384]
                    dve.wait_ge(sem("sb_log1p"), i + 1)
                    if i >= 2:
                        wait_filled(dve, f"sbx{i - 2}")
                    stt(sb_m[:, b, :], s, 0.0, sb_l[:, b, :], ALU.max, ALU.add).then_inc(sem("sb_m"), 1)
                    if i >= 2:
                        dve.wait_ge(sem("sb_exp"), i - 1)
                    stt(sb_b[:, b, :], s, 0.0, sb_l[:, b, :], ALU.min, ALU.subtract).then_inc(drained(f"sbs{i}"), 1)
                if 0 <= i - 1 < SBH:
                    j = i - 1
                    wait_filled(dve, f"sbx{j}")
                    wait_drained(dve, f"sbs{j}")
                    V.tensor_tensor(sb_b[:, j % 2, :], sb_b[:, j % 2, :], bank(f"sbx{j}")[:, 0:384],
                                    ALU.subtract).then_inc(drained(f"sbx{j}"), 1)
                if 0 <= i - 2 < SBH and i % 2 == 1:
                    g = (i - 2) // 2
                    dve.wait_ge(sem("sb_hi"), g + 1)
                    rest(xl[:, 4 + g, :], bank(f"sbo{g}")[:, 0:T], xh[:, 4 + g, :]).then_inc(drained(f"sbo{g}"), 1)
            for j in range(2):
                wait_filled(dve, f"sub{j}")
                V.tensor_scalar(att_p[:, j, :], bank(f"sub{j}"), 1.0 / P, EPS, ALU.mult,
                                ALU.add).then_inc(drained(f"sub{j}"), 1)
            for j in range(2):
                dve.wait_ge(sem("sub_sd"), j + 1)
                link(V.reciprocal(att_p[:, j, :], att_p[:, j, :]))
                o2 = pair_of(qT, j)
                stt(o2, o2, lam[:, 7:8], att_p[:, j, :], ALU.mult, ALU.mult).then_inc(sem("sub_out"), 1)
            for j in range(2):
                dve.wait_ge(sem("sub_hi"), j + 1)
                rest(pair_of(xl, j), pair_of(qT, j), pair_of(xh, j)).then_inc(sem("sub_lo"), 1)

            def gated_residual(name, j, at):
                for t in range(2):
                    o = 2 * j + t
                    ins = stt(hT[:, o, :], bank(name)[:, T * t:T * t + T], mod[:, at + o:at + o + 1], hT[:, o, :],
                              ALU.mult, ALU.add)
                ins.then_inc(drained(name), 1)

            for j in range(4):
                wait_done(dve, f"wo{j}", nb)
                gated_residual(f"wo{j}", j, 16)
                split_after(f"wo{j}", nb)
            wait_raw(dve, "mix2")
            norm_rms(6, rn)
            norm_raw(hT, gs[:, 1, :], rn)
            norm_lo_shifted("ffn2", 24)
            for name in ffn_order(FF2_CH, ("a",), "b"):
                c = int(name[1:])
                if name[0] == "a":
                    wait_done(dve, name, nb)
                    if c >= 2:
                        dve.wait_ge(sem("hid_lo"), FF0_CH + c - 1)
                    link(V.tensor_scalar(sg[:, c % 2, :], bank(name), 0.0, None, ALU.max))
                    V.tensor_tensor(sg[:, c % 2, :], sg[:, c % 2, :], bank(name), ALU.mult).then_inc(drained(name), 1)
                split_after(name, nb)
            for j in range(4):
                wait_done(dve, f"b{FF2_CH - 1}", nb)
                gated_residual(f"down2_{j}", j, 40)
            wait_raw(dve, "ffn2")
            norm_rms(7, rn)
            norm_raw(hT, gains(V_FIN2), rn)


def rope_count(j):
    return min(j, 2) + 2 * max(0, j - 2)


def units_by_columns(w):
    return w.reshape(KT, P, -1, T).transpose(2, 1, 0, 3).reshape(-1, P, UW)


def units_by_rows(w):
    return w.reshape(-1, 2, P, D).transpose(0, 2, 1, 3).reshape(-1, P, UW)


def main_units(A):
    fox, kv, win = A["fox_w_in"][0], A["w_mem_kv"], A["w_in_2"][0]
    by_name = {}

    def put(prefixes, units):
        per = len(units) // len(prefixes)
        for p, prefix in enumerate(prefixes):
            for j in range(per):
                by_name[f"{prefix}{j}"] = units[p * per + j]

    for layer in range(2):
        by_name[f"mk{layer}"], by_name[f"mv{layer}"] = units_by_columns(kv[layer])
    by_name["mq0"], = units_by_columns(fox[:, 3 * FOX + FOX_HEADS:])
    put(("fq", "fk", "fv"), units_by_columns(fox[:, :3 * FOX]))
    put(("fo",), units_by_columns(A["fox_w_out"][0]))
    put(("g",), units_by_columns(A["ffn_w_gate"][0]))
    put(("u",), units_by_columns(A["ffn_w_up"][0]))
    put(("d",), units_by_rows(A["ffn_w_down"][0]))
    put(("ci",), units_by_columns(A["conv_w_in"][0][:, :2 * CONV]))
    by_name["mq1"], = units_by_columns(A["conv_w_in"][0][:, 2 * CONV:])
    put(("ada",), units_by_columns(A["ada_w_2"][0]))
    put(("co",), units_by_columns(A["conv_w_out"][0]))
    put(("dq", "dk", "dv", "sq", "sk", "sv"), units_by_columns(win))
    put(("wo",), units_by_columns(A["w_out_2"][0]))
    put(("a",), units_by_columns(A["w_ff1_2"][0]))
    put(("b",), units_by_rows(A["w_ff2_2"][0]))
    return np.stack([by_name[name] for name in UNITS])


def moe_units(A):
    out = np.empty((E, MOE_UNITS, P, UW), np.float32)
    up = {"g": A["moe_w_gate"][0], "u": A["moe_w_up"][0]}
    for j, (kind, c, half) in enumerate(MOE_ORDER):
        if kind == "d":
            w = A["moe_w_down"][0].reshape(E, MOE_CH, 2, 2, P, D)[:, c, half]
        else:
            w = up[kind].reshape(E, 2, 4, P, MOE_CH, 512)[:, half, :, :, c]
        out[:, j] = w.transpose(0, 2, 1, 3).reshape(E, P, UW)
    return out


def vector_columns(A):
    c = np.empty((P, V_END), np.float32)

    def put(at, v):
        v = v.reshape(-1, P).T
        c[:, at:at + v.shape[1]] = v

    def twin(at, first, second):
        put(at, np.concatenate([first.reshape(-1, HD), second.reshape(-1, HD)], 1))

    for at, name in ((V_MIX, "norm_mix"), (V_MEM, "norm_mem"), (V_FFN, "norm_ffn"), (V_CB, "conv_b_in"),
                     (V_DWB, "conv_dw_b"), (V_LNG, "conv_ln_g"), (V_LNB, "conv_ln_b"), (V_MIX2, "mix_norm_g_2"),
                     (V_FFN2, "ffn_norm_g_2"), (V_FIN2, "final_norm_g_2"), (V_C, "c_2"), (V_SUB, "diff_subln_g_2"),
                     (V_ADA, "ada_b_2"), (V_TAP, "conv_dw")):
        put(at, A[name])
    for at, name in ((V_FGQ, "fox_g_q"), (V_FGK, "fox_g_k"), (V_GMQ, "g_mq"), (V_GMK, "g_mk")):
        twin(at, A[name], A[name])
    twin(V_LQ, A["lambda_q1_2"], A["lambda_q2_2"])
    twin(V_LK, A["lambda_k1_2"], A["lambda_k2_2"])
    c[:, V_BF:V_WF] = A["fox_b_f"]
    c[:, V_WF:V_RT] = by_partition(A["fox_w_in"][0][:, 3 * FOX:3 * FOX + FOX_HEADS])
    c[:, V_RT:V_END] = by_partition(A["moe_router"][0])
    return c


def by_partition(w):
    return w.reshape(KT, P, -1).transpose(1, 0, 2).reshape(P, -1)


def kernel(**inputs):
    import concourse.bacc as bacc
    from concourse.bass_utils import run_bass_kernel_spmd

    A = {name: np.asarray(a) for name, a in inputs.items()}
    arrays = {
        "in_x": by_partition(A["x"][0].T), "in_mem": by_partition(A["mem"][0].T), "in_constants": constants(),
        "in_columns": vector_columns(A), "in_units": main_units(A), "in_experts": moe_units(A)}
    nc = bacc.Bacc("TRN2", target_bir_lowering=False, num_devices=1)
    drams = []
    for name, a in arrays.items():
        arrays[name] = np.ascontiguousarray(a)
        drams.append(nc.dram_tensor(name, a.shape, F32, kind="ExternalInput").ap())
    out = nc.dram_tensor("out_0", (P, KT * T), F32, kind="ExternalOutput").ap()
    build(nc, *drams, out)
    r = run_bass_kernel_spmd(nc, [arrays], core_ids=[0])
    res = r.results[0]["out_0"].reshape(P, KT, T).transpose(2, 1, 0)
    return np.ascontiguousarray(res.reshape(1, T, D))
```

```python
from contextlib import ExitStack

import numpy as np

import concourse.bass as bass
from concourse import mybir

F32 = mybir.dt.float32
F32R = mybir.dt.float32r
I32 = mybir.dt.int32
U32 = mybir.dt.uint32
ALU = mybir.AluOpType
ACT = mybir.ActivationFunctionType
AX_X = mybir.AxisListType.X

P = 128
D = 1024
KT = D // P
T = 256
TT = T // P
HD = 64
FOX_HEADS = 12
MEM_HEADS = 4
FOX = FOX_HEADS * HD
MEM = MEM_HEADS * HD
CONV = 768
CT = CONV // P
TAPS = 31
PAD = TAPS - 1
CT_PE = 3
PE_TAPS = TAPS * CT_PE
DVE_TAPS = TAPS * (CT - CT_PE)
DIAG_RING = 8
FF0 = 2816
E = 8
EFF = 3584
EFT = EFF // P
CAP = 128
EXTRA = 3
MAXBLK = E + EXTRA
FF2 = 4096
EPS = 1e-6
NEG = -1e30
SCALE = HD ** -0.5
LAMBDA_INIT = 0.2
UW = 2048
RAW = 6
SPL = 3

C_ID, C_HEAD, C_ONES = 0, P, 2 * P
C_EPS = 3 * P
C_ROT = C_EPS + 1
C_SUF = C_ROT + P
C_TRI = C_SUF + P
C_COS = C_TRI + P
C_SIN = C_COS + T
C_FOXM = C_SIN + T
C_DIFM = C_FOXM + P
C_SBM = C_DIFM + P
C_IOTA = C_SBM + P
C_SID = C_IOTA + CAP
C_EI = C_SID + 1
C_LT = C_EI + E
C_XI = C_LT + E * E
C_END = C_XI + EXTRA * E


def constants():
    c = np.zeros((P, C_END), np.float32)
    r = np.arange(P)
    c[:, C_ID:C_ID + P] = np.eye(P)
    c[:, C_HEAD:C_HEAD + P] = r[:, None] // HD == r[None, :] // HD
    c[:, C_ONES:C_ONES + P] = 1.0
    c[:, C_EPS] = EPS
    for d in range(P):
        if d % HD < HD // 2:
            c[d + HD // 2, C_ROT + d] = -1.0
        else:
            c[d - HD // 2, C_ROT + d] = 1.0
    c[:, C_SUF:C_SUF + P] = r[:, None] > r[None, :]
    c[:, C_TRI:C_TRI + P] = r[:, None] <= r[None, :]
    inv = (np.float32(1.0) / (np.float32(10000.0) ** (np.arange(0, HD, 2, dtype=np.float32) / np.float32(HD))))
    ang = np.arange(T, dtype=np.float32)[:, None] * inv[None, :].astype(np.float32)
    ang = np.concatenate([ang, ang], -1).T
    c[:, C_COS:C_COS + T] = np.tile(np.cos(ang), (2, 1))
    c[:, C_SIN:C_SIN + T] = np.tile(np.sin(ang), (2, 1))
    c[:, C_FOXM:C_FOXM + P] = np.where(r[None, :] <= r[:, None], 0.0, NEG)
    c[:, C_DIFM:C_DIFM + P] = np.where(r[None, :] // 64 <= r[:, None] // 64, 0.0, NEG)
    c[:, C_SBM:C_SBM + P] = r[None, :] > r[:, None]
    c[:, C_IOTA:C_IOTA + CAP] = np.arange(CAP)[None, :]
    c[:, C_SID] = r
    c[:, C_EI:C_EI + E] = np.arange(E)[None, :]
    e = np.arange(E)
    c[:, C_LT:C_LT + E * E] = (e[None, :] < e[:, None]).reshape(1, -1)
    c[:, C_XI:C_XI + EXTRA * E] = np.repeat(np.arange(EXTRA), E)[None, :]
    return c


V_MIX, V_MEM, V_FFN = 0, 16, 32
V_CB, V_DWB, V_LNG, V_LNB = 48, 60, 66, 72
V_MIX2, V_FFN2, V_FIN2 = 78, 86, 94
V_SUB, V_FGQ, V_FGK, V_GMQ, V_GMK, V_LQ, V_LK = 102, 103, 104, 105, 107, 109, 110
V_ADA = 111
V_TAP = V_ADA + 48
V_BF = V_TAP + TAPS * CT
V_WF = V_BF + FOX_HEADS
V_RT = V_WF + KT * FOX_HEADS
V_END = V_RT + KT * E

FF0_CH = FF0 // T
FF2_CH = FF2 // T
MOE_CH = EFF // 512
ADA_UNITS = 6 * D // T


def ffn_order(n, ins, out):
    order = []
    for c in range(n):
        order += [f"{name}{c}" for name in ins]
        if c:
            order.append(f"{out}{c - 1}")
    return order + [f"{out}{n - 1}"]


def with_modulation(order):
    out, n = [], 0
    for name in order:
        out.append(name)
        if name[0] == "d" and n < ADA_UNITS:
            per = 3 if int(name[1:]) % 3 == 0 else 2
            out += [f"ada{j}" for j in range(n, n + per)]
            n += per
    assert n == ADA_UNITS
    return out


FF0_ORDER = with_modulation(ffn_order(FF0_CH, ("g", "u"), "d"))
UNITS_A = (["mk0", "mv0", "mq0"] + [f"{w}{j}" for w in ("fq", "fk", "fv") for j in range(3)]
           + [f"fo{j}" for j in range(4)] + FF0_ORDER + ["mk1", "mv1", "mq1"] + [f"ci{j}" for j in range(6)]
           + [f"co{j}" for j in range(4)])
UNITS_B = ([f"{w}{j}" for w in ("dq", "dk", "dv", "sq", "sk", "sv") for j in range(2)] + [f"wo{j}" for j in range(4)]
           + ffn_order(FF2_CH, ("a",), "b"))
UNITS = UNITS_A + UNITS_B
NUMBER = {name: n for n, name in enumerate(UNITS)}
SPLIT = [name for name in UNITS if not name.startswith("ada")]
POS = {name: p for p, name in enumerate(SPLIT)}
QK_UNITS = ["mk0", "mq0", "fq0", "fq1", "fq2", "fk0", "fk1", "fk2", "mk1", "mq1"]
U0 = len(UNITS_A)
POS0 = len([name for name in UNITS_A if name in POS])

MOE_ORDER = [(name[0], int(name[1:]), half) for name in ffn_order(MOE_CH, ("g", "u"), "d") for half in range(2)]
MOE_UNITS = len(MOE_ORDER)
assert MOE_UNITS % RAW == 0 and MOE_UNITS % SPL == 0
MOE_USES = {6: ["T0", "S2", "T2", "T4", "T6", "G1"], 7: ["S0", "S1", "T1", "S3", "T3", "T5", "G0"]}
MOE_BANK = {use: (b, len(uses), j) for b, uses in MOE_USES.items() for j, use in enumerate(uses)}


class Sessions:

    def __init__(self):
        self.fills, self.drains, self.at = [0] * 8, [0] * 8, {}

    def add(self, name, bank, own_signal=False, own_drain=False):
        assert name not in self.at, name
        self.at[name] = (bank, self.fills[bank] + 1, self.drains[bank])
        if not own_drain:
            self.drains[bank] += 1
        if not own_signal:
            self.fills[bank] += 1


def build(nc, x_dram, mem_dram, c_dram, cst_dram, cols_dram, main_dram, moe_dram, out):
    ctx = ExitStack()
    with ctx:
        def sb(name, shape, dt=F32):
            return ctx.enter_context(nc.sbuf_tensor(name, shape, dt))

        sems = {}

        def sem(name):
            if name not in sems:
                sems[name] = ctx.enter_context(nc.semaphore(name))
            return sems[name]

        raw = sb("raw", [P, RAW, UW])
        wh = sb("wh", [P, SPL, UW], F32R)
        wl = sb("wl", [P, SPL, UW], F32R)
        xh = sb("xh", [P, KT, T], F32R)
        xl = sb("xl", [P, KT, T], F32R)
        ah = sb("ah", [P, 2, 512], F32R)
        al = sb("al", [P, 2, 512], F32R)
        hT = sb("hT", [P, KT, T])
        big = sb("big", [P, 8192])
        sqz = sb("sqz", [P, 2048])
        cst = sb("cst", [P, C_END])
        cols = sb("cols", [P, V_END])
        att_p = sb("att_p", [P, 3, 512])
        att_pT = sb("att_pT", [P, 2, 512])
        rn = sb("rn", [P, T])
        rn_mem = sb("rn_mem", [P, T])
        lsf = sb("lsf", [P, 2, TT, FOX_HEADS])
        ctok = sb("ctok", [P, TT, FOX_HEADS])
        nmx = sb("nmx", [P, 3, TT])
        ssum = sb("ssum", [P, 3, TT])
        rsum = sb("rsum", [P, 3, TT])
        gq8 = sb("gq8", [P, 3])
        mod = sb("mod", [P, 48])
        gs = sb("gs", [P, 2, KT])
        lam = sb("lam", [P, 8])
        mx8 = sb("mx8", [P, TT, 8])
        ix8 = sb("ix8", [P, TT, 8], U32)
        lg = sb("lg", [P, TT, E])
        ixf = sb("ixf", [P, TT, 2])
        oh = sb("oh", [P, 2, TT, E])
        plan_f = sb("plan_f", [P, 16, 16])
        lt8 = sb("lt8", [P, E, E])
        kcol = sb("kcol", [P, 2, TT])
        gcol = sb("gcol", [P, 2, TT])
        pexp = sb("pexp", [P, 32])
        etab = sb("etab", [1, 16], I32)
        nbt = sb("nbt", [1, 2], I32)
        warm_out = sb("warm_out", [P, 12])

        def cc(at, n=P):
            return cst[:, at:at + n]

        ident, headones, ones, rot = cc(C_ID), cc(C_HEAD), cc(C_ONES), cc(C_ROT)
        sufx, tri, eps = cc(C_SUF), cc(C_TRI), cc(C_EPS, 1)

        def flat(t):
            return t[:, :, :].rearrange("p a b -> p (a b)")

        def view(at, a, b, base=None):
            return (big if base is None else base)[:, at:at + a * b].rearrange("p (a b) -> p a b", a=a)

        qT = view(0, 8, T)
        kz = view(2048, 16, T)
        vv = view(6144, TT, 1024)
        mem0 = view(0, KT, T)
        x_sq = big[:, 6144:8192]
        upad = view(0, CT, PAD + T)
        cacc = view(1792, CT, T)
        abuf = view(3328, CT, T)
        mem1 = view(3328, KT, T)
        q1 = view(4864, 2, T)
        mkz1 = view(5376, MEM_HEADS, T)
        mv1 = view(6400, TT, MEM)
        c_row = big[:, 6400:6400 + D]
        diag = view(6912, DIAG_RING, P)
        z_tok = view(0, TT, D)
        y_tok = big[:, 2048:3072]
        krow = view(4096, 4, T)
        sel = view(5120, TT, CAP)
        scat = big[:, 5376:5376 + T]
        scat_b = big[:, 5632:5632 + T]
        sb_l = view(2048, 4, 3 * P)
        normed = view(0, KT, T, sqz)
        selh = sqz[:, 0:FOX_HEADS * P].rearrange("p (h m) -> p h m", h=FOX_HEADS)
        negc = sqz[:, FOX_HEADS * P:FOX_HEADS * P + T]
        xgh = flat(xh)[:, 0:KT * CAP].rearrange("p (a b) -> p a b", a=KT)
        xgl = flat(xl)[:, 0:KT * CAP].rearrange("p (a b) -> p a b", a=KT)
        sg = att_p
        sb_b = view(0, 4, 3 * P, sqz)
        sub_r = att_pT
        att_flat = flat(att_p)
        sb_m = att_flat[:, 0:768].rearrange("p (a b) -> p a b", a=2)
        sb_a = att_flat[:, 768:1536].rearrange("p (a b) -> p a b", a=2)

        def pair_of(t, j):
            return t[:, 2 * j:2 * j + 2, :].rearrange("p a b -> p (a b)")

        def four_of(t, j):
            return t[:, 4 * j:4 * j + 4, :].rearrange("p a b -> p (a b)")

        ps = ctx.enter_context(nc.psum_tensor("ps", [P, 8, 512], F32))

        S = Sessions()

        def product(name, b):
            S.add(name, b, own_signal=True)

        S.add("nsum0", 6)
        product("mk0", 0)
        S.add("nsum1", 7)
        S.add("lam", 5)
        product("mv0", 1)
        S.add("qsum0", 4)
        S.add("foxf", 2)
        product("mq0", 3)
        product("fq0", 7)
        S.add("qsum1", 5)
        S.add("cum", 6)
        for j in range(1, 6):
            product(f"{'fq' if j < 3 else 'fk'}{j % 3}", j % 4)
            S.add(f"qsum{1 + j}", 4 + (1 + j) % 2)
        product("fv0", 7)
        S.add("qsum7", 5)
        product("fv1", 6)
        product("fv2", 2)

        maps = []

        def add_maps(kinds):
            first = len(maps)
            maps.extend(kinds)
            return range(first, len(maps))

        fox_maps = add_maps([
            dict(kind="fox" if h < FOX_HEADS else "mem", head=h, q=qT[:, h // 2, :], k=kz[:, h, :],
                 v=[vv[:, t, HD * h:HD * h + HD] for t in range(TT)], row=HD * (h % 2), m=HD, to=h // 2)
            for h in range(FOX_HEADS + MEM_HEADS)])
        mem_maps = add_maps([
            dict(kind="mem", head=h, q=q1[:, h // 2, :], k=mkz1[:, h, :],
                 v=[mv1[:, t, HD * h:HD * h + HD] for t in range(TT)], row=HD * (h % 2), m=HD, to=CT + h // 2)
            for h in range(MEM_HEADS)])
        diff_maps = add_maps([
            dict(kind="diff", head=m, q=qT[:, m // 2, :], k=kz[:, m, :],
                 v=[vv[:, t, P * (m // 2):P * (m // 2) + P] for t in range(TT)], row=0, m=P, to=m // 2)
            for m in range(8)])

        T_LAG, PV_LAG = 3, 4
        MEM_STEPS = MEM_HEADS + PV_LAG
        FOX_SPLITS = {16: ("fv0",), 20: ("fv1", "fv2")}
        MEM_SPLITS = {4: "ci3", 5: "ci4", 6: "ci5"}
        DIFF_SPLITS = {9: "sv0", 10: "sv1"}

        def add_attention(rng):
            n, a0 = len(rng), rng[0]
            for i in range(n + PV_LAG):
                if i < n:
                    S.add(f"sc{a0 + i}", (a0 + i) % 2)
                if 0 <= i - T_LAG < n:
                    S.add(f"pT{a0 + i - T_LAG}", 2 + (a0 + i) % 2)
                if 0 <= i - PV_LAG < n and (i - PV_LAG) % 2 == 0:
                    g = (a0 + i - PV_LAG) // 2
                    S.add(f"pv{g}", 4 + g % 2, own_signal=True)

        add_attention(fox_maps)
        for j in range(4):
            product(f"fo{j}", j)
        S.add("nsum2", 6)
        for c in range(FF0_CH):
            product(f"g{c}", 2 * c % 3)
            product(f"u{c}", (2 * c + 1) % 3)
        for j in range(4):
            product(f"down0_{j}", 4 + j)
        product("mk1", 1)
        S.add("nsum3", 4)
        product("mv1", 2)
        S.add("qsum8", 0)
        product("mq1", 3)
        for j in range(6):
            product(f"ci{j}", 5 + j % 3)
            if j == 0:
                S.add("qsum9", 4)
        for c in range(CT_PE):
            product(f"conv{c}", 6 + c % 2)
        add_attention(mem_maps)
        S.add("lnsum", 0)
        S.add("lnvar", 1)
        for j in range(4):
            product(f"co{j}", j)
        S.add("nsum4", 4)
        S.add("router", 5)
        for j in range(4):
            S.add(f"ztok{j}", j)
        S.add("mcum", 5)
        S.add("krow", 4)
        for j in range(2):
            S.add(f"gather{j}", MOE_BANK[f"G{j}"][0], own_drain=True)
        S.add("grow", 5)
        before_moe = list(S.drains)
        for j in range(4):
            S.add(f"scat{j}", 4 + j)
        S.add("nsum5", 0)
        ROPED = ("dq0", "dq1", "dk0", "dk1")
        WIN = UNITS_B[:12]
        for j, name in enumerate(WIN):
            product(name, (1 + j) % 4)
            if 1 <= j <= 4:
                S.add(f"rot{j - 1}", 4 + (j - 1) % 2)
        add_attention(diff_maps)
        SBH = 8
        DIFF_PAIRS = len(diff_maps) // 2
        SB_PAIRS = SBH // 2
        SB_BANKS = (0, 1, 6, 7)

        def pair(g):
            return (2 * g, 2 * g + 1) if 0 <= g < SB_PAIRS else ()

        for i in (*pair(0), *pair(1)):
            S.add(f"sbs{i}", SB_BANKS[i % 4])
        for j in range(2):
            S.add(f"sub{j}", 4 + j)
        for g in range(SB_PAIRS + 1):
            for i in pair(g):
                S.add(f"sbx{i}", 2 + i % 2)
            for i in pair(g + 2):
                S.add(f"sbs{i}", SB_BANKS[i % 4])
            if g >= 1:
                S.add(f"sbo{g - 1}", 4 + (g - 1) % 2, own_signal=True)
        for j in range(4):
            product(f"wo{j}", j)
        S.add("nsum6", 4)
        for c in range(FF2_CH):
            product(f"a{c}", c % 4)
        for j in range(4):
            product(f"down2_{j}", 4 + j)
        S.add("nsum7", 0)

        def bank(name):
            return ps[:, S.at[name][0], :]

        def claim(pe, name):
            b, _, k = S.at[name]
            if k:
                pe.wait_ge(sem(f"drained{b}"), k)

        def wait_filled(eng, name):
            b, k, _ = S.at[name]
            eng.wait_ge(sem(f"filled{b}"), k)

        def wait_drained(eng, name):
            b, _, k = S.at[name]
            eng.wait_ge(sem(f"drained{b}"), k + 1)

        def filled(name):
            return sem(f"filled{S.at[name][0]}")

        def drained(name):
            return sem(f"drained{S.at[name][0]}")

        def past_moe(count, nb):
            return count if nb is None else nb * MOE_UNITS + count

        def wait_done(eng, name, nb=None):
            eng.wait_ge(sem("unit_done"), past_moe(POS[name] + 1, nb))

        def wait_loaded(eng, n, nb=None):
            turns = 16 * (n // RAW + 1)
            eng.wait_ge(sem(f"ring_loaded{n % RAW}"), turns if nb is None else nb * (16 * MOE_UNITS // RAW) + turns)

        RAW_STREAM = {name: r for r, name in enumerate(
            ("mem0", "x", "ffn0", "mem1", "mix1", "ffn1", "mix2", "ffn2", "final"))}
        SPLIT_STREAM = {name: s for s, name in enumerate(("mem0", "x", "ffn0", "mem1", "mix1", "mix2", "ffn2"))}

        def wait_raw(eng, name, k=KT - 1):
            eng.wait_ge(sem("norm_raw"), KT * RAW_STREAM[name] + k + 1)

        def wait_hi(eng, name, k=KT - 1):
            eng.wait_ge(sem("norm_hi"), KT * SPLIT_STREAM[name] + k + 1)

        POOL_TILES = {"mem0": 5, "x": 5, "ffn0": 5, "mem1": KT, "mix1": 5, "mix2": 0, "ffn2": 0}

        def wait_lo(eng, name, k=None):
            before = list(POOL_TILES)[:SPLIT_STREAM[name]]
            by_pool, mine = sum(POOL_TILES[b] for b in before), POOL_TILES[name]
            if mine and (k is None or k < mine):
                eng.wait_ge(sem("norm_lo_pool"), by_pool + (mine if k is None else k + 1))
            if mine < KT and (k is None or k >= mine):
                eng.wait_ge(sem("norm_lo_dve"), KT * len(before) - by_pool + (KT if k is None else k + 1) - mine)

        block = ctx.enter_context(nc.Block())

        @block.sync
        def _(sp):
            def load(n, nb=None):
                if n >= RAW:
                    before = UNITS[n - RAW]
                    if before not in POS:
                        sp.wait_ge(sem("ada_done"), int(before[3:]) + 1)
                    elif n >= U0 + RAW or n < U0:
                        sp.wait_ge(sem("lo_ready"), past_moe(POS[before] + 1, nb))
                    else:
                        sp.wait_ge(sem("lo_ready"), past_moe(POS0 + n - U0 - RAW + 1, nb))
                src = main_dram[n:n + 1, :, :].rearrange("a p f -> p (a f)")
                sp.dma_start(raw[:, n % RAW, :], src).then_inc(sem(f"ring_loaded{n % RAW}"), 16)

            def load_expert(j, e):
                s = (U0 + j) % RAW
                src = moe_dram[e, j:j + 1, :, :].rearrange("a b p f -> p (a b f)")
                sp.dma_start(raw[:, s, :], src).then_inc(sem(f"ring_loaded{s}"), 16)

            load(0)
            sp.dma_start(flat(mem0), mem_dram).then_inc(sem("ld_mem"), 16)
            sp.dma_start(cst[:, 0:C_ROT], cst_dram[:, 0:C_ROT]).then_inc(sem("ld_cst"), 16)
            sp.dma_start(cols[:, :], cols_dram).then_inc(sem("ld_cols"), 16)
            sp.dma_start(flat(hT), x_dram).then_inc(sem("ld_x"), 16)
            for n in range(1, U0):
                load(n)
                if n == 2:
                    sp.dma_start(cst[:, C_ROT:C_END], cst_dram[:, C_ROT:C_END]).then_inc(sem("ld_cst_rest"), 16)
            for j in range(MOE_UNITS):
                sp.wait_ge(sem("lo_ready"), POS0 + j - RAW + 1)
                load_expert(j, slice(0, 1))
            sp.wait_ge(sem("moe_plan"), 2)
            nb = sp.value_load(nbt[0:1, 0:1], min_val=E, max_val=MAXBLK)
            last = sp.value_load(nbt[0:1, 1:2], min_val=E - 1, max_val=MAXBLK - 1)
            with sp.Fori(0, last) as i:
                e = sp.value_load(etab[0:1, bass.ds(i + 1, 1)], min_val=0, max_val=E - 1)
                for j in range(MOE_UNITS):
                    sp.wait_ge(sem("lo_ready"), i * MOE_UNITS + POS0 + MOE_UNITS + j - RAW + 1)
                    load_expert(j, bass.ds(e, 1))
            for n in range(U0, len(UNITS)):
                load(n, nb)
            for half in range(2):
                k = KT // 2 * half
                wait_raw(sp, "final", k + KT // 2 - 1)
                sp.dma_start(out[:, T * k:T * (k + KT // 2)],
                             sqz[:, T * k:T * (k + KT // 2)]).then_inc(sem("stored"), 16)
            sp.wait_ge(sem("stored"), 32)

        @block.gpsimd
        def _(pool):
            def zero_keys(keys, name):
                pool.memset(keys[:, :, :], 0.0).then_inc(sem(name), 1)

            def subtract_hi(name, src=normed):
                for k in range(POOL_TILES[name]):
                    wait_hi(pool, name, k)
                    pool.tensor_tensor(xl[:, k, :], src[:, k, :], xh[:, k, :].bitcast(F32),
                                       ALU.subtract).then_inc(sem("norm_lo_pool"), 1)

            zero_keys(kz, "keys_zeroed")
            subtract_hi("mem0", mem0)
            subtract_hi("x")
            wait_filled(pool, "foxf")
            wait_lo(pool, "x")
            pool.memset(negc, 0.0).then_inc(sem("negc_zeroed"), 1)

            def normalise(rng):
                for a in rng:
                    w0, w1 = (P, 3 * P) if maps[a]["kind"] != "mem" else (T, 2 * T)
                    pool.wait_ge(sem("att_rsum"), a + 1)
                    pool.tensor_scalar(att_p[:, a % 3, 0:w0], att_p[:, a % 3, 0:w0], rsum[:, a % 3, 0:1], None,
                                       ALU.mult).then_inc(sem("att_probs"), 1)
                    pool.tensor_scalar(att_p[:, a % 3, w0:w1], att_p[:, a % 3, w0:w1], rsum[:, a % 3, 1:2], None,
                                       ALU.mult).then_inc(sem("att_probs"), 1)

            normalise(fox_maps)
            pool.wait_ge(sem("att_pv"), len(fox_maps))
            pool.dma_start(big[:, 3328:3328 + KT * T], mem_dram).then_inc(sem("ld_mem1"), 16)
            pool.dma_start(c_row, c_dram.broadcast_to([P, D])).then_inc(sem("ld_c"), 16)
            zero_keys(mkz1, "keys1_zeroed")
            pool.memset(upad[:, :, 0:PAD], 0.0).then_inc(sem("upad_zeroed"), 1)
            subtract_hi("ffn0")

            def hidden_lo(c, count):
                pool.wait_ge(sem("hid_hi"), count)
                pool.tensor_tensor(al[:, c % 2, :], sg[:, c % 2, :], ah[:, c % 2, :].bitcast(F32),
                                   ALU.subtract).then_inc(sem("hid_lo"), 1)

            for name in FF0_ORDER:
                if name[0] == "u":
                    hidden_lo(int(name[1:]), int(name[1:]) + 1)
                if name == f"u{FF0_CH - 1}":
                    subtract_hi("mem1")
            subtract_hi("mix1")
            normalise(mem_maps)
            wait_done(pool, "co3")
            pool.memset(y_tok, 0.0).then_inc(sem("moe_y"), 1)
            pool.memset(scat, 0.0).then_inc(sem("moe_scat"), 1)
            for j in range(4):
                wait_drained(pool, f"scat{j}")
            zero_keys(kz, "keys_zeroed")
            normalise(diff_maps)

            sbm = cc(C_SBM)
            for g in range(SB_PAIRS + 1):
                for i in pair(g):
                    pool.wait_ge(sem("sb_m"), i + 1)
                    for at in (0, 2 * P):
                        pool.tensor_tensor(sb_m[:, i % 2, at:at + P], sb_m[:, i % 2, at:at + P], sbm,
                                           ALU.mult).then_inc(sem("sb_masked"), 1)
                for i in pair(g - 1):
                    pool.wait_ge(sem("sb_exp"), i + 1)
                    for at in (0, 2 * P):
                        pool.tensor_tensor(sb_a[:, i % 2, at:at + P], sb_a[:, i % 2, at:at + P], sbm,
                                           ALU.mult).then_inc(sem("sb_probs"), 1)
            for c in range(FF2_CH):
                hidden_lo(c, FF0_CH + c + 1)

        @block.scalar
        def _(act):
            step = [0]

            def link(ins):
                step[0] += 1
                ins.then_inc(sem("act_step"), 1)
                act.wait_ge(sem("act_step"), step[0])

            def split_hi(p, nb=None):
                n = NUMBER[SPLIT[p]]
                wait_loaded(act, n, nb)
                if p >= SPL:
                    wait_done(act, SPLIT[p - SPL], nb)
                act.activation(wh[:, p % SPL, :], raw[:, n % RAW, :], ACT.Copy).then_inc(sem("hi_ready"), 1)

            def split_after(name, nb=None):
                p = POS[name] + SPL
                if p >= len(SPLIT):
                    return
                if nb is None and p >= POS0:
                    wait_loaded(act, U0 + p - POS0)
                    wait_done(act, name)
                    act.activation(wh[:, p % SPL, :], raw[:, (U0 + p - POS0) % RAW, :],
                                   ACT.Copy).then_inc(sem("hi_ready"), 1)
                else:
                    split_hi(p, nb)

            def square(src, dst, j):
                act.activation(dst[:, 512 * j:512 * j + 512], pair_of(src, j), ACT.Square).then_inc(sem("norm_sq"), 1)

            def norm_sd(k, scale):
                wait_filled(act, f"nsum{k}")
                act.activation(scale[:, :], bank(f"nsum{k}")[:, 0:T], ACT.Sqrt, scale=1.0 / D,
                               bias=eps).then_inc(drained(f"nsum{k}"), 1)

            def warm(func):
                n = warmed[0]
                warmed[0] += 1
                act.activation(warm_out[:, n:n + 1], ones[:, 0:1], func)

            warmed = [0]

            def norm_hi(name, src=normed):
                for k in range(KT):
                    wait_raw(act, name, k)
                    act.activation(xh[:, k, :], src[:, k, :], ACT.Copy).then_inc(sem("norm_hi"), 1)

            def norm_hi_shifted(name, at):
                for k in range(KT):
                    wait_raw(act, name, k)
                    act.activation(xh[:, k, :], normed[:, k, :], ACT.Identity,
                                   bias=mod[:, at + k:at + k + 1]).then_inc(sem("norm_hi"), 1)

            def qk_square(k, name):
                wait_done(act, name)
                if k >= 2:
                    wait_filled(act, f"qsum{k - 2}")
                act.activation(att_pT[:, k % 2, :], bank(name), ACT.Square).then_inc(sem("qk_sq"), 1)

            def qk_sd(k):
                wait_filled(act, f"qsum{k}")
                if k >= 2:
                    wait_drained(act, QK_UNITS[k - 2])
                act.activation(att_p[:, k % 2, :], bank(f"qsum{k}"), ACT.Sqrt, scale=1.0 / HD,
                               bias=eps).then_inc(drained(f"qsum{k}"), 1)

            def values_out(name, dst, nb=None):
                wait_done(act, name, nb)
                act.activation(dst, bank(name).rearrange("p (a b) -> p a b", a=TT), ACT.Copy).then_inc(drained(name), 1)

            split_hi(0)
            act.wait_ge(sem("ld_mem"), 16)
            for j in range(4):
                square(mem0, sqz, j)
            act.wait_ge(sem("ld_cst"), 16)
            warm(ACT.Sqrt)
            norm_sd(0, rn_mem)
            norm_hi("mem0", mem0)
            act.wait_ge(sem("ld_x"), 16)
            for j in range(4):
                square(hT, x_sq, j)
            split_hi(1)
            norm_sd(1, rn)
            split_hi(2)
            qk_square(0, "mk0")
            split_after("mk0")
            wait_done(act, "mv0")
            norm_hi("x")
            split_after("mv0")
            wait_filled(act, "nsum1")
            values_out("mv0", vv[:, :, FOX:D])
            qk_sd(0)
            wait_filled(act, "lam")
            act.activation(lam[:, 2:4], bank("lam")[:, 0:2], ACT.Exp).then_inc(drained("lam"), 1)
            act.wait_ge(sem("fox_negabs"), 1)
            link(act.activation(lsf[:, 1, :, :], lsf[:, 1, :, :], ACT.Exp))
            act.activation(lsf[:, 1, :, :], lsf[:, 1, :, :], ACT.Ln, bias=1.0).then_inc(sem("fox_log1p"), 1)
            qk_square(1, "mq0")
            split_after("mq0")
            for j in range(6):
                name = UNITS_A[3 + j]
                qk_square(2 + j, name)
                split_after(name)
                qk_sd(1 + j)
                if j == 0:
                    act.wait_ge(sem("negc_zeroed"), 1)
                    wait_filled(act, "cum")
                    act.activation(negc[0:FOX_HEADS, :], bank("cum")[0:FOX_HEADS, 0:T], ACT.Copy,
                                   scale=-1.0).then_inc(sem("negc_ready"), 1)
            for j in range(3):
                values_out(f"fv{j}", vv[:, :, T * j:T * j + T])
                if j == 0:
                    qk_sd(7)
            warm(ACT.Exp)

            def attention(rng, meanwhile=None, before=None):
                n, a0 = len(rng), rng[0]
                for i in range(n + PV_LAG + 1):
                    if before:
                        before(i)
                    if i < n:
                        a = a0 + i
                        w0, w1 = (P, 3 * P) if maps[a]["kind"] != "mem" else (T, 2 * T)
                        act.wait_ge(sem("att_max"), 2 * (a + 1))
                        for t, (lo, hi) in enumerate(((0, w0), (w0, w1))):
                            act.activation(att_p[:, a % 3, lo:hi], att_p[:, a % 3, lo:hi], ACT.Exp,
                                           bias=nmx[:, a % 3, t:t + 1],
                                           accum_out=ssum[:, a % 3, t:t + 1]).then_inc(sem("att_exp"), 1)
                    if 0 <= i - T_LAG < n:
                        a = a0 + i - T_LAG
                        w = 3 * P if maps[a]["kind"] != "mem" else 4 * P
                        wait_filled(act, f"pT{a}")
                        if a >= 2:
                            act.wait_ge(sem("att_pv"), a - 1)
                        act.activation(att_pT[:, a % 2, 0:w], bank(f"pT{a}")[:, 0:w],
                                       ACT.Copy).then_inc(drained(f"pT{a}"), 1)
                    if 0 <= i - PV_LAG - 1 < n and (i - PV_LAG - 1) % 2 == 1 and maps[a0]["kind"] != "diff":
                        g = (a0 + i - PV_LAG - 1) // 2
                        act.wait_ge(sem("att_pv"), 2 * (g + 1))
                        act.activation(xh[:, maps[2 * g]["to"], :], bank(f"pv{g}")[:, 0:T],
                                       ACT.Copy).then_inc(sem("mix_hi"), 1)
                    if meanwhile:
                        meanwhile(i)

            attention(fox_maps, lambda i: [split_after(name) for name in FOX_SPLITS.get(i, ())])

            warm(ACT.Sqrt)
            for j in range(4):
                wait_drained(act, f"fo{j}")
                square(hT, sqz, j)
                if j < 3:
                    split_after(f"fo{j}")
            norm_sd(2, rn)
            split_after("fo3")
            norm_hi("ffn0")

            act.wait_ge(sem("ld_c"), 16)
            act.activation(c_row, c_row, ACT.Silu).then_inc(sem("c_ready"), 1)

            def hidden_hi(c, name):
                wait_drained(act, name)
                act.activation(ah[:, c % 2, :], sg[:, c % 2, :], ACT.Copy).then_inc(sem("hid_hi"), 1)

            for name in ffn_order(FF0_CH, ("g", "u"), "d"):
                c = int(name[1:])
                if name[0] == "g":
                    wait_done(act, name)
                    if c >= 2:
                        act.wait_ge(sem("hid_lo"), c - 1)
                    act.activation(sg[:, c % 2, :], bank(name), ACT.Silu).then_inc(drained(name), 1)
                split_after(name)
                if name[0] == "u":
                    hidden_hi(c, name)
                if name == f"u{FF0_CH - 1}":
                    norm_hi("mem1")
            wait_lo(act, "mem1")
            warm(ACT.Sqrt)
            for j in range(4):
                wait_drained(act, f"down0_{j}")
                square(hT, sqz, j)
            qk_square(8, "mk1")
            norm_sd(3, rn)
            split_after("mk1")
            wait_done(act, "mv1")
            norm_hi("mix1")
            split_after("mv1")
            values_out("mv1", mv1)
            qk_sd(8)
            qk_square(9, "mq1")
            split_after("mq1")

            for j in range(6):
                wait_done(act, f"ci{j}")
                for t in range(2):
                    c = 2 * j + t
                    if j < 3:
                        ins = act.activation(abuf[:, c, :], bank(f"ci{j}")[:, T * t:T * t + T], ACT.Identity,
                                             bias=cols[:, V_CB + c:V_CB + c + 1])
                    else:
                        ins = act.activation(cacc[:, c - CT, :], bank(f"ci{j}")[:, T * t:T * t + T], ACT.Sigmoid,
                                             bias=cols[:, V_CB + c:V_CB + c + 1])
                ins.then_inc(drained(f"ci{j}"), 1)
                if j < 3:
                    split_after(f"ci{j}")
                if j == 0:
                    qk_sd(9)
            warm(ACT.Exp)
            def diagonals(first, last):
                for n in range(first, last):
                    c, tap = n // TAPS, n % TAPS
                    if n >= DIAG_RING:
                        act.wait_ge(sem("tap_used"), n - DIAG_RING + 1)
                    at = V_TAP + CT * tap + c
                    act.activation(diag[:, n % DIAG_RING, :], ident, ACT.Copy,
                                   scale=cols[:, at:at + 1]).then_inc(sem("diag_ready"), 1)

            def convolved(c):
                act.wait_ge(sem("tap_used"), TAPS * (c + 1))
                act.activation(cacc[:, c, :], bank(f"conv{c}")[:, 0:T], ACT.Identity,
                               bias=cols[:, V_DWB + c:V_DWB + c + 1]).then_inc(drained(f"conv{c}"), 1)

            def meanwhile(i):
                if i < MEM_STEPS:
                    diagonals(max(DIAG_RING, PE_TAPS * i // MEM_STEPS), PE_TAPS * (i + 1) // MEM_STEPS)
                if i in MEM_SPLITS:
                    split_after(MEM_SPLITS[i])
                if i == MEM_STEPS // 2:
                    convolved(0)

            diagonals(0, DIAG_RING)
            attention(mem_maps, before=meanwhile)
            for c in range(1, CT_PE):
                convolved(c)
            warm(ACT.Sqrt)
            for c in range(CT):
                act.wait_ge(sem("ln_centred"), c + 1)
                act.activation(sqz[:, T * c:T * c + T], cacc[:, c, :], ACT.Square).then_inc(sem("ln_sq"), 1)
            wait_filled(act, "lnvar")
            act.activation(rn[:, :], bank("lnvar")[:, 0:T], ACT.Sqrt, scale=1.0 / CONV,
                           bias=eps).then_inc(drained("lnvar"), 1)
            warm(ACT.Silu)

            def conv_hi(c):
                act.wait_ge(sem("conv_silu"), c + 1)
                act.activation(xh[:, c, :], cacc[:, c, :], ACT.Copy).then_inc(sem("conv_hi"), 1)

            for c in range(CT):
                act.wait_ge(sem("ln_scaled"), c + 1)
                act.activation(cacc[:, c, :], cacc[:, c, :], ACT.Silu, bias=cols[:, V_LNB + c:V_LNB + c + 1],
                               scale=cols[:, V_LNG + c:V_LNG + c + 1]).then_inc(sem("conv_silu"), 1)
                if c:
                    conv_hi(c - 1)
            conv_hi(CT - 1)
            warm(ACT.Sqrt)
            for j in range(4):
                wait_drained(act, f"co{j}")
                square(hT, sqz, j)
                if j < 3:
                    split_after(f"co{j}")
            norm_sd(4, rn)
            split_after("co3")
            for j in range(4):
                wait_filled(act, f"ztok{j}")
                act.activation(z_tok[:, j // 2, 512 * (j % 2):512 * (j % 2) + 512], bank(f"ztok{j}"),
                               ACT.Copy).then_inc(drained(f"ztok{j}"), 1)
            act.wait_ge(sem("gate_diff"), 1)
            act.activation(pexp[:, 0:2], pexp[:, 0:2], ACT.Exp).then_inc(sem("gate_exp"), 1)
            for j in range(2):
                wait_filled(act, f"gather{j}")
                act.activation(four_of(xgh, j), bank(f"gather{j}"), ACT.Copy).then_inc(sem("gather_hi"), 1)

            act.wait_ge(sem("moe_plan"), 2)
            nb = act.value_load(nbt[0:1, 0:1], min_val=E, max_val=MAXBLK)
            with act.Fori(0, nb) as i:
                def split_next(j):
                    n, p = U0 + j + SPL, POS0 + j + SPL
                    act.wait_ge(sem(f"ring_loaded{n % RAW}"), i * (16 * MOE_UNITS // RAW) + 16 * (n // RAW + 1))
                    act.wait_ge(sem("unit_done"), i * MOE_UNITS + POS0 + j + 1)
                    act.activation(wh[:, p % SPL, :], raw[:, n % RAW, :], ACT.Copy).then_inc(sem("hi_ready"), 1)

                def turned_hi(c):
                    b, per, use = MOE_BANK[f"T{c}"]
                    act.wait_ge(sem(f"moe_filled{b}"), i * per + use + 1)
                    act.activation(ah[:, c % 2, :], ps[:, b, :], ACT.Copy).then_inc(sem("moe_hid_hi"), 1)

                for j, (kind, c, half) in enumerate(MOE_ORDER):
                    if kind == "g" and half == 1:
                        act.wait_ge(sem("unit_done"), i * MOE_UNITS + POS0 + j + 1)
                        act.activation(sg[:, c % 2, :], ps[:, 2 * (c % 2), :], ACT.Silu).then_inc(sem("moe_silu"), 1)
                    split_next(j)
                    if kind == "g" and half == 1 and c >= 1:
                        turned_hi(c - 1)
                    if (kind, c, half) == ("d", MOE_CH - 2, 1):
                        turned_hi(MOE_CH - 1)
                        for g in range(2):
                            b, per, use = MOE_BANK[f"G{g}"]
                            act.wait_ge(sem(f"moe_filled{b}"), i * per + use + 1)
                            act.activation(four_of(xgh, g), ps[:, b, :], ACT.Copy).then_inc(sem("gather_hi"), 1)
                for g in range(2):
                    act.activation(y_tok[:, 512 * g:512 * g + 512], ps[:, 4 + g, :],
                                   ACT.Copy).then_inc(sem("moe_y"), 1)

            warm(ACT.Sqrt)
            for j in range(4):
                wait_drained(act, f"scat{j}")
                square(hT, sqz, j)
            norm_sd(5, rn)
            norm_hi_shifted("mix2", 0)
            for j, name in enumerate(ROPED):
                wait_done(act, name, nb)
                if j >= 2:
                    act.wait_ge(sem("rope_done"), rope_count(j - 1))
                act.activation(att_pT[:, j % 2, :], bank(name), ACT.Copy).then_inc(drained(name), 1)
                split_after(name, nb)
            for j in range(2):
                values_out(f"dv{j}", vv[:, :, T * j:T * j + T], nb)
                split_after(f"dv{j}", nb)
            for j in range(2):
                wait_done(act, f"sq{j}", nb)
                act.activation(pair_of(qT, 2 + j), bank(f"sq{j}"), ACT.Copy, scale=SCALE).then_inc(drained(f"sq{j}"), 1)
                split_after(f"sq{j}", nb)
            act.wait_ge(sem("keys_zeroed"), 2)
            for j in range(2):
                wait_done(act, f"sk{j}", nb)
                src = bank(f"sk{j}").rearrange("p (a b) -> p a b", a=2)
                act.activation(kz[0:HD, 8 + 4 * j:12 + 4 * j:2, :], src[0:HD, :, :], ACT.Copy)
                act.activation(kz[HD:P, 9 + 4 * j:12 + 4 * j:2, :], src[HD:P, :, :],
                               ACT.Copy).then_inc(drained(f"sk{j}"), 1)
                split_after(f"sk{j}", nb)
            for j in range(2):
                values_out(f"sv{j}", vv[:, :, 512 + T * j:512 + T * j + T], nb)
            warm(ACT.Exp)
            act.wait_ge(sem("rope_done"), rope_count(4))
            attention(diff_maps, lambda i: split_after(DIFF_SPLITS[i], nb) if i in DIFF_SPLITS else None)

            def sb_hi(g):
                act.wait_ge(sem("sb_pv"), 2 * (g + 1))
                act.activation(xh[:, 4 + g, :], bank(f"sbo{g}")[:, 0:T], ACT.Copy).then_inc(sem("sb_hi"), 1)

            act.wait_ge(sem("att_pv"), len(maps))
            for j in range(2):
                for g in range(2):
                    wait_drained(act, f"pv{diff_maps[0] // 2 + 2 * j + g}")
                act.activation(att_pT[:, j, :], pair_of(qT, j), ACT.Square).then_inc(sem("sub_sq"), 1)

            for g in range(SB_PAIRS + 1):
                for i in pair(g):
                    act.wait_ge(sem("sb_abs"), i + 1)
                    act.activation(sb_l[:, i % 4, :], sb_l[:, i % 4, :], ACT.Exp).then_inc(sem("sb_exp_abs"), 1)
                for i in pair(g):
                    act.wait_ge(sem("sb_exp_abs"), i + 1)
                    act.activation(sb_l[:, i % 4, :], sb_l[:, i % 4, :], ACT.Ln, bias=1.0).then_inc(sem("sb_log1p"), 1)
                if g == 0:
                    for j in range(2):
                        wait_filled(act, f"sub{j}")
                        act.activation(sub_r[:, j, :], bank(f"sub{j}"), ACT.Sqrt, scale=1.0 / P,
                                       bias=eps).then_inc(drained(f"sub{j}"), 1)
                for i in pair(g - 1):
                    wait_drained(act, f"sbx{i}")
                    if i >= 2:
                        act.wait_ge(sem("sb_pv"), i - 1)
                    act.activation(sb_a[:, i % 2, :], sb_b[:, i % 4, :], ACT.Exp).then_inc(sem("sb_exp"), 1)
                if g >= 1:
                    act.wait_ge(sem("sub_out"), g)
                    act.activation(xh[:, g - 1, :], qT[:, g - 1, :], ACT.Copy).then_inc(sem("sub_hi"), 1)
                if g >= 2:
                    sb_hi(g - 2)
            sb_hi(SB_PAIRS - 1)

            warm(ACT.Sqrt)
            for j in range(4):
                wait_drained(act, f"wo{j}")
                square(hT, sqz, j)
                if j < 3:
                    split_after(f"wo{j}", nb)
            norm_sd(6, rn)
            split_after("wo3", nb)
            norm_hi_shifted("ffn2", 24)
            for name in ffn_order(FF2_CH, ("a",), "b"):
                c = int(name[1:])
                split_after(name, nb)
                if name[0] == "a":
                    hidden_hi(c, name)
            warm(ACT.Sqrt)
            for j in range(4):
                wait_drained(act, f"down2_{j}")
                square(hT, sqz, j)
            norm_sd(7, rn)

        @block.tensor
        def _(pe):
            mm = nc.tensor.matmul
            pe.wait_ge(sem("ld_cst"), 16)

            def exact(out_, left, right, start, stop, **kw):
                (lh, ll), (rh, rl) = left, right
                mm(out_, lh, rh, start=start, stop=False, **kw)
                mm(out_, lh, rl, start=False, stop=False, **kw)
                return mm(out_, ll, rh, start=False, stop=stop, **kw)

            def weights(name, k, nb=None):
                pe.wait_ge(sem("lo_ready"), past_moe(POS[name] + 1, nb))
                s = POS[name] % SPL
                return [w[:, s, :].rearrange("p (k n) -> p k n", k=k) for w in (wh, wl)]

            def turn(name, pieces):
                claim(pe, name)
                for at, src in pieces:
                    ins = pe.transpose(bank(name)[:, at:at + P], src, ident)
                ins.then_inc(filled(name), 1)

            def norm_sum(k, src=sqz):
                claim(pe, f"nsum{k}")
                for j in range(KT):
                    if j % 2 == 0:
                        pe.wait_ge(sem("norm_sq"), 4 * k + j // 2 + 1)
                    ins = mm(bank(f"nsum{k}")[:, 0:T], ones, src[:, T * j:T * j + T], start=(j == 0), stop=(j == KT - 1))
                ins.then_inc(filled(f"nsum{k}"), 1)

            def head_sum(k):
                pe.wait_ge(sem("qk_sq"), k + 1)
                claim(pe, f"qsum{k}")
                mm(bank(f"qsum{k}"), headones, att_pT[:, k % 2, :], start=True, stop=True).then_inc(filled(f"qsum{k}"), 1)

            def by_channels(name, nb=None, ready=None):
                h, l = weights(name, KT, nb)
                claim(pe, name)
                steps = [(t, k) for k in range(KT) for t in range(2)] if ready else [(t, k) for t in range(2) for k in range(KT)]
                for t, k in steps:
                    if ready and t == 0:
                        ready(k)
                    c = slice(P * t, P * t + P)
                    ins = exact(bank(name)[:, T * t:T * t + T], (h[:, k, c], l[:, k, c]), (xh[:, k, :], xl[:, k, :]),
                                k == 0 and (t == 0 or not ready), k == KT - 1, skip_group_check=bool(ready))
                ins.then_inc(sem("unit_done"), 1)

            def arriving(stream):
                return lambda k: wait_lo(pe, stream, k)

            def by_tokens(name, nb=None):
                h, l = weights(name, KT, nb)
                claim(pe, name)
                for t in range(TT):
                    for k in range(KT):
                        c = slice(P * t, P * t + P)
                        ins = exact(bank(name)[:, T * t:T * t + T], (xh[:, k, c], xl[:, k, c]), (h[:, k, :], l[:, k, :]),
                                    k == 0, k == KT - 1)
                ins.then_inc(sem("unit_done"), 1)

            def narrow(name, w, n, stream):
                claim(pe, name)
                for k in range(KT):
                    wait_raw(pe, stream, k)
                    for t in range(TT):
                        ins = mm(bank(name)[:, n * t:n * t + n], normed[:, k, P * t:P * t + P], w[:, k, :],
                                 start=(k == 0 and t == 0), stop=(k == KT - 1), skip_group_check=True)
                ins.then_inc(filled(name), 1)

            def down(name, acc, c, last, count, nb=None):
                if c == 0:
                    for j in range(4):
                        claim(pe, f"{acc}{j}")
                h, l = weights(name, 2, nb)
                pe.wait_ge(sem("hid_lo"), count)
                a = [t[:, c % 2, :].rearrange("p (k n) -> p k n", k=2) for t in (ah, al)]
                for o in range(KT):
                    for k in range(2):
                        n = slice(P * o, P * o + P)
                        ins = exact(bank(f"{acc}{o // 2}")[:, T * (o % 2):T * (o % 2) + T], (h[:, k, n], l[:, k, n]),
                                    (a[0][:, k, :], a[1][:, k, :]), c == 0 and k == 0 and o % 2 == 0,
                                    c == last and k == 1, skip_group_check=True)
                ins.then_inc(sem("unit_done"), 1)

            norm_sum(0)
            by_channels("mk0", ready=arriving("mem0"))
            norm_sum(1, x_sq)
            pe.wait_ge(sem("lam_prod"), 2)
            claim(pe, "lam")
            mm(bank("lam")[:, 0:2], ones, lam[:, 0:2], start=True, stop=True).then_inc(filled("lam"), 1)
            by_tokens("mv0")
            head_sum(0)

            pe.wait_ge(sem("ld_cols"), 16)
            narrow("foxf", cols[:, V_WF:V_RT].rearrange("p (k n) -> p k n", k=KT), FOX_HEADS, "x")
            by_channels("mq0", ready=arriving("x"))
            for j in range(6):
                by_channels(UNITS_A[3 + j])
                head_sum(1 + j)
                if j == 0:
                    pe.wait_ge(sem("ld_cst_rest"), 16)
                    pe.wait_ge(sem("fox_logf"), 1)
                    claim(pe, "cum")
                    lf = lsf[:, 0, :, :]
                    cum = bank("cum")
                    mm(cum[0:FOX_HEADS, 0:P], lf[:, 0, :], tri, start=True, stop=True)
                    mm(cum[0:FOX_HEADS, P:T], lf[:, 0, :], ones, start=True, stop=False)
                    mm(cum[0:FOX_HEADS, P:T], lf[:, 1, :], tri, start=False, stop=True)
                    mm(cum[:, T:T + FOX_HEADS], tri, lf[:, 0, :], start=True, stop=True)
                    mm(cum[:, T + FOX_HEADS:T + 2 * FOX_HEADS], ones, lf[:, 0, :], start=True, stop=False)
                    mm(cum[:, T + FOX_HEADS:T + 2 * FOX_HEADS], tri, lf[:, 1, :], start=False,
                       stop=True).then_inc(filled("cum"), 1)
            by_tokens("fv0")
            head_sum(7)
            by_tokens("fv1")
            by_tokens("fv2")

            def attention(rng, meanwhile=None):
                n, a0 = len(rng), rng[0]
                for i in range(n + PV_LAG):
                    if i < n:
                        a = a0 + i
                        m, s = maps[a], bank(f"sc{a}")
                        full = m["kind"] == "mem"
                        claim(pe, f"sc{a}")
                        for t, (at, nk) in enumerate(((0, T), (T, T)) if full else ((0, P), (P, T))):
                            fox = m["kind"] == "fox"
                            ins = mm(s[:, at:at + nk], m["q"][:, P * t:P * t + P], m["k"][:, 0:nk],
                                     start=True, stop=not fox)
                            if fox:
                                ins = mm(s[:, at:at + nk], selh[:, m["head"], :], negc[:, 0:nk],
                                         start=False, stop=True)
                        ins.then_inc(filled(f"sc{a}"), 1)
                    if 0 <= i - T_LAG < n:
                        a = a0 + i - T_LAG
                        pe.wait_ge(sem("att_probs"), 2 * (a + 1))
                        order = (0, 2, 1, 3) if maps[a]["kind"] == "mem" else (0, 1, 2)
                        turn(f"pT{a}", [(P * c, att_p[:, a % 3, P * o:P * o + P]) for c, o in enumerate(order)])
                    if 0 <= i - PV_LAG < n:
                        a = a0 + i - PV_LAG
                        m, g = maps[a], a // 2
                        if a % 2 == 0:
                            claim(pe, f"pv{g}")
                        o = bank(f"pv{g}")[m["row"]:m["row"] + m["m"], :]
                        wait_drained(pe, f"pT{a}")
                        pT = att_pT[:, a % 2, :]
                        second = m["kind"] == "diff" and a % 2 == 1
                        last = m["kind"] != "diff" or a % 2 == 1
                        mm(o[:, 0:T], m["v"][0], pT[:, 0:T], start=not second, stop=False, skip_group_check=True)
                        if m["kind"] == "mem":
                            ins = mm(o[:, 0:T], m["v"][1], pT[:, T:2 * T], start=False, stop=last,
                                     skip_group_check=True)
                        else:
                            ins = mm(o[:, P:T], m["v"][1], pT[:, T:T + P], start=False, stop=last,
                                     skip_group_check=True)
                        ins.then_inc(sem("att_pv"), 1)
                    if meanwhile:
                        meanwhile(i)

            pe.wait_ge(sem("keys_zeroed"), 1)
            for name in ["mk0", "mv0", "mq0"] + UNITS_A[3:12]:
                wait_drained(pe, name)
            pe.wait_ge(sem("negc_ready"), 1)
            pe.wait_ge(sem("selh_ready"), 1)
            attention(fox_maps)

            for g in range(8):
                wait_drained(pe, f"pv{g}")
            for j in range(4):
                by_channels(f"fo{j}")
            norm_sum(2)

            for name in ffn_order(FF0_CH, ("g", "u"), "d"):
                c = int(name[1:])
                if name[0] == "d":
                    down(name, "down0_", c, FF0_CH - 1, c + 1)
                else:
                    by_channels(name, ready=arriving("ffn0") if name == "g0" else None)

            by_channels("mk1", ready=arriving("mem1"))
            norm_sum(3)
            by_tokens("mv1")
            head_sum(8)
            by_channels("mq1", ready=arriving("mix1"))
            for j in range(6):
                by_channels(f"ci{j}")
                if j == 0:
                    head_sum(9)
            def convolve(first, last):
                for n in range(first, last):
                    c, tap = n // TAPS, n % TAPS
                    if n == 0:
                        pe.wait_ge(sem("glu"), 3)
                    if tap == 0:
                        claim(pe, f"conv{c}")
                    pe.wait_ge(sem("diag_ready"), n + 1)
                    mm(bank(f"conv{c}")[:, 0:T], diag[:, n % DIAG_RING, :],
                       upad[:, c, tap:tap + T], start=(tap == 0),
                       stop=(tap == TAPS - 1)).then_inc(sem("tap_used"), 1)

            for name in ("mk1", "mv1", "mq1"):
                wait_drained(pe, name)
            attention(mem_maps, lambda i: convolve(PE_TAPS * i // MEM_STEPS, PE_TAPS * (i + 1) // MEM_STEPS))
            claim(pe, "lnsum")
            for c in range(CT):
                if c < CT_PE:
                    wait_drained(pe, f"conv{c}")
                else:
                    pe.wait_ge(sem("conv_tap"), DVE_TAPS - CT + c + 1)
                ins = mm(bank("lnsum")[:, 0:T], ones, cacc[:, c, :], start=(c == 0), stop=(c == CT - 1))
            ins.then_inc(filled("lnsum"), 1)
            claim(pe, "lnvar")
            for c in range(CT):
                pe.wait_ge(sem("ln_sq"), c + 1)
                ins = mm(bank("lnvar")[:, 0:T], ones, sqz[:, T * c:T * c + T], start=(c == 0), stop=(c == CT - 1))
            ins.then_inc(filled("lnvar"), 1)
            for g in range(mem_maps[0] // 2, mem_maps[0] // 2 + 2):
                wait_drained(pe, f"pv{g}")
            for j in range(4):
                by_channels(f"co{j}", ready=(lambda k: pe.wait_ge(sem("conv_lo"), min(k + 1, CT))) if j == 0 else None)
            norm_sum(4)

            narrow("router", cols[:, V_RT:V_END].rearrange("p (k n) -> p k n", k=KT), E, "ffn1")
            def by_token(j):
                t = j // 2
                turn(f"ztok{j}", [(P * c, normed[:, 4 * (j % 2) + c, P * t:P * t + P]) for c in range(4)])

            for j in range(3):
                by_token(j)
            pe.wait_ge(sem("moe_marks"), 1)
            claim(pe, "mcum")
            b = bank("mcum")
            M = [plan_f[:, 0, E * t:E * t + E] for t in range(TT)]
            mm(b[:, 0:E], tri, M[0], start=True, stop=True)
            mm(b[:, E:2 * E], ones, M[0], start=True, stop=False)
            mm(b[:, E:2 * E], tri, M[1], start=False, stop=True)
            mm(b[:, 2 * E:3 * E], ones, M[0], start=True, stop=False)
            mm(b[:, 2 * E:3 * E], ones, M[1], start=False, stop=True).then_inc(filled("mcum"), 1)
            by_token(3)

            def as_rows(name, src):
                claim(pe, name)
                for a in range(2):
                    for t in range(TT):
                        ins = mm(bank(name)[:, T * a + P * t:T * a + P * t + P],
                                 src[:, a, t:t + 1].broadcast_to([P, P]), ident, start=True, stop=True)
                ins.then_inc(filled(name), 1)

            pe.wait_ge(sem("moe_keys"), 1)
            as_rows("krow", kcol)
            def gather(psum, j):
                for c in range(4):
                    for t in range(TT):
                        ins = mm(psum[:, CAP * c:CAP * c + CAP], z_tok[:, t, P * (4 * j + c):P * (4 * j + c) + P],
                                 sel[:, t, :], start=(t == 0), stop=(t == TT - 1))
                return ins

            for j in range(4):
                wait_drained(pe, f"ztok{j}")
            pe.wait_ge(sem("moe_sel"), TT)
            for j in range(2):
                claim(pe, f"gather{j}")
                gather(bank(f"gather{j}"), j).then_inc(filled(f"gather{j}"), 1)
            pe.wait_ge(sem("moe_plan"), 2)
            nb = pe.value_load(nbt[0:1, 0:1], min_val=E, max_val=MAXBLK)
            pe.wait_ge(sem("moe_gates"), 2)
            as_rows("grow", gcol)

            def scatter(psum, j):
                for c in range(2):
                    o = 2 * j + c
                    ins = mm(psum[:, T * c:T * c + T], y_tok[:, P * o:P * o + P], scat, start=True, stop=True)
                return ins

            for b in (0, 1, 2, 3, 6, 7):
                pe.wait_ge(sem(f"drained{b}"), before_moe[b])
            with pe.Fori(0, nb) as i:
                def unit(j, k):
                    p = POS0 + j
                    pe.wait_ge(sem("lo_ready"), i * MOE_UNITS + p + 1)
                    return [w[:, p % SPL, :].rearrange("p (k n) -> p k n", k=k) for w in (wh, wl)]

                def spare(use):
                    b, per, at = MOE_BANK[use]
                    pe.wait_ge(sem(f"moe_drained{b}"), i * per + at + 1)
                    return ps[:, b, :], sem(f"moe_filled{b}")

                def spare_drained(use):
                    b, per, at = MOE_BANK[use]
                    pe.wait_ge(sem(f"moe_drained{b}"), i * per + at + 2)

                def turned(c):
                    pe.wait_ge(sem("moe_prod"), i * MOE_CH + c + 1)
                    psum, done = spare(f"T{c}")
                    for f in range(4):
                        ins = pe.transpose(psum[:, P * f:P * f + P], sg[:, c % 2, P * f:P * f + P], ident)
                    ins.then_inc(done, 1)

                def scattered(j):
                    psum, done = spare(f"S{j}")
                    scatter(psum, j).then_inc(done, 1)

                for j, (kind, c, half) in enumerate(MOE_ORDER):
                    if j < 2:
                        b = MOE_BANK[f"G{half}"][0]
                        pe.wait_ge(sem(f"moe_drained{b}"), i * len(MOE_USES[b]) + 1)
                    if kind in "gu":
                        b = 2 * (c % 2) + (kind == "u")
                        w = unit(j, 4)
                        for k in range(4):
                            x = [t[:, 4 * half + k, :] for t in (xgh, xgl)]
                            ins = exact(ps[:, b, :], x, (w[0][:, k, :], w[1][:, k, :]), half == 0 and k == 0,
                                        half == 1 and k == 3)
                    else:
                        w = unit(j, 2)
                        if half == 0:
                            spare_drained(f"T{c}")
                            if c == 0:
                                pe.wait_ge(sem("moe_y"), i * 2 + 1)
                                for b in (4, 5):
                                    pe.wait_ge(sem(f"drained{b}"), before_moe[b])
                        for k in range(2):
                            s = slice(P * (2 * half + k), P * (2 * half + k) + P)
                            for o in range(2):
                                n = slice(512 * o, 512 * o + 512)
                                ins = exact(ps[:, 4 + o, :], (ah[:, c % 2, s], al[:, c % 2, s]),
                                            (w[0][:, k, n], w[1][:, k, n]), c == 0 and half == 0 and k == 0,
                                            c == MOE_CH - 1 and half == 1 and k == 1)
                    ins.then_inc(sem("unit_done"), 1)
                    if (kind, half) == ("g", 1) and c >= 1:
                        turned(c - 1)
                    if (kind, half) == ("u", 1) and c < 4:
                        if c == 0:
                            pe.wait_ge(sem("moe_y"), i * 2 + 1)
                            pe.wait_ge(sem("moe_scat"), i + 1)
                        scattered(c)
                    if (kind, c, half) == ("d", MOE_CH - 2, 1):
                        turned(MOE_CH - 1)
                        pe.wait_ge(sem("moe_sel"), i * TT + 2 * TT)
                        for g in range(2):
                            psum, done = spare(f"G{g}")
                            gather(psum, g).then_inc(done, 1)
            pe.wait_ge(sem("moe_y"), nb * 2 + 1)
            pe.wait_ge(sem("moe_scat"), nb + 1)
            for b in (6, 7):
                pe.wait_ge(sem(f"moe_drained{b}"), nb * len(MOE_USES[b]) + 1)
            for j in range(4):
                claim(pe, f"scat{j}")
                scatter(bank(f"scat{j}"), j).then_inc(filled(f"scat{j}"), 1)

            norm_sum(5)
            for j, name in enumerate(WIN):
                if name[1] == "v":
                    by_tokens(name, nb)
                else:
                    by_channels(name, nb, arriving("mix2") if j == 0 else None)
                if 1 <= j <= 4:
                    wait_drained(pe, ROPED[j - 1])
                    claim(pe, f"rot{j - 1}")
                    mm(bank(f"rot{j - 1}"), rot, att_pT[:, (j - 1) % 2, :], start=True,
                       stop=True).then_inc(filled(f"rot{j - 1}"), 1)
            pe.wait_ge(sem("rope_done"), rope_count(4))
            for name in WIN[4:]:
                wait_drained(pe, name)
            attention(diff_maps)

            def sb_scores(i):
                s, k, q = bank(f"sbs{i}"), kz[:, 8 + i, :], qT[:, 4 + i // 2, :]
                claim(pe, f"sbs{i}")
                mm(s[:, 0:T], k[:, 0:P], q, start=True, stop=True)
                mm(s[:, T:T + P], k[:, P:T], q[:, P:T], start=True, stop=True).then_inc(filled(f"sbs{i}"), 1)

            for i in (*pair(0), *pair(1)):
                sb_scores(i)
            for j in range(2):
                pe.wait_ge(sem("sub_sq"), j + 1)
                claim(pe, f"sub{j}")
                mm(bank(f"sub{j}"), ones, att_pT[:, j, :], start=True, stop=True).then_inc(filled(f"sub{j}"), 1)
            for g in range(SB_PAIRS + 1):
                for i in pair(g):
                    x, m = bank(f"sbx{i}"), sb_m[:, i % 2, :]
                    pe.wait_ge(sem("sb_masked"), 2 * (i + 1))
                    claim(pe, f"sbx{i}")
                    mm(x[:, 0:T], sufx, m[:, 0:T], start=True, stop=False, skip_group_check=True)
                    mm(x[:, P:T], ones, m[:, T:T + P], start=False, stop=True, skip_group_check=True)
                    mm(x[:, T:T + P], sufx, m[:, T:T + P], start=True, stop=True,
                       skip_group_check=True).then_inc(filled(f"sbx{i}"), 1)
                for i in pair(g + 2):
                    sb_scores(i)
                for i in pair(g - 1):
                    if i % 2 == 0:
                        claim(pe, f"sbo{i // 2}")
                    o = bank(f"sbo{i // 2}")[HD * (i % 2):HD * (i % 2) + HD, :]
                    pe.wait_ge(sem("sb_probs"), 2 * (i + 1))
                    v = [vv[:, t, 512 + HD * i:512 + HD * i + HD] for t in range(TT)]
                    mm(o[:, 0:T], v[0], sb_a[:, i % 2, 0:T], start=True, stop=False, skip_group_check=True)
                    mm(o[:, P:T], v[1], sb_a[:, i % 2, T:T + P], start=False, stop=True,
                       skip_group_check=True).then_inc(sem("sb_pv"), 1)
            pe.wait_ge(sem("sub_lo"), DIFF_PAIRS)
            for j in range(SBH // 2):
                wait_drained(pe, f"sbo{j}")
            for j in range(4):
                by_channels(f"wo{j}", nb)
            norm_sum(6)
            for name in ffn_order(FF2_CH, ("a",), "b"):
                c = int(name[1:])
                if name[0] == "b":
                    down(name, "down2_", c, FF2_CH - 1, FF0_CH + c + 1, nb)
                else:
                    by_channels(name, nb, arriving("ffn2") if name == "a0" else None)
            norm_sum(7)

        @block.vector
        def _(dve):
            V = nc.vector
            step = [0]

            def link(ins):
                step[0] += 1
                ins.then_inc(sem("dve_step"), 1)
                dve.wait_ge(sem("dve_step"), step[0])

            def stt(out_, in0, scalar, in1, op0, op1):
                return V.scalar_tensor_tensor(out=out_, in0=in0, scalar=scalar, in1=in1, op0=op0, op1=op1)

            def col(at):
                return cols[:, at:at + 1]

            def rest(out_, whole, leading):
                return V.tensor_tensor(out_, whole, leading.bitcast(F32), ALU.subtract)

            def split_lo(p, nb=None):
                n = NUMBER[SPLIT[p]]
                dve.wait_ge(sem("hi_ready"), past_moe(p + 1, nb))
                rest(wl[:, p % SPL, :], raw[:, n % RAW, :], wh[:, p % SPL, :]).then_inc(sem("lo_ready"), 1)

            def split_after(name, nb=None):
                p = POS[name] + SPL
                if p >= len(SPLIT):
                    return
                if nb is None and p >= POS0:
                    dve.wait_ge(sem("hi_ready"), p + 1)
                    rest(wl[:, p % SPL, :], raw[:, (U0 + p - POS0) % RAW, :],
                         wh[:, p % SPL, :]).then_inc(sem("lo_ready"), 1)
                else:
                    split_lo(p, nb)

            def gains(at):
                return cols[:, at:at + KT]

            def norm_rms(k, scale):
                wait_drained(dve, f"nsum{k}")
                link(V.reciprocal(scale[:, :], scale[:, :]))

            def norm_raw(src, gain, scale, dst=normed):
                for k in range(KT):
                    stt(dst[:, k, :], src[:, k, :], gain[:, k:k + 1], scale[:, :], ALU.mult,
                        ALU.mult).then_inc(sem("norm_raw"), 1)

            def norm_lo(name, src=normed):
                for k in range(POOL_TILES[name], KT):
                    wait_hi(dve, name, k)
                    rest(xl[:, k, :], src[:, k, :], xh[:, k, :]).then_inc(sem("norm_lo_dve"), 1)

            def norm_shifted(name, gain, scale, at):
                for k in range(KT + 2):
                    if k < KT:
                        stt(normed[:, k, :], hT[:, k, :], gain[:, k:k + 1], scale[:, :], ALU.mult,
                            ALU.mult).then_inc(sem("norm_raw"), 1)
                    if k >= 2:
                        t = k - 2
                        wait_hi(dve, name, t)
                        stt(xl[:, t, :], normed[:, t, :], mod[:, at + t:at + t + 1], xh[:, t, :].bitcast(F32), ALU.add,
                            ALU.subtract).then_inc(sem("norm_lo_dve"), 1)

            def qk_scale(name, outs):
                k = QK_UNITS.index(name)
                r = att_p[:, k % 2, :]
                wait_drained(dve, f"qsum{k}")
                link(V.reciprocal(r, r))
                heads = bank(name).rearrange("p (a b) -> p a b", a=2)
                r2 = r.rearrange("p (a b) -> p a b", a=2)
                for dst, lo, hi, gain in outs:
                    ins = stt(dst, heads[lo:hi, :, :], gain[lo:hi, :], r2[lo:hi, :, :], ALU.mult, ALU.mult)
                ins.then_inc(drained(name), 1)

            def keys(name, keys_, at, gain):
                qk_scale(name, [(keys_[0:HD, at:at + 4:2, :], 0, HD, gain),
                                (keys_[HD:P, at + 1:at + 4:2, :], HD, P, gain)])

            split_lo(0)
            dve.wait_ge(sem("ld_cols"), 16)
            dve.wait_ge(sem("ld_cst"), 16)
            V.tensor_scalar(gq8[:, 0:1], col(V_FGQ), SCALE, None, ALU.mult)
            V.tensor_scalar(gq8[:, 1:3], cols[:, V_GMQ:V_GMQ + 2], SCALE, None, ALU.mult)
            link(V.tensor_tensor(lam[:, 4:5], col(V_LQ), col(V_LK), ALU.mult))
            V.tensor_tensor(lam[:, 0:1], lam[:, 4:5], headones[:, 0:1], ALU.mult).then_inc(sem("lam_prod"), 1)
            V.tensor_tensor(lam[:, 1:2], lam[:, 4:5], headones[:, HD:HD + 1], ALU.mult).then_inc(sem("lam_prod"), 1)

            norm_rms(0, rn_mem)
            norm_raw(mem0, gains(V_MEM), rn_mem, mem0)
            norm_lo("mem0", mem0)
            split_lo(1)
            norm_rms(1, rn)
            norm_raw(hT, gains(V_MIX), rn)
            split_lo(2)
            split_after("mk0")
            norm_lo("x")
            split_after("mv0")
            dve.wait_ge(sem("keys_zeroed"), 1)
            keys("mk0", kz, FOX_HEADS, col(V_GMK))
            wait_filled(dve, "foxf")
            V.tensor_tensor(lsf[:, 0, :, :], bank("foxf")[:, 0:2 * FOX_HEADS].rearrange("p (a b) -> p a b", a=2),
                            cols[:, V_BF:V_BF + FOX_HEADS].unsqueeze(1).broadcast_to([P, TT, FOX_HEADS]),
                            ALU.add).then_inc(drained("foxf"), 1)
            wait_drained(dve, "foxf")
            stt(lsf[:, 1, :, :], lsf[:, 0, :, :], -1.0, lsf[:, 0, :, :], ALU.mult,
                ALU.min).then_inc(sem("fox_negabs"), 1)
            dve.wait_ge(sem("fox_log1p"), 1)
            stt(lsf[:, 0, :, :], lsf[:, 0, :, :], 0.0, lsf[:, 1, :, :], ALU.min,
                ALU.subtract).then_inc(sem("fox_logf"), 1)
            split_after("mq0")
            for j in range(6):
                split_after(UNITS_A[3 + j])
                if j == 0:
                    qk_scale("mq0", [(qT[:, 6:8, :], 0, P, gq8[:, 1:2])])
                    wait_lo(dve, "x")
                    V.tensor_copy(selh, ident[:, 0:FOX_HEADS].unsqueeze(2).broadcast_to([P, FOX_HEADS, P])).then_inc(
                        sem("selh_ready"), 1)
                    wait_filled(dve, "cum")
                    dve.wait_ge(sem("negc_ready"), 1)
                    V.tensor_copy(flat(ctok), bank("cum")[:, T:T + 2 * FOX_HEADS]).then_inc(drained("cum"), 1)
                    wait_drained(dve, "cum")
                elif j < 4:
                    qk_scale(f"fq{j - 1}", [(qT[:, 2 * j - 2:2 * j, :], 0, P, gq8[:, 0:1])])
                else:
                    keys(f"fk{j - 4}", kz, 4 * (j - 4), col(V_FGK))
            keys("fk2", kz, 8, col(V_FGK))

            def attention(rng, meanwhile=None):
                n, a0 = len(rng), rng[0]
                for i in range(n + PV_LAG + 1):
                    if i < n:
                        a = a0 + i
                        m, s, p = maps[a], bank(f"sc{a}"), att_p[:, a % 3, :]
                        wait_filled(dve, f"sc{a}")
                        if a >= 3:
                            wait_filled(dve, f"pT{a - 3}")
                        if m["kind"] == "fox":
                            h = m["head"]
                            c0, c1 = ctok[:, 0, h:h + 1], ctok[:, 1, h:h + 1]
                            stt(p[:, 0:P], s[:, 0:P], c0, cc(C_FOXM), ALU.add, ALU.add)
                            V.tensor_scalar(p[:, P:2 * P], s[:, P:2 * P], c1, None, ALU.add)
                            stt(p[:, 2 * P:3 * P], s[:, 2 * P:3 * P], c1, cc(C_FOXM), ALU.add,
                                ALU.add).then_inc(drained(f"sc{a}"), 1)
                            w0, w1 = P, 3 * P
                        elif m["kind"] == "diff":
                            V.tensor_tensor(p[:, 0:P], s[:, 0:P], cc(C_DIFM), ALU.add)
                            V.tensor_copy(p[:, P:2 * P], s[:, P:2 * P])
                            V.tensor_tensor(p[:, 2 * P:3 * P], s[:, 2 * P:3 * P], cc(C_DIFM),
                                            ALU.add).then_inc(drained(f"sc{a}"), 1)
                            w0, w1 = P, 3 * P
                        else:
                            V.tensor_copy(p, s).then_inc(drained(f"sc{a}"), 1)
                            w0, w1 = T, 2 * T
                        wait_drained(dve, f"sc{a}")
                        for t, (lo, hi) in enumerate(((0, w0), (w0, w1))):
                            V.tensor_reduce(nmx[:, a % 3, t:t + 1], p[:, lo:hi], AX_X, ALU.max,
                                            negate=True).then_inc(sem("att_max"), 1)
                    if 0 <= i - 1 < n:
                        a = a0 + i - 1
                        dve.wait_ge(sem("att_exp"), 2 * (a + 1))
                        ins = V.reciprocal(rsum[:, a % 3, :], ssum[:, a % 3, :])
                        if maps[a]["kind"] == "diff" and a % 2 == 1:
                            link(ins)
                            ins = V.tensor_scalar(rsum[:, a % 3, :], rsum[:, a % 3, :], lam[:, 6:7], None, ALU.mult)
                        ins.then_inc(sem("att_rsum"), 1)
                    if 0 <= i - PV_LAG - 1 < n and (i - PV_LAG - 1) % 2 == 1:
                        g = (a0 + i - PV_LAG - 1) // 2
                        o, to = bank(f"pv{g}")[:, 0:T], maps[2 * g]["to"]
                        if maps[a0]["kind"] == "diff":
                            dve.wait_ge(sem("att_pv"), 2 * (g + 1))
                            V.tensor_copy(qT[:, to, :], o).then_inc(drained(f"pv{g}"), 1)
                        else:
                            dve.wait_ge(sem("mix_hi"), g + 1)
                            rest(xl[:, to, :], o, xh[:, to, :]).then_inc(drained(f"pv{g}"), 1)
                    if meanwhile:
                        meanwhile(i)

            dve.wait_ge(sem("ld_cst_rest"), 16)
            attention(fox_maps, lambda i: [split_after(name) for name in FOX_SPLITS.get(i, ())])

            def residual(name, j):
                h2 = pair_of(hT, j)
                V.tensor_tensor(h2, h2, bank(name), ALU.add).then_inc(drained(name), 1)

            for j in range(4):
                wait_done(dve, f"fo{j}")
                residual(f"fo{j}", j)
                if j < 2:
                    split_after(f"fo{j}")
            split_after("fo2")
            norm_rms(2, rn)
            norm_raw(hT, gains(V_FFN), rn)
            norm_lo("ffn0")
            split_after("fo3")

            def modulation(j):
                n = NUMBER[f"ada{j}"]
                wait_loaded(dve, n)
                if j == 0:
                    dve.wait_ge(sem("c_ready"), 1)
                w = raw[:, n % RAW, :].rearrange("p (o k) -> p o k", o=2)
                for o in range(2):
                    ins = V.scalar_tensor_tensor(out=w[:, o, :], in0=w[:, o, :], scalar=1.0, in1=c_row, op0=ALU.mult,
                                                 op1=ALU.mult, accum_out=mod[:, 2 * j + o:2 * j + o + 1])
                ins.then_inc(sem("ada_done"), 1)

            for name in ffn_order(FF0_CH, ("g", "u"), "d"):
                c = int(name[1:])
                if name[0] == "u":
                    wait_done(dve, name)
                    wait_drained(dve, f"g{c}")
                    V.tensor_tensor(sg[:, c % 2, :], sg[:, c % 2, :], bank(name), ALU.mult).then_inc(drained(name), 1)
                split_after(name)
                n = NUMBER[SPLIT[POS[name] + SPL]] + 1
                while UNITS[n] not in POS:
                    modulation(int(UNITS[n][3:]))
                    n += 1
                if name == "g1":
                    dve.wait_ge(sem("ld_mem1"), 16)
                    wait_lo(dve, "ffn0")
                    norm_raw(mem1, gains(V_MEM + 8), rn_mem)
            for j in range(4):
                wait_done(dve, f"d{FF0_CH - 1}")
                residual(f"down0_{j}", j)
            norm_rms(3, rn)
            norm_raw(hT, gains(V_MIX + 8), rn)
            dve.wait_ge(sem("ada_done"), ADA_UNITS)
            link(V.tensor_tensor(mod[:, :], mod[:, :], cols[:, V_ADA:V_ADA + 48], ALU.add))
            stt(gs[:, 0, :], mod[:, 8:16], 1.0, gains(V_MIX2), ALU.add, ALU.mult)
            stt(gs[:, 1, :], mod[:, 32:40], 1.0, gains(V_FFN2), ALU.add, ALU.mult).then_inc(sem("gs_ready"), 1)
            wait_drained(dve, "lam")
            link(V.tensor_tensor(lam[:, 5:6], lam[:, 3:4], lam[:, 2:3], ALU.subtract))
            link(V.tensor_scalar(lam[:, 6:7], lam[:, 5:6], LAMBDA_INIT, None, ALU.subtract))
            link(V.tensor_scalar(lam[:, 7:8], col(V_SUB), 1.0 - LAMBDA_INIT, None, ALU.mult))
            split_after("mk1")
            norm_lo("mix1")
            split_after("mv1")
            dve.wait_ge(sem("keys1_zeroed"), 1)
            keys("mk1", mkz1, 0, col(V_GMK + 1))
            split_after("mq1")

            dve.wait_ge(sem("upad_zeroed"), 1)
            for j in range(6):
                if j >= 3:
                    wait_drained(dve, f"ci{j}")
                    V.tensor_tensor(upad[:, 2 * j - 6:2 * j - 4, PAD:PAD + T], abuf[:, 2 * j - 6:2 * j - 4, :],
                                    cacc[:, 2 * j - 6:2 * j - 4, :], ALU.mult).then_inc(sem("glu"), 1)
                if j < 3:
                    split_after(f"ci{j}")
                if j == 0:
                    qk_scale("mq1", [(q1[:, :, :], 0, P, gq8[:, 2:3])])

            def convolve(first, last):
                for n in range(first, last):
                    tap, c = n // (CT - CT_PE), CT_PE + n % (CT - CT_PE)
                    w = col(V_TAP + CT * tap + c)
                    u = upad[:, c, tap:tap + T]
                    if tap == 0:
                        ins = V.tensor_scalar(cacc[:, c, :], u, w, col(V_DWB + c), ALU.mult, ALU.add)
                    else:
                        dve.wait_ge(sem("conv_tap"), n - (CT - CT_PE) + 1)
                        ins = stt(cacc[:, c, :], u, w, cacc[:, c, :], ALU.mult, ALU.add)
                    ins.then_inc(sem("conv_tap"), 1)

            def meanwhile(i):
                convolve(DVE_TAPS * i // (MEM_STEPS + 1), DVE_TAPS * (i + 1) // (MEM_STEPS + 1))

            dve.wait_ge(sem("glu"), 3)
            attention(mem_maps, meanwhile)
            split_after("ci3")
            wait_filled(dve, "lnsum")
            wait_raw(dve, "mix1")
            V.tensor_scalar(rn[:, :], bank("lnsum")[:, 0:T], 1.0 / CONV, None, ALU.mult).then_inc(drained("lnsum"), 1)
            wait_drained(dve, "lnsum")
            for c in range(CT):
                V.tensor_tensor(cacc[:, c, :], cacc[:, c, :], rn[:, :], ALU.subtract).then_inc(sem("ln_centred"), 1)
            split_after("ci4")
            wait_drained(dve, "lnvar")
            link(V.reciprocal(rn[:, :], rn[:, :]))
            for c in range(CT):
                V.tensor_tensor(cacc[:, c, :], cacc[:, c, :], rn[:, :], ALU.mult).then_inc(sem("ln_scaled"), 1)
            for c in range(CT):
                dve.wait_ge(sem("conv_hi"), c + 1)
                rest(xl[:, c, :], cacc[:, c, :], xh[:, c, :]).then_inc(sem("conv_lo"), 1)
            split_after("ci5")
            for j in range(4):
                wait_done(dve, f"co{j}")
                residual(f"co{j}", j)
                if j < 2:
                    split_after(f"co{j}")
            split_after("co2")
            norm_rms(4, rn)
            norm_raw(hT, gains(V_FFN + 8), rn)
            split_after("co3")

            ei = cc(C_EI, E)
            wait_filled(dve, "router")
            V.tensor_copy(flat(lg), bank("router")[:, 0:TT * E]).then_inc(drained("router"), 1)
            wait_drained(dve, "router")
            for t in range(TT):
                link(V.max(mx8[:, t, :], lg[:, t, :]))
                link(V.max_index(ix8[:, t, :], mx8[:, t, :], lg[:, t, :]))
            link(V.tensor_copy(ixf[:, :, :], ix8[:, :, 0:2]))
            for a in range(2):
                for t in range(TT):
                    link(V.tensor_scalar(oh[:, a, t, :], ei, ixf[:, t, a:a + 1], None, ALU.is_equal))
            marks = plan_f[:, 0, :]
            V.tensor_tensor(marks, oh[:, 0, :, :].rearrange("p a b -> p (a b)"),
                            oh[:, 1, :, :].rearrange("p a b -> p (a b)"), ALU.add).then_inc(sem("moe_marks"), 1)
            V.tensor_tensor(pexp[:, 0:2].unsqueeze(2), mx8[:, :, 1:2], mx8[:, :, 0:1],
                            ALU.subtract).then_inc(sem("gate_diff"), 1)
            wait_filled(dve, "mcum")
            dve.wait_ge(sem("moe_marks"), 1)
            link(V.tensor_tensor(plan_f[:, 1, :], bank("mcum")[:, 0:2 * E], marks, ALU.subtract))
            pos = plan_f[:, 1, :]
            V.tensor_copy(plan_f[:, 2, 0:E], bank("mcum")[:, 2 * E:3 * E]).then_inc(drained("mcum"), 1)
            wait_drained(dve, "mcum")
            cnt = plan_f[:, 2, 0:E]
            link(V.tensor_scalar(plan_f[:, 3, 0:E], cnt, float(CAP), None, ALU.is_gt))
            link(stt(plan_f[:, 4, 0:E], cnt, float(2 * CAP), plan_f[:, 3, 0:E], ALU.is_gt, ALU.add))
            extra = plan_f[:, 4, 0:E]
            link(V.tensor_tensor(lt8[:, :, :], cc(C_LT, E * E).rearrange("p (a b) -> p a b", a=E),
                                 extra.unsqueeze(1).broadcast_to([P, E, E]), ALU.mult))
            link(V.tensor_reduce(plan_f[:, 5, 0:E], lt8[:, :, :], AX_X, ALU.add))
            before = plan_f[:, 5, 0:E]
            link(stt(plan_f[:, 6, 0:E], before, float(E - 1), ei, ALU.add, ALU.subtract))
            link(V.tensor_scalar(plan_f[:, 7, 0:E], plan_f[:, 6, 0:E], float(CAP), None, ALU.mult))
            link(V.tensor_scalar(plan_f[:, 8, :], pos, float(CAP), None, ALU.is_ge))
            two = lambda r: plan_f[:, r, :].rearrange("p (a b) -> p a b", a=TT)
            link(V.tensor_tensor(two(9), two(8), plan_f[:, 7, 0:E].unsqueeze(1).broadcast_to([P, TT, E]), ALU.mult))
            link(V.tensor_tensor(plan_f[:, 10, :], plan_f[:, 9, :], pos, ALU.add))
            link(V.tensor_scalar(plan_f[:, 11, 0:E], ei, float(CAP), None, ALU.mult))
            link(V.tensor_tensor(two(12), two(10), plan_f[:, 11, 0:E].unsqueeze(1).broadcast_to([P, TT, E]), ALU.add))
            for a in range(2):
                r = plan_f[:, 13 + a, :].rearrange("p (a b) -> p a b", a=TT)
                link(V.tensor_tensor(r, oh[:, a, :, :], two(12), ALU.mult))
                ins = V.tensor_reduce(kcol[:, a, :], r, AX_X, ALU.add)
                if a == 0:
                    link(ins)
            ins.then_inc(sem("moe_keys"), 1)
            iota = cc(C_IOTA, CAP)

            def select(count, first=False):
                if not first:
                    dve.wait_ge(sem("keys_moved"), count)
                for t in range(TT):
                    V.tensor_scalar(sel[:, t, :], iota, kcol[:, 0, t:t + 1], None,
                                    ALU.is_equal).then_inc(sem("sel_half"), 1)
                dve.wait_ge(sem("sel_half"), count * TT + TT)
                for t in range(TT):
                    stt(sel[:, t, :], iota, kcol[:, 1, t:t + 1], sel[:, t, :], ALU.is_equal,
                        ALU.add).then_inc(sem("moe_sel"), 1)
                dve.wait_ge(sem("moe_sel"), count * TT + TT)
                V.tensor_scalar(kcol[:, :, :], kcol[:, :, :], -float(CAP), None, ALU.add).then_inc(sem("keys_moved"), 1)
            dve.wait_ge(sem("moe_keys"), 1)
            wait_filled(dve, "krow")
            select(0, first=True)
            link(V.tensor_tensor(plan_f[0:1, 15, 0:E], plan_f[0:1, 5, 0:E], plan_f[0:1, 4, 0:E], ALU.add))
            link(V.tensor_scalar(pexp[0:1, 8:9], plan_f[0:1, 15, E - 1:E], float(E), None, ALU.add))
            link(V.tensor_tensor(lt8[0:1, 0:EXTRA, :], plan_f[0:1, 15, 0:E].unsqueeze(1).broadcast_to([1, EXTRA, E]),
                                 cst[0:1, C_XI:C_XI + EXTRA * E].rearrange("p (a b) -> p a b", a=EXTRA), ALU.is_le))
            link(V.tensor_reduce(pexp[0:1, 16:16 + EXTRA], lt8[0:1, 0:EXTRA, :], AX_X, ALU.add))
            link(V.tensor_scalar(pexp[0:1, 16:16 + EXTRA], pexp[0:1, 16:16 + EXTRA], float(E - 1), None, ALU.min))
            V.tensor_copy(etab[0:1, 0:E], cst[0:1, C_EI:C_EI + E])
            V.tensor_copy(etab[0:1, E:E + EXTRA], pexp[0:1, 16:16 + EXTRA]).then_inc(sem("moe_plan"), 1)
            V.tensor_copy(nbt[0:1, 0:1], pexp[0:1, 8:9])
            V.tensor_scalar(nbt[0:1, 1:2], pexp[0:1, 8:9], -1.0, None, ALU.add).then_inc(sem("moe_plan"), 1)
            dve.wait_ge(sem("gate_exp"), 1)
            link(V.tensor_scalar(pexp[:, 2:4], pexp[:, 0:2], 1.0, None, ALU.add))
            V.reciprocal(gcol[:, 0, :], pexp[:, 2:4]).then_inc(sem("moe_gates"), 1)
            dve.wait_ge(sem("moe_gates"), 1)
            V.tensor_tensor(gcol[:, 1, :], gcol[:, 0, :], pexp[:, 0:2], ALU.mult).then_inc(sem("moe_gates"), 1)
            wait_filled(dve, "krow")
            V.tensor_copy(krow[:, 0:2, :].rearrange("p a b -> p (a b)"), bank("krow")).then_inc(drained("krow"), 1)
            for j in range(2):
                dve.wait_ge(sem("gather_hi"), j + 1)
                rest(four_of(xgl, j), bank(f"gather{j}"),
                     four_of(xgh, j)).then_inc(sem(f"moe_drained{MOE_BANK[f'G{j}'][0]}"), 1)
            wait_filled(dve, "grow")
            V.tensor_copy(krow[:, 2:4, :].rearrange("p a b -> p (a b)"), bank("grow")).then_inc(drained("grow"), 1)
            wait_drained(dve, "krow")
            wait_drained(dve, "grow")
            sid = cst[:, C_SID:C_SID + 1]
            dve.wait_ge(sem("moe_scat"), 1)
            dve.wait_ge(sem("moe_plan"), 2)
            nb = dve.value_load(nbt[0:1, 0:1], min_val=E, max_val=MAXBLK)
            with dve.Fori(0, nb) as i:
                def split_next(j):
                    n, p = U0 + j + SPL, POS0 + j + SPL
                    dve.wait_ge(sem("hi_ready"), i * MOE_UNITS + p + 1)
                    rest(wl[:, p % SPL, :], raw[:, n % RAW, :], wh[:, p % SPL, :]).then_inc(sem("lo_ready"), 1)

                def turned_lo(c):
                    b = MOE_BANK[f"T{c}"][0]
                    dve.wait_ge(sem("moe_hid_hi"), i * MOE_CH + c + 1)
                    rest(al[:, c % 2, :], ps[:, b, :], ah[:, c % 2, :]).then_inc(sem(f"moe_drained{b}"), 1)

                def add_tokens(s):
                    b, per, use = MOE_BANK[f"S{s}"]
                    dve.wait_ge(sem(f"moe_filled{b}"), i * per + use + 1)
                    h2 = pair_of(hT, s)
                    V.tensor_tensor(h2, h2, ps[:, b, :], ALU.add).then_inc(sem(f"moe_drained{b}"), 1)

                for j, (kind, c, half) in enumerate(MOE_ORDER):
                    if (kind, half) == ("u", 1):
                        dve.wait_ge(sem("unit_done"), i * MOE_UNITS + POS0 + j + 1)
                        dve.wait_ge(sem("moe_silu"), i * MOE_CH + c + 1)
                        V.tensor_tensor(sg[:, c % 2, :], sg[:, c % 2, :], ps[:, 2 * (c % 2) + 1, :],
                                        ALU.mult).then_inc(sem("moe_prod"), 1)
                    split_next(j)
                    if (kind, half) == ("g", 1) and c >= 1:
                        turned_lo(c - 1)
                    if (kind, half) == ("u", 1) and c < 4:
                        add_tokens(c)
                    if (kind, c, half) == ("g", 3, 0):
                        select(i + 1)
                    if (kind, c, half) == ("g", 4, 0):
                        stt(scat, krow[:, 0, :], sid, krow[:, 2, :], ALU.is_equal, ALU.mult).then_inc(sem("scat_half"), 1)
                        stt(scat_b, krow[:, 1, :], sid, krow[:, 3, :], ALU.is_equal,
                            ALU.mult).then_inc(sem("scat_half"), 1)
                        dve.wait_ge(sem("scat_half"), i * 3 + 2)
                        V.tensor_scalar(krow[:, 0:2, :], krow[:, 0:2, :], -float(CAP), None,
                                        ALU.add).then_inc(sem("scat_half"), 1)
                        dve.wait_ge(sem("scat_half"), i * 3 + 3)
                        V.tensor_tensor(scat, scat, scat_b, ALU.add).then_inc(sem("moe_scat"), 1)
                    if (kind, c, half) == ("d", MOE_CH - 2, 1):
                        turned_lo(MOE_CH - 1)
                        for g in range(2):
                            b = MOE_BANK[f"G{g}"][0]
                            dve.wait_ge(sem("gather_hi"), i * 2 + 2 + g + 1)
                            rest(four_of(xgl, g), ps[:, b, :], four_of(xgh, g)).then_inc(sem(f"moe_drained{b}"), 1)
            for j in range(4):
                wait_filled(dve, f"scat{j}")
                residual(f"scat{j}", j)

            norm_rms(5, rn)
            dve.wait_ge(sem("gs_ready"), 1)
            norm_shifted("mix2", gs[:, 0, :], rn, 0)
            cos2 = cc(C_COS, T).unsqueeze(1).broadcast_to([P, 2, T])
            sin2 = cc(C_SIN, T).unsqueeze(1).broadcast_to([P, 2, T])
            t1 = att_p[:, 0, :].rearrange("p (a b) -> p a b", a=2)
            t2 = att_p[:, 1, :].rearrange("p (a b) -> p a b", a=2)
            dve.wait_ge(sem("keys_zeroed"), 2)

            def rope(j):
                scale = SCALE if j < 2 else 1.0
                wait_drained(dve, ROPED[j])
                plain = att_pT[:, j % 2, :].rearrange("p (a b) -> p a b", a=2)
                if j:
                    dve.wait_ge(sem("rope_done"), rope_count(j))
                link(stt(t1, plain, scale, cos2, ALU.mult, ALU.mult))
                wait_filled(dve, f"rot{j}")
                stt(t2, bank(f"rot{j}").rearrange("p (a b) -> p a b", a=2), scale, sin2, ALU.mult,
                    ALU.mult).then_inc(drained(f"rot{j}"), 1)
                wait_drained(dve, f"rot{j}")
                if j < 2:
                    V.tensor_tensor(qT[:, 2 * j:2 * j + 2, :], t1, t2, ALU.add).then_inc(sem("rope_done"), 1)
                else:
                    at = 4 * (j - 2)
                    V.tensor_tensor(kz[0:HD, at:at + 4:2, :], t1[0:HD, :, :], t2[0:HD, :, :],
                                    ALU.add).then_inc(sem("rope_done"), 1)
                    V.tensor_tensor(kz[HD:P, at + 1:at + 4:2, :], t1[HD:P, :, :], t2[HD:P, :, :],
                                    ALU.add).then_inc(sem("rope_done"), 1)

            for j, name in enumerate(WIN):
                if name not in DIFF_SPLITS.values():
                    split_after(name, nb)
                if 1 <= j <= 4:
                    rope(j - 1)
            attention(diff_maps)

            wait_filled(dve, f"pT{len(maps) - 1}")
            def distance(i):
                wait_filled(dve, f"sbs{i}")
                if i >= 4:
                    wait_drained(dve, f"sbs{i - 4}")
                z, l = bank(f"sbs{i}")[:, 0:3 * P], sb_l[:, i % 4, :]
                link(V.tensor_scalar(l, z, -1.0, None, ALU.mult))
                V.tensor_tensor(l, z, l, ALU.min).then_inc(sem("sb_abs"), 1)

            def sub_rest(q):
                dve.wait_ge(sem("sub_hi"), q + 1)
                rest(xl[:, q, :], qT[:, q, :], xh[:, q, :]).then_inc(sem("sub_lo"), 1)

            def sb_rest(g):
                dve.wait_ge(sem("sb_hi"), g + 1)
                rest(xl[:, 4 + g, :], bank(f"sbo{g}")[:, 0:T], xh[:, 4 + g, :]).then_inc(drained(f"sbo{g}"), 1)

            for i in (*pair(0), *pair(1)):
                distance(i)
            for g in range(SB_PAIRS):
                for i in pair(g):
                    dve.wait_ge(sem("sb_log1p"), i + 1)
                    if i >= 2:
                        wait_filled(dve, f"sbx{i - 2}")
                    stt(sb_m[:, i % 2, :], bank(f"sbs{i}")[:, 0:3 * P], 0.0, sb_l[:, i % 4, :], ALU.max,
                        ALU.add).then_inc(sem("sb_m"), 1)
                for i in pair(g):
                    if i >= 4:
                        dve.wait_ge(sem("sb_exp"), i - 3)
                    stt(sb_b[:, i % 4, :], bank(f"sbs{i}")[:, 0:3 * P], 0.0, sb_l[:, i % 4, :], ALU.min,
                        ALU.subtract).then_inc(drained(f"sbs{i}"), 1)
                wait_drained(dve, f"sub{g // 2}")
                r = sub_r[:, g // 2, T * (g % 2):T * (g % 2) + T]
                link(V.reciprocal(r, r))
                stt(qT[:, g, :], qT[:, g, :], lam[:, 7:8], r, ALU.mult, ALU.mult).then_inc(sem("sub_out"), 1)
                for i in pair(g):
                    wait_filled(dve, f"sbx{i}")
                    wait_drained(dve, f"sbs{i}")
                    V.tensor_tensor(sb_b[:, i % 4, :], sb_b[:, i % 4, :], bank(f"sbx{i}")[:, 0:3 * P],
                                    ALU.subtract).then_inc(drained(f"sbx{i}"), 1)
                for i in pair(g + 2):
                    distance(i)
                if g >= 1:
                    sub_rest(g - 1)
                if g >= 2:
                    sb_rest(g - 2)
            sub_rest(SB_PAIRS - 1)
            sb_rest(SB_PAIRS - 2)
            sb_rest(SB_PAIRS - 1)
            for name in DIFF_SPLITS.values():
                split_after(name, nb)

            def gated_residual(name, j, at):
                for t in range(2):
                    o = 2 * j + t
                    ins = stt(hT[:, o, :], bank(name)[:, T * t:T * t + T], mod[:, at + o:at + o + 1], hT[:, o, :],
                              ALU.mult, ALU.add)
                ins.then_inc(drained(name), 1)

            for j in range(4):
                wait_done(dve, f"wo{j}", nb)
                gated_residual(f"wo{j}", j, 16)
                if j < 2:
                    split_after(f"wo{j}", nb)
            split_after("wo2", nb)
            norm_rms(6, rn)
            norm_shifted("ffn2", gs[:, 1, :], rn, 24)
            split_after("wo3", nb)
            for name in ffn_order(FF2_CH, ("a",), "b"):
                c = int(name[1:])
                if name[0] == "a":
                    wait_done(dve, name, nb)
                    if c >= 2:
                        dve.wait_ge(sem("hid_lo"), FF0_CH + c - 1)
                    link(V.tensor_scalar(sg[:, c % 2, :], bank(name), 0.0, None, ALU.max))
                    V.tensor_tensor(sg[:, c % 2, :], sg[:, c % 2, :], bank(name), ALU.mult).then_inc(drained(name), 1)
                split_after(name, nb)
            for j in range(4):
                wait_done(dve, f"b{FF2_CH - 1}", nb)
                gated_residual(f"down2_{j}", j, 40)
            norm_rms(7, rn)
            norm_raw(hT, gains(V_FIN2), rn)


def rope_count(j):
    return min(j, 2) + 2 * max(0, j - 2)


def units_by_columns(w):
    return w.reshape(KT, P, -1, T).transpose(2, 1, 0, 3).reshape(-1, P, UW)


def units_by_rows(w):
    return w.reshape(-1, 2, P, D).transpose(0, 2, 1, 3).reshape(-1, P, UW)


def main_units(A):
    fox, kv, win = A["fox_w_in"][0], A["w_mem_kv"], A["w_in_2"][0]
    by_name = {}

    def put(prefixes, units):
        per = len(units) // len(prefixes)
        for p, prefix in enumerate(prefixes):
            for j in range(per):
                by_name[f"{prefix}{j}"] = units[p * per + j]

    for layer in range(2):
        by_name[f"mk{layer}"], by_name[f"mv{layer}"] = units_by_columns(kv[layer])
    by_name["mq0"], = units_by_columns(fox[:, 3 * FOX + FOX_HEADS:])
    put(("fq", "fk", "fv"), units_by_columns(fox[:, :3 * FOX]))
    put(("fo",), units_by_columns(A["fox_w_out"][0]))
    put(("g",), units_by_columns(A["ffn_w_gate"][0]))
    put(("u",), units_by_columns(A["ffn_w_up"][0]))
    put(("d",), units_by_rows(A["ffn_w_down"][0]))
    put(("ci",), units_by_columns(A["conv_w_in"][0][:, :2 * CONV]))
    by_name["mq1"], = units_by_columns(A["conv_w_in"][0][:, 2 * CONV:])
    put(("ada",), units_by_rows(A["ada_w_2"][0].T))
    put(("co",), units_by_columns(A["conv_w_out"][0]))
    put(("dq", "dk", "dv", "sq", "sk", "sv"), units_by_columns(win))
    put(("wo",), units_by_columns(A["w_out_2"][0]))
    put(("a",), units_by_columns(A["w_ff1_2"][0]))
    put(("b",), units_by_rows(A["w_ff2_2"][0]))
    return np.stack([by_name[name] for name in UNITS])


def moe_units(A):
    out = np.empty((E, MOE_UNITS, P, UW), np.float32)
    up = {"g": A["moe_w_gate"][0], "u": A["moe_w_up"][0]}
    for j, (kind, c, half) in enumerate(MOE_ORDER):
        if kind == "d":
            w = A["moe_w_down"][0].reshape(E, MOE_CH, 2, 2, P, D)[:, c, half]
        else:
            w = up[kind].reshape(E, 2, 4, P, MOE_CH, 512)[:, half, :, :, c]
        out[:, j] = w.transpose(0, 2, 1, 3).reshape(E, P, UW)
    return out


def vector_columns(A):
    c = np.empty((P, V_END), np.float32)

    def put(at, v):
        v = v.reshape(-1, P).T
        c[:, at:at + v.shape[1]] = v

    def twin(at, first, second):
        put(at, np.concatenate([first.reshape(-1, HD), second.reshape(-1, HD)], 1))

    for at, name in ((V_MIX, "norm_mix"), (V_MEM, "norm_mem"), (V_FFN, "norm_ffn"), (V_CB, "conv_b_in"),
                     (V_DWB, "conv_dw_b"), (V_LNG, "conv_ln_g"), (V_LNB, "conv_ln_b"), (V_MIX2, "mix_norm_g_2"),
                     (V_FFN2, "ffn_norm_g_2"), (V_FIN2, "final_norm_g_2"), (V_SUB, "diff_subln_g_2"),
                     (V_ADA, "ada_b_2"), (V_TAP, "conv_dw")):
        put(at, A[name])
    for at, name in ((V_FGQ, "fox_g_q"), (V_FGK, "fox_g_k"), (V_GMQ, "g_mq"), (V_GMK, "g_mk")):
        twin(at, A[name], A[name])
    twin(V_LQ, A["lambda_q1_2"], A["lambda_q2_2"])
    twin(V_LK, A["lambda_k1_2"], A["lambda_k2_2"])
    c[:, V_BF:V_WF] = A["fox_b_f"]
    c[:, V_WF:V_RT] = by_partition(A["fox_w_in"][0][:, 3 * FOX:3 * FOX + FOX_HEADS])
    c[:, V_RT:V_END] = by_partition(A["moe_router"][0])
    return c


def by_partition(w):
    return w.reshape(KT, P, -1).transpose(1, 0, 2).reshape(P, -1)


def kernel(**inputs):
    import concourse.bacc as bacc
    from concourse.bass_utils import run_bass_kernel_spmd

    A = {name: np.asarray(a) for name, a in inputs.items()}
    arrays = {
        "in_x": by_partition(A["x"][0].T), "in_mem": by_partition(A["mem"][0].T), "in_c": A["c_2"], "in_constants": constants(),
        "in_columns": vector_columns(A), "in_units": main_units(A), "in_experts": moe_units(A)}
    nc = bacc.Bacc("TRN2", target_bir_lowering=False, num_devices=1)
    drams = []
    for name, a in arrays.items():
        arrays[name] = np.ascontiguousarray(a)
        drams.append(nc.dram_tensor(name, a.shape, F32, kind="ExternalInput").ap())
    out = nc.dram_tensor("out_0", (P, KT * T), F32, kind="ExternalOutput").ap()
    build(nc, *drams, out)
    r = run_bass_kernel_spmd(nc, [arrays], core_ids=[0])
    res = r.results[0]["out_0"].reshape(P, KT, T).transpose(2, 1, 0)
    return np.ascontiguousarray(res.reshape(1, T, D))
```
